# Optimizing a Trainium2 kernel written in Bass

```python
import jax
import jax.numpy as jnp
from jax import lax
import numpy as np

D_MODEL = 2048
BATCH = 1
SEQ = 256
DEPTH = 1

HEAD_DIM = 128
SB_HEADS = 8
NSA_HEADS = 8
NSA_KV_GROUPS = 2
SB_WIDTH = SB_HEADS * HEAD_DIM
NSA_WIDTH = NSA_HEADS * HEAD_DIM
MIX_WIDTH = SB_WIDTH + NSA_WIDTH
KV_WIDTH = NSA_KV_GROUPS * HEAD_DIM
N_GATES = 3
CMP_BLOCK = 32
CMP_STRIDE = 16
CMP_HIDDEN = 256
SEL_BLOCK = 64
SEL_TOPK = 16
WINDOW = 512
Q_BLOCK = 128
MEM_TOKENS = 256
MEM_HEADS = 4
D_FF = 5504
ROPE_THETA = 10000.0
LN_EPS = 1e-5
RMS_EPS = 1e-6
MASK_FILL = -1e30
DEEPNORM_ALPHA = (2 * DEPTH) ** 0.25
DEEPNORM_BETA = (8 * DEPTH) ** -0.25
IN_SPLITS = (SB_WIDTH, SB_WIDTH, SB_WIDTH, NSA_WIDTH, KV_WIDTH, KV_WIDTH, KV_WIDTH, KV_WIDTH, KV_WIDTH, KV_WIDTH, NSA_HEADS * N_GATES)
VALUE_SEGMENTS = (2, 5, 7, 9)
IN_COLS = sum(IN_SPLITS)

kernel_name = 'hybrid_sb_nsa_macaron_deepnorm'

def layer_norm(x, g, b):
    xf = x.astype(jnp.float32)
    mu = jnp.mean(xf, axis=-1, keepdims=True)
    var = jnp.mean(jnp.square(xf - mu), axis=-1, keepdims=True)
    return ((xf - mu) * lax.rsqrt(var + LN_EPS) * g + b).astype(x.dtype)

def swiglu(x, w_gate, w_up, w_down):
    return (jax.nn.silu(x @ w_gate) * (x @ w_up)) @ w_down

def split_heads(t, n_heads):
    B, T, _ = t.shape
    return t.reshape(B, T, n_heads, HEAD_DIM).transpose(0, 2, 1, 3)

def rope(x, pos):
    half = HEAD_DIM // 2
    inv_freq = ROPE_THETA ** (-jnp.arange(half, dtype=jnp.float32) / half)
    ang = pos.astype(jnp.float32)[:, None] * inv_freq[None, :]
    cos = jnp.cos(ang).astype(x.dtype)
    sin = jnp.sin(ang).astype(x.dtype)
    x1, x2 = x[..., :half], x[..., half:]
    return jnp.concatenate([x1 * cos - x2 * sin, x1 * sin + x2 * cos], axis=-1)

def masked_softmax(s, mask, axes):
    s = jnp.where(mask, s.astype(jnp.float32), MASK_FILL)
    m = jnp.max(s, axis=axes, keepdims=True)
    p = jnp.where(mask, jnp.exp(s - m), 0.0)
    return p / jnp.maximum(jnp.sum(p, axis=axes, keepdims=True), 1e-30)

def stick_breaking_attention(q, k, v):
    B, H, T, Dh = q.shape
    nb = T // Q_BLOCK
    scale = Dh ** -0.5
    key_pos = jnp.arange(T)
    qb = jnp.moveaxis(q.reshape(B, H, nb, Q_BLOCK, Dh), 2, 0)

    def block(args):
        i, q_i = args
        q_pos = i * Q_BLOCK + jnp.arange(Q_BLOCK)
        z = jnp.einsum('bhqd,bhkd->bhqk', q_i, k).astype(jnp.float32) * scale
        strict = key_pos[None, :] < q_pos[:, None]
        log_beta = jax.nn.log_sigmoid(z)
        log_1m_beta = jnp.where(strict, jax.nn.log_sigmoid(-z), 0.0)
        log_stay = lax.cumsum(log_1m_beta, axis=3, reverse=True) - log_1m_beta
        w = jnp.where(strict, jnp.exp(log_beta + log_stay), 0.0)
        return jnp.einsum('bhqk,bhkd->bhqd', w.astype(v.dtype), v)

    out = lax.map(block, (jnp.arange(nb), qb))
    return jnp.moveaxis(out, 0, 2).reshape(B, H, T, Dh)

def compress(x_tok, pos_emb, w1, w2):
    B, G, T, Dh = x_tok.shape
    n_cmp = (T - CMP_BLOCK) // CMP_STRIDE + 1
    idx = jnp.arange(n_cmp)[:, None] * CMP_STRIDE + jnp.arange(CMP_BLOCK)[None, :]
    blocks = x_tok[:, :, idx, :] + pos_emb
    flat = blocks.reshape(B, G, n_cmp, CMP_BLOCK * Dh)
    return jax.nn.gelu(flat @ w1) @ w2

def native_sparse_attention(q, k_cmp, v_cmp, k_slc, v_slc, k_win, v_win, gates):
    B, H, T, Dh = q.shape
    G = NSA_KV_GROUPS
    R = H // G
    scale = Dh ** -0.5
    nb = T // Q_BLOCK
    n_cmp = k_cmp.shape[2]
    n_sel = T // SEL_BLOCK
    k_top = min(SEL_TOPK, n_sel)
    cmp_start = jnp.arange(n_cmp) * CMP_STRIDE
    cmp_end = cmp_start + CMP_BLOCK - 1
    sel_start = jnp.arange(n_sel) * SEL_BLOCK
    blk_ids = jnp.arange(n_sel)
    overlap = jnp.clip(jnp.minimum(cmp_start[:, None] + CMP_BLOCK, sel_start[None, :] + SEL_BLOCK)
                       - jnp.maximum(cmp_start[:, None], sel_start[None, :]), 0, None)
    cmp_to_sel = overlap.astype(jnp.float32) / CMP_BLOCK
    ks_blocks = k_slc.reshape(B, G, n_sel, SEL_BLOCK, Dh)
    vs_blocks = v_slc.reshape(B, G, n_sel, SEL_BLOCK, Dh)
    pad = ((0, 0), (0, 0), (WINDOW, 0), (0, 0))
    kw_pad = jnp.pad(k_win, pad)
    vw_pad = jnp.pad(v_win, pad)
    b_idx = jnp.arange(B)[:, None, None, None]
    g_idx = jnp.arange(G)[None, :, None, None]
    qb = jnp.moveaxis(q.reshape(B, G, R, nb, Q_BLOCK, Dh), 3, 0)
    gb = jnp.moveaxis(gates.reshape(B, G, R, nb, Q_BLOCK, N_GATES), 3, 0)

    def block(args):
        i, q_i, g_i = args
        q0 = i * Q_BLOCK
        q_pos = q0 + jnp.arange(Q_BLOCK)
        s_c = jnp.einsum('bgrqd,bgcd->bgrqc', q_i, k_cmp).astype(jnp.float32) * scale
        p_c = masked_softmax(s_c, cmp_end[None, :] <= q_pos[:, None], (-1,))
        o_c = jnp.einsum('bgrqc,bgcd->bgrqd', p_c.astype(v_cmp.dtype), v_cmp)
        imp = jnp.einsum('bgrqc,cn->bgqn', p_c, cmp_to_sel)
        forced = (blk_ids[None, :] == 0) | (blk_ids[None, :] == q_pos[:, None] // SEL_BLOCK)
        valid = sel_start[None, :] <= q_pos[:, None]
        imp = jnp.where(forced, jnp.inf, jnp.where(valid, imp, -jnp.inf))
        _, sel = lax.top_k(imp, k_top)
        k_g = ks_blocks[b_idx, g_idx, sel]
        v_g = vs_blocks[b_idx, g_idx, sel]
        tok_pos = sel[..., None] * SEL_BLOCK + jnp.arange(SEL_BLOCK)
        m_s = (tok_pos <= q_pos[:, None, None])[:, :, None]
        s_s = jnp.einsum('bgrqd,bgqnsd->bgrqns', q_i, k_g).astype(jnp.float32) * scale
        p_s = masked_softmax(s_s, m_s, (-2, -1))
        o_s = jnp.einsum('bgrqns,bgqnsd->bgrqd', p_s.astype(v_g.dtype), v_g)
        k_w = lax.dynamic_slice_in_dim(kw_pad, q0, WINDOW + Q_BLOCK, axis=2)
        v_w = lax.dynamic_slice_in_dim(vw_pad, q0, WINDOW + Q_BLOCK, axis=2)
        kv_pos = q0 - WINDOW + jnp.arange(WINDOW + Q_BLOCK)
        dist = q_pos[:, None] - kv_pos[None, :]
        m_w = (dist >= 0) & (dist < WINDOW) & (kv_pos[None, :] >= 0)
        s_w = jnp.einsum('bgrqd,bgkd->bgrqk', q_i, k_w).astype(jnp.float32) * scale
        p_w = masked_softmax(s_w, m_w, (-1,))
        o_w = jnp.einsum('bgrqk,bgkd->bgrqd', p_w.astype(v_w.dtype), v_w)
        out = g_i[..., 0:1] * o_c + g_i[..., 1:2] * o_s + g_i[..., 2:3] * o_w
        return out.astype(q_i.dtype)

    out = lax.map(block, (jnp.arange(nb), qb, gb))
    return jnp.moveaxis(out, 0, 3).reshape(B, H, T, Dh)

def group_rms(o, g):
    B, H, T, Dh = o.shape
    o = o.transpose(0, 2, 1, 3).reshape(B, T, H * Dh).astype(jnp.float32)
    return o * lax.rsqrt(jnp.mean(o * o, axis=-1, keepdims=True) + RMS_EPS) * g

def hybrid_mixer(h, w_in, cmp_pos_k, cmp_w1_k, cmp_w2_k, cmp_pos_v, cmp_w1_v, cmp_w2_v, mix_norm_g, w_out):
    B, T, _ = h.shape
    bounds = [int(b) for b in np.cumsum(IN_SPLITS)[:-1]]
    (sb_q, sb_k, sb_v, nsa_q, kc, vc, ksl, vsl, kwn, vwn, gate_logits) = jnp.split(h @ w_in, bounds, axis=-1)
    pos = jnp.arange(T)
    o_sb = stick_breaking_attention(split_heads(sb_q, SB_HEADS), split_heads(sb_k, SB_HEADS), split_heads(sb_v, SB_HEADS))
    q = rope(split_heads(nsa_q, NSA_HEADS), pos)
    k_cmp = compress(rope(split_heads(kc, NSA_KV_GROUPS), pos), cmp_pos_k, cmp_w1_k, cmp_w2_k)
    v_cmp = compress(split_heads(vc, NSA_KV_GROUPS), cmp_pos_v, cmp_w1_v, cmp_w2_v)
    k_slc = rope(split_heads(ksl, NSA_KV_GROUPS), pos)
    v_slc = split_heads(vsl, NSA_KV_GROUPS)
    k_win = rope(split_heads(kwn, NSA_KV_GROUPS), pos)
    v_win = split_heads(vwn, NSA_KV_GROUPS)
    gates = jax.nn.sigmoid(gate_logits.astype(jnp.float32)).reshape(B, T, NSA_HEADS, N_GATES).transpose(0, 2, 1, 3)
    o_nsa = native_sparse_attention(q, k_cmp, v_cmp, k_slc, v_slc, k_win, v_win, gates)
    y = jnp.concatenate([group_rms(o_sb, mix_norm_g[:SB_WIDTH]), group_rms(o_nsa, mix_norm_g[SB_WIDTH:])], axis=-1)
    return y.astype(h.dtype) @ w_out

def memory_cross_attention(x, mem, w_q, w_k, w_v, w_o):
    B, T, D = x.shape
    M = mem.shape[1]
    dh = D // MEM_HEADS
    q = (x @ w_q).reshape(B, T, MEM_HEADS, dh)
    k = (mem @ w_k).reshape(B, M, MEM_HEADS, dh)
    v = (mem @ w_v).reshape(B, M, MEM_HEADS, dh)
    s = jnp.einsum('bthd,bmhd->bhtm', q, k).astype(jnp.float32) * dh ** -0.5
    p = jax.nn.softmax(s, axis=-1).astype(v.dtype)
    o = jnp.einsum('bhtm,bmhd->bthd', p, v).reshape(B, T, D)
    return o @ w_o

def setup_inputs(seed: int = 0) -> dict:
    key = jax.random.key(seed)
    keys = iter(jax.random.split(key, 48))
    D = D_MODEL
    beta = DEEPNORM_BETA

    def nrm(shape, scale):
        return jax.random.normal(next(keys), shape, jnp.float32) * scale

    def gain(n):
        return 1.0 + nrm((DEPTH, n), 0.02)

    def bias(n):
        return nrm((DEPTH, n), 0.02)

    in_scale = jnp.asarray(np.concatenate([np.full((n,), beta if i in VALUE_SEGMENTS else 1.0, np.float32)
                                           for i, n in enumerate(IN_SPLITS)]))
    return {
        'x': nrm((BATCH, SEQ, D), 1.0),
        'mem': nrm((BATCH, MEM_TOKENS, D), 1.0),
        'ln1_g': gain(D), 'ln1_b': bias(D),
        'ffn1_gate': nrm((DEPTH, D, D_FF), D ** -0.5),
        'ffn1_up': nrm((DEPTH, D, D_FF), D ** -0.5 * beta),
        'ffn1_down': nrm((DEPTH, D_FF, D), D_FF ** -0.5 * beta),
        'w_in': nrm((DEPTH, D, IN_COLS), D ** -0.5) * in_scale,
        'cmp_pos_k': nrm((DEPTH, CMP_BLOCK, HEAD_DIM), 0.02),
        'cmp_w1_k': nrm((DEPTH, CMP_BLOCK * HEAD_DIM, CMP_HIDDEN), (CMP_BLOCK * HEAD_DIM) ** -0.5),
        'cmp_w2_k': nrm((DEPTH, CMP_HIDDEN, HEAD_DIM), CMP_HIDDEN ** -0.5),
        'cmp_pos_v': nrm((DEPTH, CMP_BLOCK, HEAD_DIM), 0.02),
        'cmp_w1_v': nrm((DEPTH, CMP_BLOCK * HEAD_DIM, CMP_HIDDEN), (CMP_BLOCK * HEAD_DIM) ** -0.5),
        'cmp_w2_v': nrm((DEPTH, CMP_HIDDEN, HEAD_DIM), CMP_HIDDEN ** -0.5),
        'mix_norm_g': gain(MIX_WIDTH),
        'w_out': nrm((DEPTH, MIX_WIDTH, D), MIX_WIDTH ** -0.5 * beta),
        'ln2_g': gain(D), 'ln2_b': bias(D),
        'mem_wq': nrm((DEPTH, D, D), D ** -0.5),
        'mem_wk': nrm((DEPTH, D, D), D ** -0.5),
        'mem_wv': nrm((DEPTH, D, D), D ** -0.5 * beta),
        'mem_wo': nrm((DEPTH, D, D), D ** -0.5 * beta),
        'ln3_g': gain(D), 'ln3_b': bias(D),
        'ffn2_gate': nrm((DEPTH, D, D_FF), D ** -0.5),
        'ffn2_up': nrm((DEPTH, D, D_FF), D ** -0.5 * beta),
        'ffn2_down': nrm((DEPTH, D_FF, D), D_FF ** -0.5 * beta),
        'ln4_g': gain(D), 'ln4_b': bias(D),
    }

def reference(x, mem, ln1_g, ln1_b, ffn1_gate, ffn1_up, ffn1_down, w_in, cmp_pos_k, cmp_w1_k, cmp_w2_k,
              cmp_pos_v, cmp_w1_v, cmp_w2_v, mix_norm_g, w_out, ln2_g, ln2_b, mem_wq, mem_wk, mem_wv, mem_wo,
              ln3_g, ln3_b, ffn2_gate, ffn2_up, ffn2_down, ln4_g, ln4_b):
    a = DEEPNORM_ALPHA
    for l in range(DEPTH):
        x = layer_norm(a * x + 0.5 * swiglu(x, ffn1_gate[l], ffn1_up[l], ffn1_down[l]), ln1_g[l], ln1_b[l])
        x = layer_norm(a * x + hybrid_mixer(x, w_in[l], cmp_pos_k[l], cmp_w1_k[l], cmp_w2_k[l], cmp_pos_v[l],
                                            cmp_w1_v[l], cmp_w2_v[l], mix_norm_g[l], w_out[l]), ln2_g[l], ln2_b[l])
        x = layer_norm(a * x + memory_cross_attention(x, mem, mem_wq[l], mem_wk[l], mem_wv[l], mem_wo[l]), ln3_g[l], ln3_b[l])
        x = layer_norm(a * x + 0.5 * swiglu(x, ffn2_gate[l], ffn2_up[l], ffn2_down[l]), ln4_g[l], ln4_b[l])
    return x


_drawn_inputs = setup_inputs


def setup_inputs(seed=0):
    import zlib

    import numpy as np

    out = dict(_drawn_inputs(seed))
    spreads = {}
    factors = {'cmp_pos_k': 8.0,
     'cmp_pos_v': 3.881,
     'mix_norm_g': 17.639,
     'ln2_g': 8.027,
     'ln2_b': 7.823,
     'ln3_g': 7.62,
     'ln3_b': 7.776,
     'ln4_g': 7.926,
     'ln4_b': 7.705}
    for name, (base, spread) in spreads.items():
        noise = np.random.default_rng([zlib.crc32(name.encode()), seed]).standard_normal(out[name].shape)
        drawn = base * np.exp(spread * noise) if base else spread * noise
        out[name] = jnp.asarray(drawn.astype(out[name].dtype))
    for name, factor in factors.items():
        out[name] = (out[name] * factor).astype(out[name].dtype)
    return out
```

```python
from contextlib import ExitStack

import numpy as np

import concourse.bass as bass
import concourse.mybir as mybir
from concourse.alu_op_type import AluOpType as ALU

F32 = mybir.dt.float32
F32R = mybir.dt.float32r
ACT = mybir.ActivationFunctionType
AX = mybir.AxisListType

P = 128
T = 256
TT = T // P
D = 2048
KD = D // P
DFF = 5504
KF = DFF // P
W = 512
NFULL = DFF // W
WL = DFF - NFULL * W
HD = 128
HALF = HD // 2
SBH, NSH, GROUPS = 8, 8, 2
REP = NSH // GROUPS
CB, CS, CH = 32, 16, 256
NC = (T - CB) // CS + 1
GC = GROUPS * NC
LOROW = 64
MH = 4
MK = D // MH // P
SCALE = float(HD) ** -0.5
MSCALE = float(D // MH) ** -0.5
ALPHA = 2.0 ** 0.25
LN_EPS, RMS_EPS = 1e-5, 1e-6
NEG = -1e30

AHEAD = 4
NRAW = 4
CHUNK = 1024
KHALF = 44
A, B, T0, T1 = range(4)
GELU = 0.7978845608028654
EPS1 = LN_EPS / ALPHA ** 2

C_FFN1 = 0
C_DOWN1 = C_FFN1 + 16 * (NFULL + 1)
C_K0 = C_DOWN1 + 2 * KHALF
C_WIN = C_K0 + 8
NWIN = 11
C_K1 = C_WIN + 8 * NWIN
C_CMP = C_K1 + 8
C_FILL = C_CMP + 16
C_V2 = C_FILL + 32
C_WOUT = C_V2 + 8
C_V3 = C_WOUT + 32
C_WQ = C_V3 + 8
C_WO = C_WQ + 32
C_FFN2 = C_WO + 32
C_DOWN2 = C_FFN2 + 16 * (NFULL + 1)
C_END = C_DOWN2 + 2 * KHALF

WIN = [("q", 0, 0), ("k", 0, 1024), ("v", 0, 2048), ("nq", 0, 3072), ("nq", 1, 3584), ("q", 1, 512),
       ("k", 1, 1536), ("v", 1, 2560), ("cmp", 0, 4096), ("slc", 0, 4608), ("win", 0, 5120)]
GATE_COL = 5632
NG = 24
SB_AT = {3: 0, 4: 2, 8: 4, 9: 6}

UNITS = [(g, br, tt) for g in range(GROUPS) for br in range(2) for tt in range(TT)]

K_ID, K_NEGU, K_NEG1, K_TRI, K_CAP, K_CM, K_SEL, K_CADD, K_CMUL, NCONST = (
    0, 128, 256, 384, 512, 896, 1152, 1184, 1216, 1248)


def constants():
    c = np.zeros((P, NCONST), np.float32)
    r, q = np.arange(P)[:, None], np.arange(P)[None, :]
    c[:, K_ID:K_ID + P] = r == q
    c[:, K_NEGU:K_NEGU + P] = np.where(r >= q, -1.0, 0.0)
    c[:, K_NEG1:K_NEG1 + P] = -1.0
    c[:, K_TRI:K_TRI + P] = q > r
    cap = np.where(q > r, 0.0, NEG)
    c[:, K_CAP:K_CAP + 3 * P] = np.concatenate([cap, np.zeros((P, P)), cap], 1)
    c[:, K_CM + P:K_CM + 2 * P] = np.where(q <= r, 0.0, NEG)
    for n in range(GC):
        c[n, K_SEL + n] = 1.0
        c[LOROW + n, K_SEL + n] = 1.0
    end = np.arange(NC) * CS + CB - 1
    for t in range(TT):
        ok = end[None, :] <= t * P + np.arange(P)[:, None]
        c[:, K_CADD + t * 16:K_CADD + t * 16 + NC] = np.where(ok, 0.0, NEG)
        c[:, K_CMUL + t * 16:K_CMUL + t * 16 + NC] = ok
    inv = np.float32(10000.0) ** (-np.arange(HALF, dtype=np.float32) / np.float32(HALF))
    pos = np.arange(T, dtype=np.float32).reshape(TT, P)
    ang = (pos[:, :, None] * inv).astype(np.float32).transpose(1, 0, 2)
    co, si = np.cos(ang), np.sin(ang)
    a = np.stack([np.concatenate([co, co], 2), np.concatenate([-si, si], 2)], 1)
    return c, np.ascontiguousarray(a, np.float32)


class Turns:

    def __init__(self):
        self.n = [0, 0, 0, 0]
        self.said = [0, 0, 0, 0]
        self.at = {}
        self.sends = {}
        self.split = {}

    def take(self, name, pair, split=False):
        self.at[name] = (pair, self.n[pair])
        self.n[pair] += 1
        if name not in ("sb", "z0", "z1") and name[0] not in ("acc", "d"):
            self.said[pair] += 1
            self.sends[name] = self.said[pair]
        if split:
            self.split[name] = len(self.split)


def turns():
    u = Turns()

    def acc(c, pair):
        u.take(("acc", c), pair)

    for g in range(4):
        u.take(("x", g), g, True)
    for f, c0 in ((1, C_FFN1), (2, C_FFN2)):
        if f == 2:
            for g in range(4):
                u.take(("x3", g), T0 + g % 2, True)
        acc(c0, A)
        for j in range(NFULL + 1):
            acc(c0 + 16 * j + 8, B)
            if j < NFULL:
                acc(c0 + 16 * j + 16, A)
            u.take(("h", f, j), T0, True)
        c1 = c0 + 16 * (NFULL + 1)
        u.take(("d", f, 0), A)
        u.take(("d", f, 1), B)
        if f == 1:
            for g in range(4):
                u.take(("mem", g), (T1, T0)[g % 2], True)
        u.take(("d", f, 2), T0)
        u.take(("d", f, 3), T1)
        if f == 2:
            break
        acc(C_K0, A)
        for g in range(4):
            u.take(("x1", g), T0 + g % 2, True)
        u.take(("kt", 0), T0)
        for n in range(NWIN):
            acc(C_WIN + 8 * n, (B, A)[n % 2])
            if n and WIN[n - 1][0] != "v":
                u.take(("w", n - 1), T0)
        u.take("sb", T1)
        acc(C_K1, A)
        u.take("gates", T1)
        u.take(("w", NWIN - 1), T0)
        acc(C_CMP, B)
        u.take(("kt", 1), T0)
        acc(C_CMP + 8, A)
        for s in range(32):
            n, k = divmod(s, 4)
            if k == 0:
                if n < 4:
                    u.take(("l1", "l2", "cs", "cp")[n], T1)
                if n == 2:
                    u.take(("kt", 2), T0)
                if n == 4:
                    u.take(("kt", 3), T0)
                u.take(("s", n), T0)
            if k == 2:
                u.take(("p", n), T1)
            if k == 3 and n % 4 == 0:
                u.take(("O", n // 4), B)
        for b in range(4):
            u.take(("acc", C_FILL + 8 * b), A)
        acc(C_V2, A)
        for g in range(4):
            u.take(("y", g), T0 + g % 2, True)
        for b in range(4):
            acc(C_WOUT + 8 * b, (B, A)[b % 2])
        acc(C_V3, B)
        for g in range(4):
            u.take(("x2", g), T0 + g % 2, True)
        for b in range(4):
            acc(C_WQ + 8 * b, (A, B)[b % 2])
            u.take(("qt", b), T0)
        u.take("z0", A)
        u.take("z1", B)
        for h in range(MH):
            u.take(("mp", h), T0)
            u.take(("mo", h), T1)
            if h:
                u.take(("ot", h - 1), A, True)
        u.take(("ot", MH - 1), B, True)
        for b in range(4):
            acc(C_WO + 8 * b, (A, B)[b % 2])
    return u


def w_raw(t, slot, cols, half=None):
    n = CHUNK * cols // W if cols < W and cols != CH else CHUNK
    if half is None:
        return t[:, slot, 0:2 * n].rearrange("p (k w) -> p k w", w=cols)
    return t[:, slot, half * n:(half + 1) * n]


def hybrid_layer(nc, d, out):
    U = turns()
    KB = 1024
    base = (nc.sbuf_base + 31) // 32 * 32
    o_raw, o_hi, o_lo, o_x = base, base + 32 * KB, base + 48 * KB, base + 64 * KB
    o_X, o_H, o_S = base + 80 * KB, base + 112 * KB, base + 200 * KB

    def sb(name, shape, dt, offset):
        return nc.alloc_sbuf_tensor_at(name, shape, dt, offset=offset)

    def two(name, kt, offset):
        return [sb(f"{name}_{n}", [P, kt, T], F32R, offset + i * kt * KB) for i, n in enumerate(("hi", "lo"))]

    raw = sb("raw", [P, NRAW, 2 * CHUNK], F32, o_raw)
    whi = sb("whi", [P, AHEAD, CHUNK], F32R, o_hi)
    wlo = sb("wlo", [P, AHEAD, CHUNK], F32R, o_lo)
    x_tok = sb("x_tok", [P, TT, D], F32, o_x)
    xT0 = two("xT0", KD, o_X)
    memT = two("memT", KD, o_X)
    oT = two("oT", KD, o_X)
    xT3 = two("xT3", KD, o_X)
    gb4 = sb("gb4", [P, 2, D], F32, o_X)
    hT = {1: two("hT1", KF, o_H), 2: two("hT2", KF, o_H)}
    gb1 = sb("gb1", [P, 2, D], F32, o_H)
    V = sb("V", [P, TT, D], F32, o_H)
    sba = sb("sba", [P, 2, 384], F32, o_H)
    sbl = sb("sbl", [P, 2, 384], F32, o_H + 3 * KB)
    rot = sb("rot", [P, W], F32, o_H + 6 * KB)
    angle = sb("angle", [P, 2, TT, P], F32, o_H + 8 * KB)
    kcT = sb("kcT", [P, 4, T], F32, o_H + 12 * KB)
    kstage = sb("kstage", [P, TT, W], F32, o_H)
    fs = sb("fs", [P, CB, GC], F32, o_H + 4 * KB)
    ug = sb("ug", [P, 4, 4, 32], F32, o_H + 4 * KB)
    w2 = sb("w2", [P, 2, 2, HD], F32, o_H + 10 * KB)
    x1T = two("x1T", KD, o_H + 16 * KB)
    FC = [sb(f"FC{i}", [P, CB, LOROW + GC], F32R, o_H + (16 + i * 12) * KB) for i in range(2)]
    pcs = sb("pcs", [P, TT, NSH, NC], F32, o_H + 16 * KB)
    pcp = sb("pcp", [P, TT, NSH, 32], F32, o_H + 18 * KB)
    pcT = sb("pcT", [P, TT, GROUPS, P], F32, o_H + 20 * KB)
    scrap = sb("scrap", [P, REP, T], F32, o_H + 32 * KB)
    hc = sb("hc", [P, 2, CH], F32, o_H + 40 * KB)
    vblk = sb("vblk", [P, GROUPS, W], F32, o_H + 42 * KB)
    posT = sb("posT", [P, 2, CB], F32, o_H + 46 * KB)
    kcmp = sb("kcmp", [P, GC], F32, o_H + 46 * KB + 512)
    yT = two("yT", KD, o_H + 16 * KB)
    x2T = two("x2T", KD, o_H + 16 * KB)
    mo_tok = sb("mo_tok", [P, TT, D], F32, o_H + 16 * KB)
    gb3 = sb("gb3", [P, 2, D], F32, o_H + 32 * KB)
    KT = sb("KT", [P, KD, T], F32, o_H + 48 * KB)
    sbq = sb("sbq", [P, SBH, T], F32, o_H + 64 * KB)
    nsq = sb("nsq", [P, NSH, T], F32, o_H + 72 * KB)
    gb2 = sb("gb2", [P, 2, D], F32, o_H + 64 * KB)
    qT = sb("qT", [P, KD, T], F32, o_H + 64 * KB)
    sbk = sb("sbk", [P, 4, T], F32, o_H + 80 * KB)
    sbv = sb("sbv", [P, TT, W], F32, o_H + 84 * KB)
    mg = sb("mg", [P, D], F32, o_H + 80 * KB)
    at = [o_S]

    def small(name, shape):
        t = sb(name, shape, F32, at[0])
        at[0] += (4 * int(np.prod(shape[1:])) + 31) // 32 * 32
        return t

    const = small("const", [P, NCONST])
    o_stage = at[0]
    stage = [small("stage0", [P, TT, W]), small("stage1", [P, TT, W])]
    sil = sb("sil", [P, TT, W], F32, o_stage)
    hbuf = sb("hbuf", [P, TT, W], F32, o_stage + 4 * KB)
    prob = sb("prob", [P, REP, T], F32, o_stage)
    probT = sb("probT", [P, REP, TT, P], F32, o_stage + 4 * KB)
    mprob = [sb(f"mprob{i}", [P, TT, T], F32, o_stage + 2 * i * KB) for i in range(2)]
    mprobT = [sb(f"mprobT{i}", [P, TT, TT, P], F32, o_stage + (4 + 2 * i) * KB) for i in range(2)]
    kslT = small("kslT", [P, GROUPS, T])
    kwnT = small("kwnT", [P, GROUPS, T])
    wg = sb("wg", [P, KD, NG], F32, at[0] - 2 * KB)
    vsw = small("vsw", [P, 2, TT, T])
    st = small("st", [P, TT, 4, 6])
    mv = small("mv", [P, TT, 2])
    rs = small("rs", [P, 4])
    rv = small("rv", [P, 4])
    ss = small("ss", [P, 4])
    gate = small("gate", [P, TT, NG])
    mx = small("mx", [P, 8])
    nm = small("nm", [P, 8])
    sm = small("sm", [P, 8])
    cf = small("cf", [P, 8])
    cmx = small("cmx", [P, 16])
    csm = small("csm", [P, 16])
    ccf = small("ccf", [P, 16])
    assert at[0] <= 229368

    ident = const[:, K_ID:K_ID + P]
    negu = const[:, K_NEGU:K_NEGU + P]
    neg1 = const[:, K_NEG1:K_NEG1 + P]
    tri = const[:, K_TRI:K_TRI + P]
    cap = const[:, K_CAP:K_CAP + 3 * P]
    cmask = const[:, K_CM:K_CM + 2 * P]
    sel = const[:, K_SEL:K_SEL + GC]
    cadd = const[:, K_CADD:K_CADD + 32].rearrange("p (t o c) -> p t o c", t=TT, o=1)[:, :, :, 0:NC]
    cmul = const[:, K_CMUL:K_CMUL + 32].rearrange("p (t o c) -> p t o c", t=TT, o=1)[:, :, :, 0:NC]

    with ExitStack() as ctx:
        ps = [ctx.enter_context(nc.psum_tensor(f"ps_{n}", [P, 2 * W], F32)) for n in ("A", "B", "T0", "T1")]

        def sem(name):
            return ctx.enter_context(nc.semaphore(name))

        landed = [sem(f"landed{i}") for i in range(NRAW)]
        hi_made, lo_made, multiplied = sem("hi_made"), sem("lo_made"), sem("multiplied")
        ready = [sem(f"ready_{n}") for n in ("A", "B", "T0", "T1")]
        freed = [sem(f"freed_{n}") for n in ("A", "B", "T0", "T1")]
        split_hi = sem("split_hi")
        x_in = [sem(f"x_in{g}") for g in range(4)]
        mem_in = [sem(f"mem_in{g}") for g in range(4)]
        const_in, angle_in, gate_in, cmp_in, mg_in = (
            sem("const_in"), sem("angle_in"), sem("gate_in"), sem("cmp_in"), sem("mg_in"))
        gb_in = [sem(f"gb_in{i}") for i in range(4)]
        norm_stats, norm_rs, normed = sem("norm_stats"), sem("norm_rs"), sem("normed")
        sb_z, sb_ln, sb_l, sb_r, sb_em, sb_w, sb_o, sb_out = (
            sem("sb_z"), sem("sb_ln"), sem("sb_l"), sem("sb_r"), sem("sb_em"), sem("sb_w"),
            sem("sb_o"), sem("sb_out"))
        cleared, fc_made, gelu_x, gelu_e, gelu_made = (
            sem("cleared"), sem("fc_made"), sem("gelu_x"), sem("gelu_e"), sem("gelu_made"))
        cs_max, cs_exp, cs_made = sem("cs_max"), sem("cs_exp"), sem("cs_made")
        ns_max, ns_exp, ns_prob = sem("ns_max"), sem("ns_exp"), sem("ns_prob")
        sq_made, rms_v, rms_rs, y_made = sem("sq_made"), sem("rms_v"), sem("rms_rs"), sem("y_made")
        m_z, m_max, m_exp = sem("m_z"), sem("m_max"), sem("m_exp")
        dve_step, act_step = sem("dve_step"), sem("act_step")
        stored = sem("stored")
        block = ctx.enter_context(nc.Block())

        def w_ready(e, name):
            e.wait_ge(ready[U.at[name][0]], U.sends[name])

        def w_free(e, name, more=0):
            p, n = U.at[name]
            if n:
                e.wait_ge(freed[p], n + more)

        def w_over(e, name):
            p, n = U.at[name]
            e.wait_ge(freed[p], n + 1)

        @block.sync
        def _(sp):
            def piece(n, slot, src, cols, wait=True):
                if wait:
                    sp.wait_ge(lo_made, 2 * (n - NRAW) + 2)
                k = src.shape[1]
                sp.dma_start(w_raw(raw, slot, cols)[:, 0:k, :], src).then_inc(landed[slot], 16)

            def cols_of(w, k0, k1, c0, n):
                return w.rearrange("(k p) n -> p k n", p=P)[:, k0:k1, bass.ds(c0, n)]

            def blk(w, c, c0, n=W, wait=True):
                for k in range(4):
                    piece(c // 2 + k if isinstance(c, int) else c.piece + k, k,
                          cols_of(w, 4 * k, 4 * k + 4, c0, n), n, wait or k > 3)

            class Chunk:
                def __init__(self, piece):
                    self.piece = piece

            def half_ffn(f, c0):
                g, u, dn = d[f"ffn{f}_gate"], d[f"ffn{f}_up"], d[f"ffn{f}_down"]
                blk(g, c0, 0, wait=f == 2)
                with sp.Fori(0, NFULL - 1) as i:
                    blk(u, Chunk(i * 8 + (c0 + 8) // 2), i * W)
                    blk(g, Chunk(i * 8 + (c0 + 16) // 2), i * W + W)
                blk(u, c0 + 16 * NFULL - 8, (NFULL - 1) * W)
                blk(g, c0 + 16 * NFULL, NFULL * W, WL)
                blk(u, c0 + 16 * NFULL + 8, NFULL * W, WL)
                for hf in range(2):
                    for m in range(KHALF // 2):
                        n = (c0 + 16 * (NFULL + 1)) // 2 + hf * KHALF // 2 + m
                        piece(n, n % NRAW, cols_of(dn, 2 * m, min(2 * m + 2, KF), hf * 2 * W, 2 * W), 2 * W)

            for g in range(4):
                sp.dma_start(x_tok[:, :, g * W:(g + 1) * W],
                             d["x"].rearrange("(t p) n -> p t n", p=P)[:, :, g * W:(g + 1) * W]).then_inc(x_in[g], 16)
            half_ffn(1, C_FFN1)
            blk(d["mem_wk"], C_K0, 0)
            for n, (_, _, c0) in enumerate(WIN):
                blk(d["w_in"], C_WIN + 8 * n, c0)
            blk(d["mem_wk"], C_K1, W)
            for i, w in enumerate(("cmp_w1_k", "cmp_w1_v")):
                for k in range(4):
                    piece((C_CMP + 8 * i) // 2 + k, k, cols_of(d[w], 8 * k, 8 * k + 8, 0, CH), CH)
            for b, (w, c) in enumerate((("mem_wk", 2), ("mem_wk", 3), ("mem_wv", 0), ("mem_wv", 1), ("mem_wv", 2))):
                blk(d[w], C_FILL + 8 * b, c * W)
            with sp.Fori(0, 4) as i:
                blk(d["w_out"], Chunk(i * 4 + C_WOUT // 2), i * W)
            blk(d["mem_wv"], C_V3, 3 * W)
            with sp.Fori(0, 4) as i:
                blk(d["mem_wq"], Chunk(i * 4 + C_WQ // 2), i * W)
            with sp.Fori(0, 4) as i:
                blk(d["mem_wo"], Chunk(i * 4 + C_WO // 2), i * W)
            half_ffn(2, C_FFN2)
            for g in range(4):
                sp.wait_ge(normed, 13 + g)
                sp.dma_start(out.rearrange("(t p) n -> p t n", p=P)[:, :, g * W:(g + 1) * W],
                             x_tok[:, :, g * W:(g + 1) * W]).then_inc(stored, 16)
            sp.wait_ge(stored, 64)

        @block.tensor
        def _(pe):
            def chunk(c, slot, lhs, kts, n, outs, first, last, skip=None):
                pe.wait_ge(lo_made, c + 1)
                for q, kt in enumerate(kts):
                    for t in range(TT):
                        for a, w in ((0, whi), (0, wlo), (1, whi)):
                            for cb, o in enumerate(outs[t]):
                                col = q * n * len(outs[t]) + cb * n
                                mm = pe.matmul(o[:, 0:n], lhs[a][:, kt, t * P:(t + 1) * P],
                                               w[:, slot, col:col + n],
                                               start=first and q == 0 and a == 0 and w is whi,
                                               stop=last and q == len(kts) - 1 and a == 1,
                                               skip_group_check=True)
                mm.then_inc(multiplied, skip or 1)

            def acc(pair):
                return [[ps[pair][:, t * W:(t + 1) * W]] for t in range(TT)]

            def step(c, k, lhs, pair, n=W):
                chunk(c + k, k % AHEAD, lhs, (2 * k, 2 * k + 1), n, acc(pair), k == 0, k == 7)

            def turn_group(name, src, n=4, more=None):
                p, _ = U.at[name]
                w_free(pe, name, 0) if more is None else pe.wait_ge(freed[p], more)
                for i in range(n):
                    for t in range(TT):
                        mm = pe.transpose(ps[p][:, i * T + t * P:i * T + (t + 1) * P], src(t, i), ident)
                mm.then_inc(ready[p], 1)

            def half_ffn(f, c0, xT, names):
                def h_group(j, n=4, i=None):
                    n_up = U.at[("acc", c0 + 16 * j + 8)][1] + 1
                    pe.wait_ge(freed[B], n_up if i is None else i + n_up)
                    turn_group(("h", f, j), lambda t, k: hbuf[:, t, k * P:(k + 1) * P], n,
                               None if i is None else i + U.at[("h", f, 0)][1])

                w_free(pe, ("acc", c0))
                for k in range(8):
                    if k % 2 == 0:
                        w_over(pe, names[k // 2])
                    step(c0, k, xT, A)
                with pe.Fori(0, NFULL - 1) as i:
                    pe.wait_ge(freed[B], i + U.at[("acc", c0 + 8)][1])
                    for k in range(8):
                        step(i * 16 + (c0 + 8), k, xT, B)
                    pe.wait_ge(freed[A], i + U.at[("acc", c0 + 16)][1])
                    for k in range(8):
                        if k == 3:
                            h_group(0, i=i)
                        step(i * 16 + (c0 + 16), k, xT, A)
                c = c0 + 16 * NFULL - 8
                w_free(pe, ("acc", c))
                for k in range(8):
                    step(c, k, xT, B)
                w_free(pe, ("acc", c + 8))
                for k in range(8):
                    if k == 3:
                        h_group(NFULL - 1)
                    step(c + 8, k, xT, A, WL)
                w_free(pe, ("acc", c + 16))
                for k in range(8):
                    step(c + 16, k, xT, B, WL)
                for hf in range(2):
                    pairs = ((A, B), (T0, T1))[hf]
                    for cb in range(2):
                        w_free(pe, ("d", f, 2 * hf + cb))
                    outs = [[ps[p][:, t * W:(t + 1) * W] for p in pairs] for t in range(TT)]
                    for kt in range(KF):
                        if hf == 0 and kt == 0:
                            w_over(pe, ("h", f, NFULL - 1))
                        if hf == 0 and kt == 3:
                            h_group(NFULL, WL // P)
                        if hf == 0 and kt == 4 * NFULL:
                            w_over(pe, ("h", f, NFULL))
                        if hf == 0 and f == 1 and kt % 8 == 0 and 8 <= kt <= 32:
                            g = kt // 8 - 1
                            pe.wait_ge(mem_in[g], 16)
                            turn_group(("mem", g), lambda t, i: stage[g % 2][:, t, i * P:(i + 1) * P])
                        chunk(c + 24 + hf * KHALF + kt, kt % AHEAD, hT[f], (kt,), W, outs, kt == 0, kt == KF - 1,
                              2 if kt == KF - 1 else 1)

            def norm_group(i, g):
                pe.wait_ge(normed, 4 * i + g + 1)
                turn_group((f"x{i + 1}", g), lambda t, k: x_tok[:, t, g * W + k * P:g * W + (k + 1) * P])

            def kt_group(b):
                src = stage[1] if b == 0 else kstage
                w_over(pe, ("acc", (C_K0, C_K1, C_FILL, C_FILL + 8)[b]))
                turn_group(("kt", b), lambda t, i: src[:, t, i * P:(i + 1) * P])

            pe.wait_ge(const_in, 16)
            for g in range(4):
                pe.wait_ge(x_in[g], 16)
                turn_group(("x", g), lambda t, i: x_tok[:, t, g * W + i * P:g * W + (i + 1) * P])
            half_ffn(1, C_FFN1, xT0, [("x", g) for g in range(4)])

            w_free(pe, ("acc", C_K0))
            w_over(pe, ("mem", 2))
            w_over(pe, ("mem", 3))
            for k in range(8):
                if k >= 6:
                    norm_group(0, k - 6)
                step(C_K0, k, memT, A)

            def sb_scores(h):
                hh = h % 4
                if h == 0:
                    w_free(pe, "sb")
                else:
                    pe.wait_ge(sb_em, h)
                z = ps[T1][:, 0:384]
                pe.matmul(z[:, 0:T], sbk[:, hh, 0:P], sbq[:, h, :], start=True, stop=True, skip_group_check=True)
                pe.matmul(z[:, T:384], sbk[:, hh, P:T], sbq[:, h, P:T], start=False, stop=True,
                          skip_group_check=True).then_inc(sb_z, 1)

            def sb_rest(h):
                pe.wait_ge(sb_l, h + 1)
                z, l = ps[T1][:, 0:384], sbl[:, h % 2, :]
                pe.matmul(z, negu, l, start=False, stop=True, skip_group_check=True)
                pe.matmul(z[:, P:T], neg1, l[:, T:384], start=False, stop=True,
                          skip_group_check=True).then_inc(sb_r, 1)

            def sb_values(h):
                pe.wait_ge(sb_w, h + 1)
                if h:
                    pe.wait_ge(sb_out, h)
                o, w, v = ps[T1][:, W:W + T], sba[:, h % 2, :], sbv[:, :, h % 4 * HD:(h % 4 + 1) * HD]
                pe.matmul(o[:, 0:P], w[:, 0:P], v[:, 0, :], start=True, stop=True, skip_group_check=True)
                pe.matmul(o[:, P:T], w[:, P:T], v[:, 0, :], start=False, stop=False, skip_group_check=True)
                pe.matmul(o[:, P:T], w[:, T:384], v[:, 1, :], start=False, stop=True,
                          skip_group_check=True).then_inc(sb_o, 1)

            def w_group(n):
                w_over(pe, ("acc", C_WIN + 8 * n))
                turn_group(("w", n), lambda t, i: stage[n % 2][:, t, i * P:(i + 1) * P],
                           2 if WIN[n][0] in ("slc", "win") else 4)

            for n in range(NWIN):
                c = C_WIN + 8 * n
                w_free(pe, ("acc", c))
                for k in range(8):
                    if n == 0:
                        if k in (1, 3):
                            norm_group(0, 2 + k // 2)
                        if k == 5:
                            kt_group(0)
                        if k % 2 == 0:
                            w_over(pe, ("x1", k // 2))
                    elif k == 3 and WIN[n - 1][0] != "v":
                        w_group(n - 1)
                    if k == 0 and n - 1 in SB_AT:
                        sb_values(SB_AT[n - 1] + 1)
                    if n in SB_AT:
                        h = SB_AT[n]
                        if k == 0:
                            if h in (0, 4):
                                w_over(pe, ("w", 1 if h == 0 else 6))
                                w_over(pe, ("acc", C_WIN + 8 * (2 if h == 0 else 7)))
                            sb_scores(h)
                        if k == 2:
                            sb_rest(h)
                        if k == 4:
                            sb_values(h)
                            sb_scores(h + 1)
                        if k == 6:
                            sb_rest(h + 1)
                    step(c, k, x1T, (B, A)[n % 2])

            w_free(pe, ("acc", C_K1))
            for k in range(8):
                if k == 1:
                    w_free(pe, "gates")
                    pe.wait_ge(gate_in, 16)
                    for t in range(TT):
                        for kt in range(KD):
                            for a in range(2):
                                mm = pe.matmul(ps[T1][:, t * NG:(t + 1) * NG],
                                               x1T[a][:, kt, t * P:(t + 1) * P].bitcast(F32), wg[:, kt, :],
                                               start=kt == 0 and a == 0, stop=kt == KD - 1 and a == 1,
                                               skip_group_check=True)
                    mm.then_inc(ready[T1], 1)
                if k == 3:
                    w_group(NWIN - 1)
                step(C_K1, k, memT, A)

            for i in range(2):
                c, pair = C_CMP + 8 * i, (B, A)[i]
                w_free(pe, ("acc", c))
                pe.wait_ge(fc_made, i + 1)
                for k in range(8):
                    if i == 0 and k == 3:
                        kt_group(1)
                    pe.wait_ge(lo_made, c + k + 1)
                    for q in range(4):
                        for w in (whi, wlo):
                            mm = pe.matmul(ps[pair][0:LOROW + GC, 0:CH], FC[i][:, 4 * k + q, :],
                                           w[:, k % AHEAD, q * CH:(q + 1) * CH],
                                           start=k == 0 and q == 0 and w is whi, stop=k == 7 and q == 3 and w is wlo,
                                           skip_group_check=True)
                    mm.then_inc(multiplied, 1)

            def cmp_step(n):
                if n == 0:
                    w_free(pe, "l1")
                    for i in range(2):
                        w_over(pe, ("acc", C_CMP + 8 * i))
                    for i in range(2):
                        for m in range(2):
                            mm = pe.matmul(ps[T1][:, (2 * i + m) * 32:(2 * i + m) * 32 + GC],
                                           hc[0:LOROW + GC, i, m * P:(m + 1) * P], sel[0:LOROW + GC, :],
                                           start=True, stop=True, skip_group_check=True)
                    mm.then_inc(ready[T1], 1)
                if n == 1:
                    w_free(pe, "l2")
                    pe.wait_ge(gelu_made, 1)
                    for m in range(2):
                        pe.matmul(ps[T1][:, 0:GC], w2[:, 0, m, :], ug[:, 3, m, 0:GC],
                                  start=m == 0, stop=m == 1, skip_group_check=True)
                    for g in range(GROUPS):
                        for r in range(REP):
                            for m in range(2):
                                mm = pe.matmul(ps[T1][32 * r:32 * r + NC, W + g * HD:W + (g + 1) * HD],
                                               ug[:, 3, 2 + m, g * NC:(g + 1) * NC], w2[:, 1, m, :],
                                               start=m == 0, stop=m == 1, skip_group_check=True)
                    mm.then_inc(ready[T1], 1)
                if n == 2:
                    w_free(pe, "cs")
                    w_over(pe, "l2")
                    for t in range(TT):
                        for h in range(NSH):
                            g = h // REP
                            o = (t * NSH + h) * NC
                            mm = pe.matmul(ps[T1][:, o:o + NC], nsq[:, h, t * P:(t + 1) * P],
                                           kcmp[:, g * NC:(g + 1) * NC], start=True, stop=True, skip_group_check=True)
                    mm.then_inc(ready[T1], 1)
                if n == 3:
                    w_free(pe, "cp")
                    pe.wait_ge(cs_made, 1)
                    for t in range(TT):
                        for g in range(GROUPS):
                            o = (t * GROUPS + g) * P
                            mm = pe.transpose(ps[T1][:, o:o + P],
                                              pcp[:, t, g * REP:(g + 1) * REP, :].rearrange("p a b -> p (a b)"), ident)
                    mm.then_inc(ready[T1], 1)

            for s in range(32):
                b, k = divmod(s, 8)
                n, part = divmod(s, 4)
                g, br, tq = UNITS[n]
                keys = (tq + 1) * P
                if part == 0:
                    if n < 4:
                        cmp_step(n)
                    if n == 2:
                        kt_group(2)
                    if n == 4:
                        kt_group(3)
                    w_free(pe, ("s", n))
                    if n == 0:
                        w_over(pe, ("w", NWIN - 1))
                    kT = (kslT, kwnT)[br]
                    for r in range(REP):
                        mm = pe.matmul(ps[T0][:, r * T:r * T + keys], nsq[:, g * REP + r, tq * P:(tq + 1) * P],
                                       kT[:, g, 0:keys], start=True, stop=True, skip_group_check=True)
                    mm.then_inc(ready[T0], 1)
                if part == 2:
                    w_free(pe, ("p", n))
                    pe.wait_ge(ns_prob, n + 1)
                    for r in range(REP):
                        for kk in range(tq + 1):
                            o = (r * TT + kk) * P
                            mm = pe.transpose(ps[T1][:, o:o + P], prob[:, r, kk * P:(kk + 1) * P], ident)
                    mm.then_inc(ready[T1], 1)
                if part == 3:
                    w_over(pe, ("p", n))
                    if n % 4 == 0:
                        w_free(pe, ("O", g))
                    for r in range(REP):
                        for kk in range(tq + 1):
                            mm = pe.matmul(ps[B][:, tq * W + r * HD:tq * W + (r + 1) * HD], probT[:, r, kk, :],
                                           vsw[:, br, kk, g * HD:(g + 1) * HD], start=br == 0 and r == 0 and kk == 0,
                                           stop=False, skip_group_check=True)
                    if n % 4 == 3:
                        w_over(pe, "cp")
                        for t in range(TT):
                            mm = pe.matmul(ps[B][:, t * W:(t + 1) * W], pcT[:, t, g, :], vblk[:, g, :],
                                           start=False, stop=True, skip_group_check=True)
                        mm.then_inc(ready[B], 1)
                if k == 0:
                    w_free(pe, ("acc", C_FILL + 8 * b))
                step(C_FILL + 8 * b, k, memT, A)

            w_free(pe, ("acc", C_V2))
            for k in range(8):
                if k in (3, 4, 5, 6):
                    g = k - 3
                    pe.wait_ge(y_made, 1 + g // 2)
                    src = (sbq, nsq)[g // 2]
                    turn_group(("y", g), lambda t, i: src[:, 4 * (g % 2) + i, t * P:(t + 1) * P])
                step(C_V2, k, memT, A)

            for b in range(4):
                c, pair = C_WOUT + 8 * b, (B, A)[b % 2]
                w_free(pe, ("acc", c))
                for k in range(8):
                    if b == 0 and k % 2 == 0:
                        w_over(pe, ("y", k // 2))
                    step(c, k, yT, pair)

            w_free(pe, ("acc", C_V3))
            for k in range(8):
                if k >= 6:
                    norm_group(1, k - 6)
                step(C_V3, k, memT, B)

            for b in range(4):
                c, pair = C_WQ + 8 * b, (A, B)[b % 2]
                w_free(pe, ("acc", c))
                for k in range(8):
                    if b == 0:
                        if k in (1, 3):
                            norm_group(1, 2 + k // 2)
                        if k % 2 == 0:
                            w_over(pe, ("x2", k // 2))
                    elif k == 3:
                        w_over(pe, ("acc", C_WQ + 8 * b - 8))
                        turn_group(("qt", b - 1), lambda t, i: stage[(b - 1) % 2][:, t, i * P:(i + 1) * P])
                    step(c, k, x2T, pair)
            w_over(pe, ("acc", C_WQ + 24))
            turn_group(("qt", 3), lambda t, i: stage[1][:, t, i * P:(i + 1) * P])

            for h in range(MH):
                if h % 2 == 0:
                    w_free(pe, f"z{h // 2}")
                w_over(pe, ("qt", h))
                for t in range(TT):
                    for k in range(MK):
                        mm = pe.matmul(ps[h // 2][:, h % 2 * W + t * T:h % 2 * W + (t + 1) * T],
                                       qT[:, MK * h + k, t * P:(t + 1) * P], KT[:, MK * h + k, :],
                                       start=k == 0, stop=k == MK - 1, skip_group_check=True)
                mm.then_inc(m_z, 1)

            def o_group(h):
                w_over(pe, ("mo", h))
                turn_group(("ot", h), lambda t, i: mo_tok[:, t, h * W + i * P:h * W + (i + 1) * P])

            for h in range(MH):
                w_free(pe, ("mp", h))
                pe.wait_ge(m_exp, h + 1)
                for t in range(TT):
                    for m in range(TT):
                        mm = pe.transpose(ps[T0][:, (t * TT + m) * P:(t * TT + m + 1) * P],
                                          mprob[h % 2][:, t, m * P:(m + 1) * P], ident)
                mm.then_inc(ready[T0], 1)
                w_over(pe, ("mp", h))
                w_free(pe, ("mo", h))
                for t in range(TT):
                    for m in range(TT):
                        mm = pe.matmul(ps[T1][:, t * W:(t + 1) * W], mprobT[h % 2][:, t, m, :],
                                       V[:, m, h * W:(h + 1) * W], start=m == 0, stop=m == TT - 1,
                                       skip_group_check=True)
                mm.then_inc(ready[T1], 1)
                if h:
                    o_group(h - 1)
            o_group(MH - 1)

            for b in range(4):
                c, pair = C_WO + 8 * b, (A, B)[b % 2]
                w_free(pe, ("acc", c))
                for k in range(8):
                    if b == 0 and k % 2 == 0:
                        w_over(pe, ("ot", k // 2))
                    step(c, k, oT, pair)

            for g in range(4):
                norm_group(2, g)
            half_ffn(2, C_FFN2, xT3, [("x3", g) for g in range(4)])

        def size(c):
            for c0 in (C_FFN1, C_FFN2):
                if c0 + 16 * NFULL <= c < c0 + 16 * (NFULL + 1):
                    return CHUNK * WL // W
            return CHUNK

        def void(c):
            return any(c == c0 + hf * KHALF + KF for c0 in (C_DOWN1, C_DOWN2) for hf in range(2))

        def plus(i, step, x):
            return x if i is None else i * step + x

        def make_hi(act, c, i=None):
            if c >= C_END or void(c):
                return
            slot, half, n = c // 2 % NRAW, c % 2, size(c)
            if half == 0:
                act.wait_ge(landed[slot], plus(i, 32, 16 * (c // 8 + 1)))
            if c >= AHEAD:
                act.wait_ge(multiplied, plus(i, 16, c - AHEAD + 1))
            act.activation(whi[:, c % AHEAD, 0:n], raw[:, slot, half * n:(half + 1) * n], ACT.Copy).then_inc(
                hi_made, 2 if void(c + 1) else 1)

        def make_lo(dve, c, i=None):
            if c >= C_END or void(c):
                return
            slot, half, n = c // 2 % NRAW, c % 2, size(c)
            dve.wait_ge(hi_made, plus(i, 16, c + 1))
            dve.tensor_tensor(wlo[:, c % AHEAD, 0:n], raw[:, slot, half * n:(half + 1) * n],
                              whi[:, c % AHEAD, 0:n].bitcast(F32), ALU.subtract).then_inc(
                lo_made, 2 if void(c + 1) else 1)

        def split_wait(e, name, i=None):
            e.wait_ge(split_hi, plus(i, 1, U.split[name] + 1))

        sb_slot = {}
        for n, h in SB_AT.items():
            sb_slot[8 * n] = [("z", h)]
            sb_slot[8 * n + 2] = [("r", h)]
            sb_slot[8 * n + 4] = [("o", h), ("z", h + 1)]
            sb_slot[8 * n + 6] = [("r", h + 1)]
            sb_slot[8 * n + 8] = [("o", h + 1)]
        for n, h in SB_AT.items():
            if n + 1 in SB_AT:
                sb_slot[8 * n + 8] = [("o", h + 1), ("z", SB_AT[n + 1])]

        @block.scalar
        def _(act):
            steps = [0]

            def chain(ins):
                steps[0] += 1
                ins.then_inc(act_step, 1)
                act.wait_ge(act_step, steps[0])

            def group_hi(name, dst, kt, n=4, i=None):
                p, _ = U.at[name]
                act.wait_ge(ready[p], plus(i, 1, U.sends[name]))
                to = dst[0][:, kt:kt + n, :] if i is None else dst[0][:, bass.ds(i * 4, n), :]
                act.activation(to, ps[p][:, 0:n * T].rearrange("p (k t) -> p k t", t=T), ACT.Copy).then_inc(split_hi, 1)

            def group_copy(name, dst):
                w_ready(act, name)
                p, _ = U.at[name]
                n = dst.shape[1]
                act.activation(dst, ps[p][:, 0:n * T].rearrange("p (k t) -> p k t", t=T), ACT.Copy).then_inc(freed[p], 1)

            def block_copy(c, dst, scale=1.0):
                act.wait_ge(multiplied, c + 8)
                p, _ = U.at[("acc", c)]
                act.activation(dst, ps[p][:, :].rearrange("p (t w) -> p t w", t=TT), ACT.Copy,
                               scale=scale).then_inc(freed[p], 1)

            def root(made, n, done, col=0):
                act.wait_ge(made, n)
                chain(act.activation(rs[:, col:col + 2], rv[:, col:col + 2], ACT.Ln))
                act.activation(rs[:, col:col + 2], rs[:, col:col + 2], ACT.Exp, scale=-0.5).then_inc(done, 1)

            def half_ffn(f, c0, extra):
                def silu(j, n=W, i=None):
                    act.wait_ge(multiplied, plus(i, 16, c0 + 16 * j + 8))
                    if i is not None or j:
                        act.wait_ge(freed[B], plus(i, 1, U.at[("acc", c0 + 16 * j - 8)][1] + 1))
                    act.activation(sil[:, :, 0:n], ps[A][:, :].rearrange("p (t w) -> p t w", t=TT)[:, :, 0:n],
                                   ACT.Silu).then_inc(freed[A], 1)

                for k in range(8):
                    make_hi(act, c0 + k + AHEAD)
                silu(0)
                with act.Fori(0, NFULL - 1) as i:
                    for k in range(8):
                        make_hi(act, c0 + 8 + k + AHEAD, i)
                    for k in range(8):
                        if k == 4:
                            group_hi(("h", f, 0), hT[f], 0, 4, i)
                        make_hi(act, c0 + 16 + k + AHEAD, i)
                    silu(1, W, i)
                c = c0 + 16 * NFULL - 8
                for k in range(8):
                    make_hi(act, c + k + AHEAD)
                for k in range(8):
                    if k == 4:
                        group_hi(("h", f, NFULL - 1), hT[f], 4 * NFULL - 4)
                    make_hi(act, c + 8 + k + AHEAD)
                silu(NFULL, WL)
                for k in range(8):
                    make_hi(act, c + 16 + k + AHEAD)
                for hf in range(2):
                    for kt in range(KF):
                        if hf == 0 and kt == 4:
                            group_hi(("h", f, NFULL), hT[f], 4 * NFULL, WL // P)
                        extra(hf, kt)
                        for q in ((kt + 4,) if kt < KF - 1 else (KHALF + 2, KHALF + 3)):
                            make_hi(act, c + 24 + hf * KHALF + q)

            mem_r = d["mem"].rearrange("(t p) n -> p t n", p=P)

            def load_mem(g):
                act.dma_start(stage[g % 2][:, :, :], mem_r[:, :, g * W:(g + 1) * W]).then_inc(mem_in[g], 16)

            def load_gb(i, dst, wait):
                act.wait_ge(multiplied, wait)
                act.dma_start(dst[:, :, :], d["ln"][i:i + 1, :, :].to_broadcast([P, 2, D])).then_inc(gb_in[i], 16)

            def extra1(hf, kt):
                if hf == 0 and kt == 5:
                    w_over(act, ("acc", C_DOWN1 - 8))
                    load_mem(0)
                    load_mem(1)
                if hf == 0 and kt % 8 == 0 and 8 <= kt <= 32:
                    g = kt // 8 - 1
                    group_hi(("mem", g), memT, 4 * g)
                    if g < 2:
                        load_mem(g + 2)
                if hf == 1 and kt == 20:
                    load_gb(0, gb1, C_DOWN1 + KHALF + 16)

            def extra2(hf, kt):
                if hf == 0 and kt == 8:
                    load_gb(3, gb4, C_DOWN2)

            act.dma_start(const[:, :], d["const"]).then_inc(const_in, 16)
            act.dma_start(wg[:, :, :], d["gate_w"]).then_inc(gate_in, 16)
            for c in range(AHEAD):
                if c == 2:
                    group_hi(("x", 0), xT0, 0)
                    group_hi(("x", 1), xT0, 4)
                make_hi(act, c)
            group_hi(("x", 2), xT0, 8)
            group_hi(("x", 3), xT0, 12)
            half_ffn(1, C_FFN1, extra1)

            for k in range(8):
                if k == 1:
                    root(norm_stats, 1, norm_rs)
                if k >= 6:
                    group_hi(("x1", k - 6), x1T, 4 * (k - 6))
                make_hi(act, C_K0 + k + AHEAD)
            block_copy(C_K0, stage[1][:, :, :])

            dest = {"q": lambda i: sbq[:, 4 * i:4 * i + 4, :], "k": lambda i: sbk[:, :, :],
                    "nq": lambda i: nsq[:, 4 * i:4 * i + 4, :], "cmp": lambda i: kcT[:, :, :],
                    "slc": lambda i: kslT[:, :, :], "win": lambda i: kwnT[:, :, :]}
            for n, (what, i, _) in enumerate(WIN):
                c = C_WIN + 8 * n
                for k in range(8):
                    if n == 0:
                        if k == 1:
                            group_hi(("x1", 2), x1T, 8)
                        if k == 3:
                            group_hi(("x1", 3), x1T, 12)
                        if k == 4:
                            act.wait_ge(normed, 4)
                            act.dma_start(angle[:, :, :, :], d["angle"]).then_inc(angle_in, 16)
                            act.dma_start(w2[:, :, :, :], d["cmp_w2"]).then_inc(cmp_in, 16)
                        if k == 5:
                            group_copy(("kt", 0), KT[:, 0:4, :])
                    elif k == 3 and WIN[n - 1][0] != "v":
                        group_copy(("w", n - 1), dest[WIN[n - 1][0]](WIN[n - 1][1]))
                    for part, h in sb_slot.get(8 * n + k, ()):
                        w = sba[:, h % 2, :]
                        if part == "z":
                            act.wait_ge(sb_z, h + 1)
                            if h >= 2:
                                act.wait_ge(sb_o, h - 1)
                            chain(act.activation(w, ps[T1][:, 0:384], ACT.Abs))
                            chain(act.activation(w, w, ACT.Exp, scale=-1.0))
                            act.activation(w, w, ACT.Ln, bias=1.0).then_inc(sb_ln, 1)
                        if part == "r":
                            act.wait_ge(sb_em, h + 1)
                            act.activation(w, w, ACT.Exp).then_inc(sb_w, 1)
                    make_hi(act, c + k + AHEAD)
                if what == "q":
                    block_copy(c, stage[n % 2][:, :, :], SCALE)
                if what == "k":
                    block_copy(c, stage[n % 2][:, :, :])
                if what == "v":
                    block_copy(c, sbv[:, :, :])

            for k in range(8):
                if k == 1:
                    w_ready(act, "gates")
                    act.dma_start(posT[:, :, :], d["pos"]).then_inc(cmp_in, 16)
                    act.dma_start(mg[:, :], d["mix_norm_g"].to_broadcast([P, D])).then_inc(mg_in, 16)
                    act.activation(gate[:, :, :], ps[T1][:, 0:TT * NG].rearrange("p (t n) -> p t n", t=TT), ACT.Exp,
                                   scale=-1.0).then_inc(freed[T1], 1)
                if k == 3:
                    group_copy(("w", NWIN - 1), dest["win"](0))
                make_hi(act, C_K1 + k + AHEAD)
            block_copy(C_K1, kstage[:, :, :])

            for i in range(2):
                for k in range(8):
                    if i == 0 and k == 3:
                        group_copy(("kt", 1), KT[:, 4:8, :])
                    make_hi(act, C_CMP + 8 * i + k + AHEAD)
                c, p = C_CMP + 8 * i, (B, A)[i]
                act.wait_ge(multiplied, c + 8)
                act.activation(hc[0:LOROW + GC, i, :], ps[p][0:LOROW + GC, 0:CH], ACT.Copy).then_inc(freed[p], 1)

            def outputs(g):
                w_ready(act, ("O", g))
                act.activation(nsq[:, g * REP:(g + 1) * REP, :].rearrange("p r (t d) -> p t r d", t=TT),
                               ps[B][:, :].rearrange("p (t r d) -> p t r d", t=TT, r=REP), ACT.Copy).then_inc(freed[B], 1)

            for s in range(32):
                b, k = divmod(s, 8)
                n, part = divmod(s, 4)
                g, br, tq = UNITS[n]
                keys = (tq + 1) * P
                if part == 0:
                    if n == 2:
                        group_copy(("kt", 2), KT[:, 8:12, :])
                    if n == 4:
                        group_copy(("kt", 3), KT[:, 12:16, :])
                        outputs(0)
                    if n == 3:
                        w_ready(act, "cp")
                        act.activation(pcT[:, :, :, :].rearrange("p t g q -> p (t g q)"), ps[T1][:, 0:TT * GROUPS * P],
                                       ACT.Copy).then_inc(freed[T1], 1)
                    act.wait_ge(ns_max, n + 1)
                    for r in range(REP):
                        e = act.activation(prob[:, r, 0:keys], prob[:, r, 0:keys], ACT.Exp, bias=nm[:, r:r + 1],
                                           scale=SCALE, accum_out=sm[:, r:r + 1])
                    e.then_inc(ns_exp, 1)
                if s == 1:
                    act.wait_ge(gelu_x, 1)
                    act.activation(ug[:, 2, :, 0:GC], ug[:, 1, :, 0:GC], ACT.Exp, scale=-2.0 * GELU).then_inc(gelu_e, 1)
                if s == 9:
                    act.wait_ge(cs_max, 1)
                    act.activation(pcs[:, :, :, :], pcs[:, :, :, :], ACT.Exp, scale=SCALE).then_inc(cs_exp, 1)
                if part == 2:
                    w_ready(act, ("p", n))
                    act.activation(probT[:, :, 0:tq + 1, :],
                                   ps[T1][:, :].rearrange("p (r k q) -> p r k q", r=REP, k=TT)[:, :, 0:tq + 1, :],
                                   ACT.Copy).then_inc(freed[T1], 1)
                make_hi(act, C_FILL + s + AHEAD)
                if k == 7:
                    if b < 2:
                        block_copy(C_FILL + 8 * b, kstage[:, :, :])
                    else:
                        block_copy(C_FILL + 8 * b, V[:, :, (b - 2) * W:(b - 1) * W])

            def squares(half, src):
                for t, o in enumerate((prob, scrap)):
                    e = act.activation(o[:, :, :].rearrange("p a b -> p (a b)").rearrange("p (h d) -> p h d", h=8),
                                       src[:, :, t * P:(t + 1) * P], ACT.Square, scale=1.0 / 32,
                                       accum_out=ss[:, 2 * half + t:2 * half + t + 1])
                e.then_inc(sq_made, 1)

            for k in range(8):
                if k == 0:
                    squares(0, sbq)
                    root(rms_v, 1, rms_rs)
                    outputs(1)
                    act.wait_ge(freed[B], U.at[("O", 1)][1] + 1)
                    squares(1, nsq)
                if k == 1:
                    root(rms_v, 2, rms_rs, 2)
                if k in (3, 4, 5, 6):
                    group_hi(("y", k - 3), yT, 4 * (k - 3))
                make_hi(act, C_V2 + k + AHEAD)
            block_copy(C_V2, V[:, :, 2 * W:3 * W])

            for k in range(32):
                if k == 4:
                    load_gb(1, gb2, C_V2 + 8)
                make_hi(act, C_WOUT + k + AHEAD)

            for k in range(8):
                if k == 1:
                    root(norm_stats, 2, norm_rs)
                if k >= 6:
                    group_hi(("x2", k - 6), x2T, 4 * (k - 6))
                make_hi(act, C_V3 + k + AHEAD)
            block_copy(C_V3, V[:, :, 3 * W:4 * W])

            for b in range(4):
                for k in range(8):
                    if b == 0 and k in (1, 3):
                        group_hi(("x2", 2 + k // 2), x2T, 8 + 4 * (k // 2))
                    if b and k == 3:
                        group_copy(("qt", b - 1), qT[:, 4 * b - 4:4 * b, :])
                    make_hi(act, C_WQ + 8 * b + k + AHEAD)
                block_copy(C_WQ + 8 * b, stage[b % 2][:, :, :])
            group_copy(("qt", 3), qT[:, 12:16, :])

            def m_exps(h):
                act.wait_ge(m_max, h + 1)
                if h >= 2:
                    w_ready(act, ("mp", h - 2))
                for t in range(TT):
                    e = act.activation(mprob[h % 2][:, t, :], ps[h // 2][:, h % 2 * W + t * T:h % 2 * W + (t + 1) * T],
                                       ACT.Exp, bias=nm[:, 2 * h + t:2 * h + t + 1], scale=MSCALE,
                                       accum_out=sm[:, 2 * h + t:2 * h + t + 1])
                e.then_inc(m_exp, 1)

            m_exps(0)
            m_exps(1)
            for h in range(MH):
                if h:
                    group_hi(("ot", h - 1), oT, 4 * h - 4)
                if h + 2 < MH:
                    m_exps(h + 2)
            group_hi(("ot", MH - 1), oT, 4 * MH - 4)
            for k in range(32):
                if k == 2:
                    load_gb(2, gb3, C_WO)
                make_hi(act, C_WO + k + AHEAD)

            root(norm_stats, 3, norm_rs)
            for g in range(4):
                group_hi(("x3", g), xT3, 4 * g)
            half_ffn(2, C_FFN2, extra2)
            root(norm_stats, 4, norm_rs)

        @block.vector
        def _(dve):
            steps = [0]

            def did(ins):
                steps[0] += 1
                ins.then_inc(dve_step, 1)

            def see():
                dve.wait_ge(dve_step, steps[0])

            def chain(ins):
                did(ins)
                see()

            def group_lo(name, dst, kt, n=4, i=None):
                p, _ = U.at[name]
                split_wait(dve, name, i)
                at = slice(kt, kt + n) if i is None else bass.ds(i * 4, n)
                dve.tensor_tensor(dst[1][:, at, :], ps[p][:, 0:n * T].rearrange("p (k t) -> p k t", t=T),
                                  dst[0][:, at, :].bitcast(F32), ALU.subtract).then_inc(freed[p], 1)

            def half_ffn(f, c0, extra):
                def hidden(j, n=W, i=None):
                    dve.wait_ge(multiplied, plus(i, 16, c0 + 16 * j + 16))
                    dve.wait_ge(freed[A], plus(i, 1, U.at[("acc", c0 + 16 * j)][1] + 1))
                    dve.tensor_tensor(hbuf[:, :, 0:n], ps[B][:, :].rearrange("p (t w) -> p t w", t=TT)[:, :, 0:n],
                                      sil[:, :, 0:n], ALU.mult).then_inc(freed[B], 1)

                for k in range(8):
                    make_lo(dve, c0 + k + AHEAD)
                with dve.Fori(0, NFULL - 1) as i:
                    for k in range(8):
                        make_lo(dve, c0 + 8 + k + AHEAD, i)
                    hidden(0, W, i)
                    for k in range(8):
                        if k == 4:
                            group_lo(("h", f, 0), hT[f], 0, 4, i)
                        make_lo(dve, c0 + 16 + k + AHEAD, i)
                c = c0 + 16 * NFULL - 8
                for k in range(8):
                    make_lo(dve, c + k + AHEAD)
                hidden(NFULL - 1)
                for k in range(8):
                    if k == 4:
                        group_lo(("h", f, NFULL - 1), hT[f], 4 * NFULL - 4)
                    make_lo(dve, c + 8 + k + AHEAD)
                for k in range(8):
                    make_lo(dve, c + 16 + k + AHEAD)
                hidden(NFULL, WL)
                for hf in range(2):
                    for kt in range(KF):
                        if hf == 0 and kt == 4:
                            group_lo(("h", f, NFULL), hT[f], 4 * NFULL, WL // P)
                        extra(hf, kt)
                        if hf == 1 and kt == 0:
                            norm_add(C[f] + KHALF, ("d", f, 0), 0, 0.5)
                        if hf == 1 and kt == 1:
                            norm_add(C[f] + KHALF, ("d", f, 1), 1, 0.5)
                        for q in ((kt + 4,) if kt < KF - 1 else (KHALF + 2, KHALF + 3)):
                            make_lo(dve, c + 24 + hf * KHALF + q)

            C = {1: C_DOWN1, 2: C_DOWN2}

            def norm_add(c, name, b, factor):
                p, _ = U.at[name]
                dve.wait_ge(multiplied, c)
                x = x_tok[:, :, b * W:(b + 1) * W]
                dve.scalar_tensor_tensor(out=x, in0=ps[p][:, :].rearrange("p (t w) -> p t w", t=TT),
                                         scalar=factor / ALPHA, in1=x, op0=ALU.mult, op1=ALU.add).then_inc(freed[p], 1)
                w_over(dve, name)
                for t in range(TT):
                    did(dve.bn_stats(st[:, t, b, :], x_tok[:, t, b * W:(b + 1) * W]))

            def norm_finish():
                see()
                for t in range(TT):
                    did(dve.bn_aggr(mv[:, t, :], st[:, t, :, :].rearrange("p a b -> p (a b)")))
                see()
                dve.tensor_scalar(rv[:, 0:TT], mv[:, :, 1], EPS1, None, ALU.add).then_inc(norm_stats, 1)

            def sharpen(col=0):
                r, v, w = rs[:, col:col + 2], rv[:, col:col + 2], cf[:, 0:2]
                chain(dve.tensor_tensor(w, r, r, ALU.mult))
                chain(dve.scalar_tensor_tensor(out=w, in0=w, scalar=-0.5, in1=v, op0=ALU.mult, op1=ALU.mult))
                chain(dve.scalar_tensor_tensor(out=r, in0=w, scalar=1.5, in1=r, op0=ALU.add, op1=ALU.mult))

            def norm_piece(i, g, gb):
                if g == 0:
                    dve.wait_ge(norm_rs, i + 1)
                    sharpen()
                    dve.wait_ge(gb_in[i], 16)
                x = [x_tok[:, t, g * W:(g + 1) * W] for t in range(TT)]
                for t in range(TT):
                    did(dve.scalar_tensor_tensor(out=x[t], in0=x[t], scalar=mv[:, t, 0:1],
                                                 in1=gb[:, 0, g * W:(g + 1) * W], op0=ALU.subtract, op1=ALU.mult))
                see()
                for t in range(TT):
                    e = dve.scalar_tensor_tensor(out=x[t], in0=x[t], scalar=rs[:, t:t + 1],
                                                 in1=gb[:, 1, g * W:(g + 1) * W], op0=ALU.mult, op1=ALU.add)
                e.then_inc(normed, 1)

            def extra1(hf, kt):
                if hf == 0 and kt % 8 == 0 and 8 <= kt <= 32:
                    g = kt // 8 - 1
                    group_lo(("mem", g), memT, 4 * g)

            for c in range(AHEAD):
                if c == 2:
                    group_lo(("x", 0), xT0, 0)
                    group_lo(("x", 1), xT0, 4)
                make_lo(dve, c)
            group_lo(("x", 2), xT0, 8)
            group_lo(("x", 3), xT0, 12)
            half_ffn(1, C_FFN1, extra1)

            for k in range(8):
                if k == 0:
                    norm_add(C_K0, ("d", 1, 2), 2, 0.5)
                    norm_add(C_K0, ("d", 1, 3), 3, 0.5)
                    norm_finish()
                if 1 <= k <= 4:
                    norm_piece(0, k - 1, gb1)
                if k >= 6:
                    group_lo(("x1", k - 6), x1T, 4 * (k - 6))
                make_lo(dve, C_K0 + k + AHEAD)

            def rotate(c, n, dst, cols):
                p, _ = U.at[("acc", c)]
                heads = cols // HD
                for t in range(TT):
                    x = ps[p][:, t * W:t * W + cols].rearrange("p (h d) -> p h d", d=HD)
                    o = dst[:, t, 0:cols].rearrange("p (h d) -> p h d", d=HD)
                    r = rot[:, 0:cols].rearrange("p (h d) -> p h d", d=HD)
                    co = angle[:, 0, t:t + 1, :].to_broadcast([P, heads, HD])
                    si = angle[:, 1, t:t + 1, :].to_broadcast([P, heads, HD])
                    dve.tensor_tensor(o, x, co, ALU.mult)
                    dve.tensor_tensor(r[:, :, 0:HALF], x[:, :, HALF:HD], si[:, :, 0:HALF], ALU.mult)
                    chain(dve.tensor_tensor(r[:, :, HALF:HD], x[:, :, 0:HALF], si[:, :, HALF:HD], ALU.mult))
                    e = dve.tensor_tensor(o, o, r, ALU.add)
                    if t == 0 or cols < W:
                        chain(e)
                return e

            for n, (what, i, _) in enumerate(WIN):
                c = C_WIN + 8 * n
                for k in range(8):
                    if n == 0 and k in (1, 3):
                        group_lo(("x1", 2 + k // 2), x1T, 8 + 4 * (k // 2))
                    work = sb_slot.get(8 * n + k, ())
                    for part, h in work:
                        if part == "r":
                            dve.wait_ge(sb_r, h + 1)
                            dve.tensor_tensor(sba[:, h % 2, :], ps[T1][:, 0:384], cap, ALU.min).then_inc(sb_em, 1)
                        if part == "o":
                            dve.wait_ge(sb_o, h + 1)
                            e = dve.tensor_copy(sbq[:, h, :], ps[T1][:, W:W + T])
                            e.then_inc(*((freed[T1], 1) if h == SBH - 1 else (sb_out, 1)))
                    make_lo(dve, c + k + AHEAD)
                    for part, h in work:
                        if part == "z":
                            l = sbl[:, h % 2, :]
                            dve.wait_ge(sb_ln, h + 1)
                            chain(dve.scalar_tensor_tensor(out=l, in0=ps[T1][:, 0:384], scalar=0.0, in1=sba[:, h % 2, :],
                                                           op0=ALU.max, op1=ALU.add))
                            diag = l.rearrange("p (a q) -> p a q", a=3)[:, 0:3:2, :]
                            dve.tensor_tensor(diag, diag, const[:, K_TRI:K_TRI + P].rearrange(
                                "p (o q) -> p o q", o=1).to_broadcast([P, 2, P]), ALU.mult).then_inc(sb_l, 1)
                if what in ("nq", "cmp", "slc", "win"):
                    p, _ = U.at[("acc", c)]
                    dve.wait_ge(multiplied, c + 8)
                    dve.wait_ge(angle_in, 16)
                    e = rotate(c, n, stage[n % 2], W if what == "nq" else T)
                    if what != "nq":
                        right = ps[p][:, :].rearrange("p (t w) -> p t w", t=TT)[:, :, T:W]
                        to = {"cmp": stage[n % 2][:, :, T:W], "slc": vsw[:, 0, :, :], "win": vsw[:, 1, :, :]}[what]
                        e = dve.tensor_copy(to, right)
                    e.then_inc(freed[p], 1)

            def operand(i):
                if i:
                    dve.wait_ge(fc_made, i)
                for hf in range(2):
                    for g in range(GROUPS):
                        src = kcT[:, 2 * i + g, :].rearrange("p (n s) -> p s n", s=CS)[:, :, hf:hf + NC]
                        po = posT[:, i, hf * CS:(hf + 1) * CS].rearrange("p (s o) -> p s o", o=1).to_broadcast([P, CS, NC])
                        did(dve.tensor_tensor(fs[:, hf * CS:(hf + 1) * CS, g * NC:(g + 1) * NC], src, po, ALU.add))
                see()
                chain(dve.tensor_copy(FC[i][:, :, 0:GC], fs[:, :, :]))
                dve.tensor_tensor(FC[i][:, :, LOROW:LOROW + GC], fs[:, :, :], FC[i][:, :, 0:GC].bitcast(F32),
                                  ALU.subtract).then_inc(fc_made, 1)

            for k in range(8):
                if k == 2:
                    w_over(dve, "gates")
                    g = gate[:, :, :]
                    chain(dve.tensor_scalar(g, g, 1.0, None, ALU.add))
                    did(dve.reciprocal(g, g))
                if k == 3:
                    dve.wait_ge(cmp_in, 32)
                    dve.wait_ge(cleared, 1)
                    operand(0)
                if k == 5:
                    operand(1)
                make_lo(dve, C_K1 + k + AHEAD)
            for k in range(16):
                make_lo(dve, C_CMP + k + AHEAD)

            def cmp_step(n):
                if n == 0:
                    w_ready(dve, "l1")
                    x, t = ug[:, 0, :, 0:GC], ug[:, 1, :, 0:GC]
                    dve.tensor_copy(x, ps[T1][:, 0:P].rearrange("p (a b) -> p a b", a=4)[:, :, 0:GC]).then_inc(freed[T1], 1)
                    w_over(dve, "l1")
                    chain(dve.tensor_tensor(t, x, x, ALU.mult))
                    chain(dve.tensor_scalar(t, t, 0.044715, 1.0, ALU.mult, ALU.add))
                    dve.tensor_tensor(t, t, x, ALU.mult).then_inc(gelu_x, 1)
                if n == 1:
                    w_ready(dve, "l2")
                    dve.tensor_copy(kcmp[:, :], ps[T1][:, 0:GC])
                    for g in range(GROUPS):
                        for r in range(REP):
                            e = dve.tensor_copy(vblk[32 * r:32 * r + NC, g, r * HD:(r + 1) * HD],
                                                ps[T1][32 * r:32 * r + NC, W + g * HD:W + (g + 1) * HD])
                    e.then_inc(freed[T1], 1)
                if n == 2:
                    w_ready(dve, "cs")
                    dve.tensor_tensor(pcs[:, :, :, :], ps[T1][:, 0:TT * NSH * NC].rearrange(
                        "p (t h c) -> p t h c", t=TT, h=NSH), cadd.to_broadcast([P, TT, NSH, NC]),
                        ALU.add).then_inc(freed[T1], 1)
                    w_over(dve, "cs")
                    chain(dve.tensor_reduce(cmx[:, :], pcs[:, :, :, :].rearrange("p t h c -> p (t h) c"), AX.X, ALU.max))
                    flat = pcs[:, :, :, :].rearrange("p t h c -> p (t h) c")
                    dve.tensor_tensor(flat, flat, cmx[:, :].rearrange("p (n o) -> p n o", o=1).to_broadcast(
                        [P, 16, NC]), ALU.subtract).then_inc(cs_max, 1)

            for s in range(32):
                b, k = divmod(s, 8)
                n, part = divmod(s, 4)
                g, br, tq = UNITS[n]
                keys = (tq + 1) * P
                if part == 0:
                    if n < 3:
                        cmp_step(n)
                    w_ready(dve, ("s", n))
                    if n:
                        w_ready(dve, ("p", n - 1))
                    p = ps[T0]
                    for r in range(REP):
                        e = dve.tensor_tensor_reduce(
                            out=prob[:, r, 0:keys], in0=p[:, r * T:r * T + keys], in1=cmask[:, T - keys:T],
                            scale=1.0, scalar=-3.0e38, op0=ALU.add, op1=ALU.max, accum_out=mx[:, r:r + 1])
                    e.then_inc(freed[T0], 1)
                    w_over(dve, ("s", n))
                    dve.tensor_scalar(nm[:, 0:REP], mx[:, 0:REP], -SCALE, None, ALU.mult).then_inc(ns_max, 1)
                make_lo(dve, C_FILL + s + AHEAD)
                if part == 0:
                    dve.wait_ge(ns_exp, n + 1)
                    chain(dve.reciprocal(cf[:, 0:REP], sm[:, 0:REP]))
                    gt = gate[:, tq, :].rearrange("p (h j) -> p h j", j=3)[:, g * REP:(g + 1) * REP, 1 + br]
                    chain(dve.tensor_tensor(cf[:, 0:REP], cf[:, 0:REP], gt, ALU.mult))
                    pr = prob[:, :, 0:keys]
                    dve.tensor_tensor(pr, pr, cf[:, 0:REP].rearrange("p (r o) -> p r o", o=1).to_broadcast(
                        [P, REP, keys]), ALU.mult).then_inc(ns_prob, 1)
                if s == 1:
                    dve.wait_ge(gelu_e, 1)
                    e = ug[:, 2, :, 0:GC]
                    chain(dve.tensor_scalar(e, e, 1.0, None, ALU.add))
                    chain(dve.reciprocal(e, e))
                    dve.tensor_tensor(ug[:, 3, :, 0:GC], ug[:, 0, :, 0:GC], e, ALU.mult).then_inc(gelu_made, 1)
                if s == 9:
                    dve.wait_ge(cs_exp, 1)
                    dve.wait_ge(cleared, 2)
                    flat = pcs[:, :, :, :].rearrange("p t h c -> p (t h) c")
                    chain(dve.tensor_tensor(pcs[:, :, :, :], pcs[:, :, :, :], cmul.to_broadcast([P, TT, NSH, NC]), ALU.mult))
                    chain(dve.tensor_reduce(csm[:, :], flat, AX.X, ALU.add))
                    chain(dve.tensor_scalar(csm[:, :], csm[:, :], 1e-30, None, ALU.max))
                    chain(dve.reciprocal(ccf[:, :], csm[:, :]))
                    cg = ccf[:, :].rearrange("p (t h) -> p t h", t=TT)
                    chain(dve.tensor_tensor(cg, cg, gate[:, :, :].rearrange("p t (h j) -> p t h j", j=3)[:, :, :, 0],
                                            ALU.mult))
                    dve.tensor_tensor(pcp[:, :, :, 0:NC].rearrange("p t h c -> p (t h) c"), flat,
                                      ccf[:, :].rearrange("p (n o) -> p n o", o=1).to_broadcast([P, 16, NC]),
                                      ALU.mult).then_inc(cs_made, 1)

            for k in range(8):
                if k in (0, 1):
                    dve.wait_ge(sq_made, k + 1)
                    dve.tensor_scalar(rv[:, 2 * k:2 * k + 2], ss[:, 2 * k:2 * k + 2], RMS_EPS, None,
                                      ALU.add).then_inc(rms_v, 1)
                    dve.wait_ge(rms_rs, k + 1)
                    sharpen(2 * k)
                    dve.wait_ge(mg_in, 16)
                    src = (sbq, nsq)[k]
                    for t in range(TT):
                        o = src[:, :, t * P:(t + 1) * P]
                        e = dve.scalar_tensor_tensor(
                            out=o, in0=o, scalar=rs[:, 2 * k + t:2 * k + t + 1],
                            in1=mg[:, k * 1024:(k + 1) * 1024].rearrange("p (h d) -> p h d", d=HD),
                            op0=ALU.mult, op1=ALU.mult)
                    e.then_inc(y_made, 1)
                if k in (3, 4, 5, 6):
                    group_lo(("y", k - 3), yT, 4 * (k - 3))
                make_lo(dve, C_V2 + k + AHEAD)

            for b in range(4):
                c = C_WOUT + 8 * b
                for k in range(8):
                    make_lo(dve, c + k + AHEAD)
                norm_add(c + 8, ("acc", c), b, 1.0)

            norm_finish()
            for k in range(8):
                if 1 <= k <= 4:
                    norm_piece(1, k - 1, gb2)
                if k >= 6:
                    group_lo(("x2", k - 6), x2T, 4 * (k - 6))
                make_lo(dve, C_V3 + k + AHEAD)

            for s in range(32):
                if s in (1, 3):
                    group_lo(("x2", 2 + s // 2), x2T, 8 + 4 * (s // 2))
                make_lo(dve, C_WQ + s + AHEAD)

            for h in range(MH):
                dve.wait_ge(m_z, h + 1)
                chain(dve.tensor_reduce(mx[:, 2 * h:2 * h + 2], ps[h // 2][:, h % 2 * W:(h % 2 + 1) * W].rearrange(
                    "p (t m) -> p t m", t=TT), AX.X, ALU.max))
                dve.tensor_scalar(nm[:, 2 * h:2 * h + 2], mx[:, 2 * h:2 * h + 2], -MSCALE, None,
                                  ALU.mult).then_inc(m_max, 1)
            for h in range(MH):
                dve.wait_ge(m_exp, h + 1)
                e = dve.reciprocal(cf[:, 2 * h:2 * h + 2], sm[:, 2 * h:2 * h + 2])
                if h % 2:
                    e.then_inc(freed[h // 2], 1)
                    w_over(dve, f"z{h // 2}")
                else:
                    chain(e)
                w_ready(dve, ("mp", h))
                dve.tensor_copy(mprobT[h % 2][:, :, :, :].rearrange("p t m q -> p (t m q)"),
                                ps[T0][:, 0:TT * TT * P]).then_inc(freed[T0], 1)
                w_ready(dve, ("mo", h))
                for t in range(TT):
                    e = dve.tensor_scalar(mo_tok[:, t, h * W:(h + 1) * W], ps[T1][:, t * W:(t + 1) * W],
                                          cf[:, 2 * h + t:2 * h + t + 1], None, ALU.mult)
                e.then_inc(freed[T1], 1)
                if h:
                    group_lo(("ot", h - 1), oT, 4 * h - 4)
            group_lo(("ot", MH - 1), oT, 4 * MH - 4)
            for b in range(4):
                c = C_WO + 8 * b
                for k in range(8):
                    make_lo(dve, c + k + AHEAD)
                norm_add(c + 8, ("acc", c), b, 1.0)

            norm_finish()
            for g in range(4):
                norm_piece(2, g, gb3)
                if g:
                    group_lo(("x3", g - 1), xT3, 4 * g - 4)
            group_lo(("x3", 3), xT3, 12)
            half_ffn(2, C_FFN2, lambda hf, kt: None)
            norm_add(C_END, ("d", 2, 2), 2, 0.5)
            norm_add(C_END, ("d", 2, 3), 3, 0.5)
            norm_finish()
            for g in range(4):
                norm_piece(3, g, gb4)

        @block.gpsimd
        def _(pool):
            w_ready(pool, "gates")
            for i in range(2):
                pool.memset(FC[i][:, :, GC:LOROW].bitcast(F32), 0.0)
            pool.memset(vblk[:, :, :], 0.0).then_inc(cleared, 1)
            pool.wait_ge(multiplied, C_FILL)
            pool.memset(pcp[:, :, :, :], 0.0).then_inc(cleared, 1)


_OUT = "out_0_dram"


def kernel(**inputs):
    import concourse.bacc as bacc
    from concourse.bass_utils import run_bass_kernel_spmd

    a = {k: np.asarray(v) for k, v in inputs.items()}
    const, angle = constants()
    arrays = {
        "x": a["x"][0], "mem": a["mem"][0], "const": const, "angle": angle,
        "ln": np.stack([np.stack([a[f"ln{i}_g"][0], a[f"ln{i}_b"][0]]) for i in (1, 2, 3, 4)]),
        "pos": np.stack([a["cmp_pos_k"][0].T, a["cmp_pos_v"][0].T], 1),
        "gate_w": a["w_in"][0][:, GATE_COL:].reshape(KD, P, NG).transpose(1, 0, 2),
        "cmp_w2": np.stack([a[f"cmp_w2_{i}"][0].reshape(2, P, HD) for i in "kv"]).transpose(2, 0, 1, 3),
        "mix_norm_g": a["mix_norm_g"],
    }
    for n in ("ffn1_gate", "ffn1_up", "ffn1_down", "w_in", "cmp_w1_k", "cmp_w1_v", "w_out", "mem_wq", "mem_wk",
              "mem_wv", "mem_wo", "ffn2_gate", "ffn2_up", "ffn2_down"):
        arrays[n] = a[n][0]
    arrays = {f"in_{k}_dram": np.ascontiguousarray(v) for k, v in arrays.items()}
    nc = bacc.Bacc("TRN2", target_bir_lowering=False, num_devices=1, dynamic_dma_scratch_size=1024)
    d = {k[3:-5]: nc.dram_tensor(k, v.shape, F32, kind="ExternalInput").ap() for k, v in arrays.items()}
    out = nc.dram_tensor(_OUT, (T, D), F32, kind="ExternalOutput").ap()
    hybrid_layer(nc, d, out)
    r = run_bass_kernel_spmd(nc, [arrays], core_ids=[0])
    return r.results[0][_OUT].reshape(1, T, D)
```

```python
from contextlib import ExitStack

import numpy as np

import concourse.bass as bass
import concourse.mybir as mybir
from concourse.alu_op_type import AluOpType as ALU

F32 = mybir.dt.float32
F32R = mybir.dt.float32r
I32 = mybir.dt.int32
ACT = mybir.ActivationFunctionType
AX = mybir.AxisListType

P = 128
T = 256
TT = T // P
D = 2048
KD = D // P
DFF = 5504
KF = DFF // P
W = 512
NFULL = DFF // W
WL = DFF - NFULL * W
HD = 128
HALF = HD // 2
SBH, NSH, GROUPS = 8, 8, 2
REP = NSH // GROUPS
CB, CS, CH = 32, 16, 256
NC = (T - CB) // CS + 1
GC = GROUPS * NC
LOROW = 64
MH = 4
MK = D // MH // P
SCALE = float(HD) ** -0.5
MSCALE = float(D // MH) ** -0.5
ALPHA = 2.0 ** 0.25
LN_EPS, RMS_EPS = 1e-5, 1e-6
NEG = -1e30

S_MEM = (6, 10, 14, 18)
AHEAD = 4
NRAW = 4
CHUNK = 1024
KD2 = (KF + 1) // 2
A, B, T0, T1 = range(4)
GELU = 0.7978845608028654
EPS1 = LN_EPS / ALPHA ** 2

C_FFN1 = 0
C_DOWN1 = C_FFN1 + 16 * (NFULL + 1)
C_K0 = C_DOWN1 + 4 * KD2
C_WIN = C_K0 + 8
NWIN = 11
C_K1 = C_WIN + 8 * NWIN
C_CMP = C_K1 + 8
C_FILL = C_CMP + 16
C_V2 = C_FILL + 32
C_WOUT = C_V2 + 8
C_V3 = C_WOUT + 32
C_WQ = C_V3 + 8
C_WO = C_WQ + 32
C_FFN2 = C_WO + 32
C_DOWN2 = C_FFN2 + 16 * (NFULL + 1)
C_END = C_DOWN2 + 4 * KD2

WIN = [("q", 0, 0), ("k", 0, 1024), ("v", 0, 2048), ("nq", 0, 3072), ("nq", 1, 3584), ("q", 1, 512),
       ("k", 1, 1536), ("v", 1, 2560), ("cmp", 0, 4096), ("slc", 0, 4608), ("win", 0, 5120)]
GATE_COL = 5632
NG = 24
SB_Z = (24, 32, 40, 48, 64, 70, 76, 82)
SB_R, SB_O = 3, 6
S_GATES = 8

UNITS = [(g, br, tt) for g in range(GROUPS) for br in range(2) for tt in range(TT)]

S_CMP = (1, 5, 9, 13)
S_KT = (10, 18)
S_Y = (3, 4, 6, 7)

K_ID, K_NEGU, K_NEG1, K_TRI, K_CAP, K_CM, K_SEL, K_CADD, K_CMUL, NCONST = (
    0, 128, 256, 384, 512, 896, 1152, 1184, 1216, 1248)


def constants():
    c = np.zeros((P, NCONST), np.float32)
    r, q = np.arange(P)[:, None], np.arange(P)[None, :]
    c[:, K_ID:K_ID + P] = r == q
    c[:, K_NEGU:K_NEGU + P] = np.where(r >= q, -1.0, 0.0)
    c[:, K_NEG1:K_NEG1 + P] = -1.0
    c[:, K_TRI:K_TRI + P] = q > r
    cap = np.where(q > r, 0.0, NEG)
    c[:, K_CAP:K_CAP + 3 * P] = np.concatenate([cap, np.zeros((P, P)), cap], 1)
    c[:, K_CM + P:K_CM + 2 * P] = np.where(q <= r, 0.0, NEG)
    for n in range(GC):
        c[n, K_SEL + n] = 1.0
        c[LOROW + n, K_SEL + n] = 1.0
    end = np.arange(NC) * CS + CB - 1
    for t in range(TT):
        ok = end[None, :] <= t * P + np.arange(P)[:, None]
        c[:, K_CADD + t * 16:K_CADD + t * 16 + NC] = np.where(ok, 0.0, NEG)
        c[:, K_CMUL + t * 16:K_CMUL + t * 16 + NC] = ok
    inv = np.float32(10000.0) ** (-np.arange(HALF, dtype=np.float32) / np.float32(HALF))
    pos = np.arange(T, dtype=np.float32).reshape(TT, P)
    ang = (pos[:, :, None] * inv).astype(np.float32).transpose(1, 0, 2)
    co, si = np.cos(ang), np.sin(ang)
    a = np.stack([np.concatenate([co, co], 2), np.concatenate([-si, si], 2)], 1)
    return c, np.ascontiguousarray(a, np.float32)


class Turns:

    def __init__(self):
        self.n = [0, 0, 0, 0]
        self.said = [0, 0, 0, 0]
        self.at = {}
        self.sends = {}
        self.split = {}

    def take(self, name, pair, split=False):
        self.at[name] = (pair, self.n[pair])
        self.n[pair] += 1
        if name not in ("sb", "z0", "z1") and name[0] not in ("acc", "d"):
            self.said[pair] += 1
            self.sends[name] = self.said[pair]
        if split:
            self.split[name] = len(self.split)


def turns():
    u = Turns()

    def acc(c, pair):
        u.take(("acc", c), pair)

    for g in range(4):
        u.take(("x", g), g, True)
    for f, c0 in ((1, C_FFN1), (2, C_FFN2)):
        if f == 2:
            for g in range(4):
                u.take(("x3", g), T0 + g % 2, True)
        acc(c0, A)
        for j in range(NFULL + 1):
            acc(c0 + 16 * j + 8, B)
            if j < NFULL:
                acc(c0 + 16 * j + 16, A)
            u.take(("h", f, j), T0, True)
        c1 = c0 + 16 * (NFULL + 1)
        for b in range(4):
            u.take(("d", f, b), (A, B)[b % 2])
            if f == 1 and b == 0:
                for g in range(4):
                    u.take(("mem", g), (T1, T0)[g % 2], True)
        if f == 2:
            break
        acc(C_K0, A)
        for g in range(4):
            u.take(("x1", g), T0 + g % 2, True)
        u.take(("kt", 0), T0)
        for n in range(NWIN):
            acc(C_WIN + 8 * n, (B, A)[n % 2])
            if n and WIN[n - 1][0] != "v":
                u.take(("w", n - 1), T0)
        u.take("gates", T1)
        u.take("gates_t", T1)
        u.take("sb", T1)
        acc(C_K1, A)
        u.take(("w", NWIN - 1), T0)
        acc(C_CMP, B)
        u.take(("kt", 1), T0)
        acc(C_CMP + 8, A)
        for s in range(32):
            n, k = divmod(s, 4)
            if s in S_CMP:
                u.take(("l1", "l2", "cs", "cp")[S_CMP.index(s)], T1)
            if s in S_KT:
                u.take(("kt", 2 + S_KT.index(s)), T0)
            if k == 0:
                u.take(("s", n), T0)
            if k == 3:
                u.take(("p", n), T1)
            if s % 16 == 5:
                u.take(("O", s // 16), B)
        for b in range(4):
            u.take(("acc", C_FILL + 8 * b), A)
        acc(C_V2, A)
        for g in range(4):
            u.take(("y", g), T0 + g % 2, True)
        for b in range(4):
            acc(C_WOUT + 8 * b, (B, A)[b % 2])
        acc(C_V3, B)
        for g in range(4):
            u.take(("x2", g), T0 + g % 2, True)
        for b in range(4):
            acc(C_WQ + 8 * b, (A, B)[b % 2])
            u.take(("qt", b), T0)
        u.take("z0", A)
        u.take("z1", B)
        for h in range(MH):
            u.take(("mp", h), T0)
            u.take(("mo", h), T1)
            if h:
                u.take(("ot", h - 1), A, True)
        u.take(("ot", MH - 1), B, True)
        for b in range(4):
            acc(C_WO + 8 * b, (A, B)[b % 2])
    return u


def w_raw(t, slot, cols, half=None):
    n = CHUNK * cols // W if cols < W and cols != CH else CHUNK
    if half is None:
        return t[:, slot, 0:2 * n].rearrange("p (k w) -> p k w", w=cols)
    return t[:, slot, half * n:(half + 1) * n]


def hybrid_layer(nc, d, out):
    U = turns()
    KB = 1024
    base = (nc.sbuf_base + 31) // 32 * 32
    o_raw, o_hi, o_lo, o_x = base, base + 32 * KB, base + 48 * KB, base + 64 * KB
    o_X, o_H, o_S = base + 80 * KB, base + 112 * KB, base + 200 * KB

    def sb(name, shape, dt, offset):
        return nc.alloc_sbuf_tensor_at(name, shape, dt, offset=offset)

    def two(name, kt, offset):
        return [sb(f"{name}_{n}", [P, kt, T], F32R, offset + i * kt * KB) for i, n in enumerate(("hi", "lo"))]

    raw = sb("raw", [P, NRAW, 2 * CHUNK], F32, o_raw)
    whi = sb("whi", [P, AHEAD, CHUNK], F32R, o_hi)
    wlo = sb("wlo", [P, AHEAD, CHUNK], F32R, o_lo)
    x_tok = sb("x_tok", [P, TT, D], F32, o_x)
    xT0 = two("xT0", KD, o_X)
    memT = two("memT", KD, o_X)
    oT = two("oT", KD, o_X)
    xT3 = two("xT3", KD, o_X)
    gb4 = sb("gb4", [P, 2, D], F32, o_X)
    hT = {1: two("hT1", KF, o_H), 2: two("hT2", KF, o_H)}
    gb1 = sb("gb1", [P, 2, D], F32, o_H)
    V = sb("V", [P, TT, D], F32, o_H)
    sba = sb("sba", [P, 2, 384], F32, o_H)
    sbl = sb("sbl", [P, 2, 384], F32, o_H + 3 * KB)
    rot = sb("rot", [P, W], F32, o_H + 6 * KB)
    angle = sb("angle", [P, 2, TT, P], F32, o_H + 8 * KB)
    kcT = sb("kcT", [P, 4, T], F32, o_H + 12 * KB)
    kstage = sb("kstage", [P, TT, W], F32, o_H)
    fs = sb("fs", [P, CB, GC], F32, o_H + 4 * KB)
    ug = sb("ug", [P, 4, 4, 32], F32, o_H + 4 * KB)
    w2 = sb("w2", [P, 2, 2, HD], F32, o_H + 10 * KB)
    x1T = two("x1T", KD, o_H + 16 * KB)
    FC = [sb(f"FC{i}", [P, CB, LOROW + GC], F32R, o_H + (16 + i * 12) * KB) for i in range(2)]
    pcs = sb("pcs", [P, TT, NSH, NC], F32, o_H + 16 * KB)
    pcp = sb("pcp", [P, TT, NSH, 32], F32, o_H + 18 * KB)
    pcT = sb("pcT", [P, TT, GROUPS, P], F32, o_H + 20 * KB)
    scrap = sb("scrap", [P, REP, T], F32, o_H + 32 * KB)
    hc = sb("hc", [P, 2, CH], F32, o_H + 40 * KB)
    vblk = sb("vblk", [P, GROUPS, W], F32, o_H + 42 * KB)
    posT = sb("posT", [P, 2, CB], F32, o_H + 46 * KB)
    kcmp = sb("kcmp", [P, GC], F32, o_H + 46 * KB + 512)
    yT = two("yT", KD, o_H + 16 * KB)
    x2T = two("x2T", KD, o_H + 16 * KB)
    mo_tok = sb("mo_tok", [P, TT, D], F32, o_H + 16 * KB)
    gb3 = sb("gb3", [P, 2, D], F32, o_H + 32 * KB)
    KT = sb("KT", [P, KD, T], F32, o_H + 48 * KB)
    sbq = sb("sbq", [P, SBH, T], F32, o_H + 64 * KB)
    nsq = sb("nsq", [P, NSH, T], F32, o_H + 72 * KB)
    gb2 = sb("gb2", [P, 2, D], F32, o_H + 64 * KB)
    qT = sb("qT", [P, KD, T], F32, o_H + 64 * KB)
    sbk = sb("sbk", [P, 4, T], F32, o_H + 80 * KB)
    sbv = sb("sbv", [P, TT, W], F32, o_H + 84 * KB)
    mg = sb("mg", [P, D], F32, o_H + 80 * KB)
    at = [o_S]

    def small(name, shape):
        t = sb(name, shape, F32, at[0])
        at[0] += (4 * int(np.prod(shape[1:])) + 31) // 32 * 32
        return t

    const = small("const", [P, NCONST])
    o_stage = at[0]
    stage = [small("stage0", [P, TT, W]), small("stage1", [P, TT, W])]
    sil = sb("sil", [P, TT, W], F32, o_stage)
    hbuf = sb("hbuf", [P, TT, W], F32, o_stage + 4 * KB)
    prob = sb("prob", [P, REP, T], F32, o_stage)
    probT = sb("probT", [P, REP, TT, P], F32, o_stage + 4 * KB)
    mprob = [sb(f"mprob{i}", [P, TT, T], F32, o_stage + 2 * i * KB) for i in range(2)]
    mprobT = [sb(f"mprobT{i}", [P, TT, TT, P], F32, o_stage + (4 + 2 * i) * KB) for i in range(2)]
    kslT = small("kslT", [P, GROUPS, T])
    kwnT = small("kwnT", [P, GROUPS, T])
    wg = sb("wg", [P, KD * NG], F32, at[0] - 2 * KB)
    gate_t = sb("gate_t", [P, T], F32, at[0] - 4 * KB)
    wg_parts = [sb(f"wg_{n}", [P, KD * NG + P - NG], F32R, at[0] + 2 * KB * i) for i, n in enumerate(("hi", "lo"))]
    vsw = small("vsw", [P, 2, TT, T])
    st = small("st", [P, TT, 4, 6])
    mv = small("mv", [P, TT, 2])
    rs = small("rs", [P, 4])
    rv = small("rv", [P, 4])
    rw = small("rw", [P, 4])
    nb = small("nb", [P, TT])
    ss = small("ss", [P, 4])
    gate = small("gate", [P, TT, NG])
    mx = small("mx", [P, 8])
    nm = small("nm", [P, 8])
    sm = small("sm", [P, 8])
    cf = small("cf", [P, 8])
    cmx = small("cmx", [P, 16])
    csm = small("csm", [P, 16])
    ccf = small("ccf", [P, 16])
    assert at[0] <= 229368

    ident = const[:, K_ID:K_ID + P]
    negu = const[:, K_NEGU:K_NEGU + P]
    neg1 = const[:, K_NEG1:K_NEG1 + P]
    tri = const[:, K_TRI:K_TRI + P]
    cap = const[:, K_CAP:K_CAP + 3 * P]
    cmask = const[:, K_CM:K_CM + 2 * P]
    sel = const[:, K_SEL:K_SEL + GC]
    cadd = const[:, K_CADD:K_CADD + 32].rearrange("p (t o c) -> p t o c", t=TT, o=1)[:, :, :, 0:NC]
    cmul = const[:, K_CMUL:K_CMUL + 32].rearrange("p (t o c) -> p t o c", t=TT, o=1)[:, :, :, 0:NC]

    with ExitStack() as ctx:
        ps = [ctx.enter_context(nc.psum_tensor(f"ps_{n}", [P, 2 * W], F32)) for n in ("A", "B", "T0", "T1")]

        def sem(name):
            return ctx.enter_context(nc.semaphore(name))

        landed = [sem(f"landed{i}") for i in range(NRAW)]
        hi_made, lo_made, multiplied = sem("hi_made"), sem("lo_made"), sem("multiplied")
        ready = [sem(f"ready_{n}") for n in ("A", "B", "T0", "T1")]
        freed = [sem(f"freed_{n}") for n in ("A", "B", "T0", "T1")]
        split_hi = sem("split_hi")
        x_in = [sem(f"x_in{g}") for g in range(4)]
        mem_in = [sem(f"mem_in{g}") for g in range(4)]
        const_in, angle_in, gate_in, cmp_in, mg_in = (
            sem("const_in"), sem("angle_in"), sem("gate_in"), sem("cmp_in"), sem("mg_in"))
        gate_hi, gate_lo = sem("gate_hi"), sem("gate_lo")
        gb_in = [sem(f"gb_in{i}") for i in range(4)]
        norm_rs, norm_hat, norm_gain, normed0, normed1 = (
            sem("norm_rs"), sem("norm_hat"), sem("norm_gain"), sem("normed0"), sem("normed1"))
        sb_z, sb_ln, sb_l, sb_r, sb_em, sb_w, sb_o, sb_out = (
            sem("sb_z"), sem("sb_ln"), sem("sb_l"), sem("sb_r"), sem("sb_em"), sem("sb_w"),
            sem("sb_o"), sem("sb_out"))
        cleared, fc_made, gelu_x, gelu_e, gelu_made = (
            sem("cleared"), sem("fc_made"), sem("gelu_x"), sem("gelu_e"), sem("gelu_made"))
        cs_max, cs_exp, cs_made = sem("cs_max"), sem("cs_exp"), sem("cs_made")
        ns_max, ns_exp, ns_prob = sem("ns_max"), sem("ns_exp"), sem("ns_prob")
        sq_made, y_made = sem("sq_made"), sem("y_made")
        m_z, m_max, m_exp = sem("m_z"), sem("m_max"), sem("m_exp")
        dve_step, act_step = sem("dve_step"), sem("act_step")
        stored = sem("stored")
        block = ctx.enter_context(nc.Block())

        def w_ready(e, name):
            e.wait_ge(ready[U.at[name][0]], U.sends[name])

        def w_free(e, name, more=0):
            p, n = U.at[name]
            if n:
                e.wait_ge(freed[p], n + more)

        def w_normed(e, n):
            e.wait_ge(normed0, n)
            e.wait_ge(normed1, n)

        def w_over(e, name):
            p, n = U.at[name]
            e.wait_ge(freed[p], n + 1)

        @block.sync
        def _(sp):
            def piece(n, slot, src, cols, wait=True):
                if wait:
                    sp.wait_ge(lo_made, 2 * (n - NRAW) + 2)
                k = src.shape[1]
                sp.dma_start(w_raw(raw, slot, cols)[:, 0:k, :], src).then_inc(landed[slot], 16)

            def cols_of(w, k0, k1, c0, n):
                return w.rearrange("(k p) n -> p k n", p=P)[:, k0:k1, bass.ds(c0, n)]

            def blk(w, c, c0, n=W):
                for k in range(4):
                    piece(c // 2 + k if isinstance(c, int) else c.piece + k, k,
                          cols_of(w, 4 * k, 4 * k + 4, c0, n), n)

            class Chunk:
                def __init__(self, piece):
                    self.piece = piece

            def half_ffn(f, c0):
                g, u, dn = d[f"ffn{f}_gate"], d[f"ffn{f}_up"], d[f"ffn{f}_down"]
                if f == 2:
                    blk(g, c0, 0)
                else:
                    for k in range(4):
                        sp.dma_start(x_tok[:, :, k * W:(k + 1) * W], d["x"].rearrange("(t p) n -> p t n", p=P)[
                            :, :, k * W:(k + 1) * W]).then_inc(x_in[k], 16)
                        piece(k, k, cols_of(g, 4 * k, 4 * k + 4, 0, W), W, False)
                with sp.Fori(0, NFULL - 1) as i:
                    blk(u, Chunk(i * 8 + (c0 + 8) // 2), i * W)
                    blk(g, Chunk(i * 8 + (c0 + 16) // 2), i * W + W)
                blk(u, c0 + 16 * NFULL - 8, (NFULL - 1) * W)
                blk(g, c0 + 16 * NFULL, NFULL * W, WL)
                blk(u, c0 + 16 * NFULL + 8, NFULL * W, WL)
                for b in range(4):
                    for m in range(KD2 // 2):
                        n = (c0 + 16 * (NFULL + 1) + b * KD2) // 2 + m
                        piece(n, n % NRAW, cols_of(dn, 4 * m, min(4 * m + 4, KF), b * W, W), W)

            half_ffn(1, C_FFN1)
            blk(d["mem_wk"], C_K0, 0)
            for n, (_, _, c0) in enumerate(WIN):
                blk(d["w_in"], C_WIN + 8 * n, c0)
            blk(d["mem_wk"], C_K1, W)
            for i, w in enumerate(("cmp_w1_k", "cmp_w1_v")):
                for k in range(4):
                    piece((C_CMP + 8 * i) // 2 + k, k, cols_of(d[w], 8 * k, 8 * k + 8, 0, CH), CH)
            for b, (w, c) in enumerate((("mem_wk", 2), ("mem_wk", 3), ("mem_wv", 0), ("mem_wv", 1), ("mem_wv", 2))):
                blk(d[w], C_FILL + 8 * b, c * W)
            with sp.Fori(0, 4) as i:
                blk(d["w_out"], Chunk(i * 4 + C_WOUT // 2), i * W)
            blk(d["mem_wv"], C_V3, 3 * W)
            with sp.Fori(0, 4) as i:
                blk(d["mem_wq"], Chunk(i * 4 + C_WQ // 2), i * W)
            with sp.Fori(0, 4) as i:
                blk(d["mem_wo"], Chunk(i * 4 + C_WO // 2), i * W)
            half_ffn(2, C_FFN2)
            for g in range(4):
                w_normed(sp, 13 + g)
                sp.dma_start(out.rearrange("(t p) n -> p t n", p=P)[:, :, g * W:(g + 1) * W],
                             x_tok[:, :, g * W:(g + 1) * W]).then_inc(stored, 16)
            sp.wait_ge(stored, 64)

        @block.tensor
        def _(pe):
            def chunk(c, slot, lhs, kts, n, pair, first, last):
                pe.wait_ge(lo_made, c + 1)
                for q, kt in enumerate(kts):
                    for t in range(TT):
                        for a, w in ((0, whi), (0, wlo), (1, whi)):
                            mm = pe.matmul(ps[pair][:, t * W:t * W + n], lhs[a][:, kt, t * P:(t + 1) * P],
                                           w[:, slot, q * n:(q + 1) * n],
                                           start=first and q == 0 and a == 0 and w is whi,
                                           stop=last and q == len(kts) - 1 and a == 1, skip_group_check=True)
                mm.then_inc(multiplied, 1)

            def step(c, k, lhs, pair, n=W):
                chunk(c + k, k % AHEAD, lhs, (2 * k, 2 * k + 1), n, pair, k == 0, k == 7)

            def turn_group(name, src, n=4, more=None):
                p, _ = U.at[name]
                w_free(pe, name, 0) if more is None else pe.wait_ge(freed[p], more)
                for i in range(n):
                    for t in range(TT):
                        mm = pe.transpose(ps[p][:, i * T + t * P:i * T + (t + 1) * P], src(t, i), ident)
                mm.then_inc(ready[p], 1)

            def half_ffn(f, c0, xT, group):
                name = ("x", "x3")[f - 1]

                def h_group(j, n=4, i=None):
                    n_up = U.at[("acc", c0 + 16 * j + 8)][1] + 1
                    pe.wait_ge(freed[B], n_up if i is None else i + n_up)
                    turn_group(("h", f, j), lambda t, k: hbuf[:, t, k * P:(k + 1) * P], n,
                               None if i is None else i + U.at[("h", f, 0)][1])

                group(0)
                w_free(pe, ("acc", c0))
                for k in range(8):
                    if k % 2 == 0:
                        w_over(pe, (name, k // 2))
                    elif k < 7:
                        group(k // 2 + 1)
                    step(c0, k, xT, A)
                with pe.Fori(0, NFULL - 1) as i:
                    pe.wait_ge(freed[B], i + U.at[("acc", c0 + 8)][1])
                    for k in range(8):
                        step(i * 16 + (c0 + 8), k, xT, B)
                    pe.wait_ge(freed[A], i + U.at[("acc", c0 + 16)][1])
                    for k in range(8):
                        if k == 3:
                            h_group(0, i=i)
                        step(i * 16 + (c0 + 16), k, xT, A)
                c = c0 + 16 * NFULL - 8
                w_free(pe, ("acc", c))
                for k in range(8):
                    step(c, k, xT, B)
                w_free(pe, ("acc", c + 8))
                for k in range(8):
                    if k == 3:
                        h_group(NFULL - 1)
                    step(c + 8, k, xT, A, WL)
                w_free(pe, ("acc", c + 16))
                for k in range(8):
                    step(c + 16, k, xT, B, WL)
                for b in range(4):
                    w_free(pe, ("d", f, b))
                    for m in range(KD2):
                        if b == 0 and m == 2:
                            h_group(NFULL, WL // P)
                        if b == 0 and m == 2 * NFULL - 2:
                            w_over(pe, ("h", f, NFULL - 1))
                        if b == 0 and m == 2 * NFULL:
                            w_over(pe, ("h", f, NFULL))
                        if b == 0 and f == 1 and m in S_MEM:
                            g = S_MEM.index(m)
                            pe.wait_ge(mem_in[g], 16)
                            turn_group(("mem", g), lambda t, i: stage[g % 2][:, t, i * P:(i + 1) * P])
                        c = c0 + 16 * (NFULL + 1) + b * KD2 + m
                        chunk(c, c % AHEAD, hT[f], range(2 * m, min(2 * m + 2, KF)), W, (A, B)[b % 2], m == 0,
                              m == KD2 - 1)

            def norm_group(i, g):
                w_normed(pe, 4 * i + g + 1)
                turn_group((f"x{i + 1}", g), lambda t, k: x_tok[:, t, g * W + k * P:g * W + (k + 1) * P])

            def kt_group(b):
                src = stage[1] if b == 0 else kstage
                w_over(pe, ("acc", (C_K0, C_K1, C_FILL, C_FILL + 8)[b]))
                turn_group(("kt", b), lambda t, i: src[:, t, i * P:(i + 1) * P])

            pe.wait_ge(const_in, 16)

            def x_group(g):
                pe.wait_ge(x_in[g], 16)
                turn_group(("x", g), lambda t, i: x_tok[:, t, g * W + i * P:g * W + (i + 1) * P])

            half_ffn(1, C_FFN1, xT0, x_group)

            w_free(pe, ("acc", C_K0))
            w_over(pe, ("mem", 2))
            w_over(pe, ("mem", 3))
            for k in range(8):
                if k >= 5:
                    norm_group(0, k - 5)
                step(C_K0, k, memT, A)

            def sb_scores(h):
                hh = h % 4
                if h == 0:
                    w_free(pe, "sb")
                else:
                    pe.wait_ge(sb_em, h)
                z = ps[T1][:, 0:384]
                pe.matmul(z[:, 0:T], sbk[:, hh, 0:P], sbq[:, h, :], start=True, stop=True, skip_group_check=True)
                pe.matmul(z[:, T:384], sbk[:, hh, P:T], sbq[:, h, P:T], start=False, stop=True,
                          skip_group_check=True).then_inc(sb_z, 1)

            def sb_rest(h):
                pe.wait_ge(sb_l, h + 1)
                z, l = ps[T1][:, 0:384], sbl[:, h % 2, :]
                pe.matmul(z, negu, l, start=False, stop=True, skip_group_check=True)
                pe.matmul(z[:, P:T], neg1, l[:, T:384], start=False, stop=True,
                          skip_group_check=True).then_inc(sb_r, 1)

            def sb_values(h):
                pe.wait_ge(sb_w, h + 1)
                if h:
                    pe.wait_ge(sb_out, h)
                o, w, v = ps[T1][:, W:W + T], sba[:, h % 2, :], sbv[:, :, h % 4 * HD:(h % 4 + 1) * HD]
                pe.matmul(o[:, 0:P], w[:, 0:P], v[:, 0, :], start=True, stop=True, skip_group_check=True)
                pe.matmul(o[:, P:T], w[:, P:T], v[:, 0, :], start=False, stop=False, skip_group_check=True)
                pe.matmul(o[:, P:T], w[:, T:384], v[:, 1, :], start=False, stop=True,
                          skip_group_check=True).then_inc(sb_o, 1)

            def w_group(n):
                w_over(pe, ("acc", C_WIN + 8 * n))
                turn_group(("w", n), lambda t, i: stage[n % 2][:, t, i * P:(i + 1) * P],
                           2 if WIN[n][0] in ("slc", "win") else 4)

            def gates():
                w_free(pe, "gates")
                pe.wait_ge(gate_lo, 1)
                pe.wait_ge(cleared, 1)
                for kt in range(KD):
                    cols = slice(kt * NG, kt * NG + P)
                    for a, x in ((0, 0), (0, 1), (1, 0)):
                        mm = pe.matmul(ps[T1][:, 0:T], wg_parts[a][:, cols], x1T[x][:, kt, :],
                                       start=kt == 0 and a == x, stop=kt == KD - 1 and a == 1, skip_group_check=True)
                mm.then_inc(ready[T1], 1)

            def gates_turn():
                w_over(pe, "gates")
                for t in range(TT):
                    mm = pe.transpose(ps[T1][:, t * NG:(t + 1) * NG], gate_t[0:NG, t * P:(t + 1) * P],
                                      ident[0:NG, 0:NG])
                mm.then_inc(ready[T1], 1)

            def stick_breaking(s):
                for h, z in enumerate(SB_Z):
                    if s == z:
                        if h in (0, 4):
                            w_over(pe, ("w", 1 if h == 0 else 6))
                        sb_scores(h)
                for h, z in enumerate(SB_Z):
                    if s == z + SB_R:
                        sb_rest(h)
                    if s == z + SB_O:
                        if h in (0, 4):
                            w_over(pe, ("acc", C_WIN + 8 * (2 if h == 0 else 7)))
                        sb_values(h)

            for n in range(NWIN):
                c = C_WIN + 8 * n
                w_free(pe, ("acc", c))
                for k in range(8):
                    if n == 0:
                        if k == 1:
                            norm_group(0, 3)
                        if k == 5:
                            kt_group(0)
                        if k % 2 == 0:
                            w_over(pe, ("x1", k // 2))
                    elif k == 3 and WIN[n - 1][0] != "v":
                        w_group(n - 1)
                    if 8 * n + k == S_GATES:
                        gates()
                    if 8 * n + k == S_GATES + 2:
                        gates_turn()
                    stick_breaking(8 * n + k)
                    step(c, k, x1T, (B, A)[n % 2])

            w_free(pe, ("acc", C_K1))
            for k in range(8):
                stick_breaking(8 * NWIN + k)
                if k == 3:
                    w_group(NWIN - 1)
                step(C_K1, k, memT, A)

            for i in range(2):
                c, pair = C_CMP + 8 * i, (B, A)[i]
                w_free(pe, ("acc", c))
                pe.wait_ge(fc_made, i + 1)
                for k in range(8):
                    if i == 0 and k == 3:
                        kt_group(1)
                    pe.wait_ge(lo_made, c + k + 1)
                    for q in range(4):
                        for w in (whi, wlo):
                            mm = pe.matmul(ps[pair][0:LOROW + GC, 0:CH], FC[i][:, 4 * k + q, :],
                                           w[:, k % AHEAD, q * CH:(q + 1) * CH],
                                           start=k == 0 and q == 0 and w is whi, stop=k == 7 and q == 3 and w is wlo,
                                           skip_group_check=True)
                    mm.then_inc(multiplied, 1)

            def cmp_step(n):
                if n == 0:
                    w_free(pe, "l1")
                    for i in range(2):
                        w_over(pe, ("acc", C_CMP + 8 * i))
                    for i in range(2):
                        for m in range(2):
                            mm = pe.matmul(ps[T1][:, (2 * i + m) * 32:(2 * i + m) * 32 + GC],
                                           hc[0:LOROW + GC, i, m * P:(m + 1) * P], sel[0:LOROW + GC, :],
                                           start=True, stop=True, skip_group_check=True)
                    mm.then_inc(ready[T1], 1)
                if n == 1:
                    w_free(pe, "l2")
                    pe.wait_ge(gelu_made, 1)
                    for m in range(2):
                        pe.matmul(ps[T1][:, 0:GC], w2[:, 0, m, :], ug[:, 3, m, 0:GC],
                                  start=m == 0, stop=m == 1, skip_group_check=True)
                    for g in range(GROUPS):
                        for r in range(REP):
                            for m in range(2):
                                mm = pe.matmul(ps[T1][32 * r:32 * r + NC, W + g * HD:W + (g + 1) * HD],
                                               ug[:, 3, 2 + m, g * NC:(g + 1) * NC], w2[:, 1, m, :],
                                               start=m == 0, stop=m == 1, skip_group_check=True)
                    mm.then_inc(ready[T1], 1)
                if n == 2:
                    w_free(pe, "cs")
                    w_over(pe, "l2")
                    for t in range(TT):
                        for h in range(NSH):
                            g = h // REP
                            o = (t * NSH + h) * NC
                            mm = pe.matmul(ps[T1][:, o:o + NC], nsq[:, h, t * P:(t + 1) * P],
                                           kcmp[:, g * NC:(g + 1) * NC], start=True, stop=True, skip_group_check=True)
                    mm.then_inc(ready[T1], 1)
                if n == 3:
                    w_free(pe, "cp")
                    pe.wait_ge(cs_made, 1)
                    for t in range(TT):
                        for g in range(GROUPS):
                            o = (t * GROUPS + g) * P
                            mm = pe.transpose(ps[T1][:, o:o + P],
                                              pcp[:, t, g * REP:(g + 1) * REP, :].rearrange("p a b -> p (a b)"), ident)
                    mm.then_inc(ready[T1], 1)

            def unit_values(s):
                n, part = divmod(s - 5, 4)
                if part or not 0 <= n < len(UNITS):
                    return
                g, br, tq = UNITS[n]
                w_over(pe, ("p", n))
                if n % 4 == 0:
                    w_free(pe, ("O", g))
                for r in range(REP):
                    for kk in range(tq + 1):
                        pe.matmul(ps[B][:, tq * W + r * HD:tq * W + (r + 1) * HD], probT[:, r, kk, :],
                                  vsw[:, br, kk, g * HD:(g + 1) * HD], start=br == 0 and r == 0 and kk == 0,
                                  stop=False, skip_group_check=True)
                if n % 4 == 3:
                    w_over(pe, "cp")
                    for t in range(TT):
                        mm = pe.matmul(ps[B][:, t * W:(t + 1) * W], pcT[:, t, g, :], vblk[:, g, :],
                                       start=False, stop=True, skip_group_check=True)
                    mm.then_inc(ready[B], 1)

            for s in range(32):
                b, k = divmod(s, 8)
                n, part = divmod(s, 4)
                g, br, tq = UNITS[n]
                keys = (tq + 1) * P
                unit_values(s)
                if s in S_CMP:
                    cmp_step(S_CMP.index(s))
                if s in S_KT:
                    kt_group(2 + S_KT.index(s))
                if part == 0:
                    w_free(pe, ("s", n))
                    if n == 0:
                        w_over(pe, ("w", NWIN - 1))
                    kT = (kslT, kwnT)[br]
                    for r in range(REP):
                        mm = pe.matmul(ps[T0][:, r * T:r * T + keys], nsq[:, g * REP + r, tq * P:(tq + 1) * P],
                                       kT[:, g, 0:keys], start=True, stop=True, skip_group_check=True)
                    mm.then_inc(ready[T0], 1)
                if part == 3:
                    w_free(pe, ("p", n))
                    pe.wait_ge(ns_prob, n + 1)
                    for r in range(REP):
                        for kk in range(tq + 1):
                            o = (r * TT + kk) * P
                            mm = pe.transpose(ps[T1][:, o:o + P], prob[:, r, kk * P:(kk + 1) * P], ident)
                    mm.then_inc(ready[T1], 1)
                if k == 0:
                    w_free(pe, ("acc", C_FILL + 8 * b))
                step(C_FILL + 8 * b, k, memT, A)

            w_free(pe, ("acc", C_V2))
            for k in range(8):
                unit_values(32 + k)
                if k in S_Y:
                    g = S_Y.index(k)
                    pe.wait_ge(y_made, 1 + g // 2)
                    src = (sbq, nsq)[g // 2]
                    turn_group(("y", g), lambda t, i: src[:, 4 * (g % 2) + i, t * P:(t + 1) * P])
                step(C_V2, k, memT, A)

            for b in range(4):
                c, pair = C_WOUT + 8 * b, (B, A)[b % 2]
                w_free(pe, ("acc", c))
                for k in range(8):
                    if b == 0 and k % 2 == 0:
                        w_over(pe, ("y", k // 2))
                    step(c, k, yT, pair)

            w_free(pe, ("acc", C_V3))
            for k in range(8):
                if k >= 5:
                    norm_group(1, k - 5)
                step(C_V3, k, memT, B)

            for b in range(4):
                c, pair = C_WQ + 8 * b, (A, B)[b % 2]
                w_free(pe, ("acc", c))
                for k in range(8):
                    if b == 0:
                        if k == 1:
                            norm_group(1, 3)
                        if k % 2 == 0:
                            w_over(pe, ("x2", k // 2))
                    elif k == 3:
                        w_over(pe, ("acc", C_WQ + 8 * b - 8))
                        turn_group(("qt", b - 1), lambda t, i: stage[(b - 1) % 2][:, t, i * P:(i + 1) * P])
                    step(c, k, x2T, pair)
            w_over(pe, ("acc", C_WQ + 24))
            turn_group(("qt", 3), lambda t, i: stage[1][:, t, i * P:(i + 1) * P])

            for h in range(MH):
                if h % 2 == 0:
                    w_free(pe, f"z{h // 2}")
                w_over(pe, ("qt", h))
                for t in range(TT):
                    for k in range(MK):
                        mm = pe.matmul(ps[h // 2][:, h % 2 * W + t * T:h % 2 * W + (t + 1) * T],
                                       qT[:, MK * h + k, t * P:(t + 1) * P], KT[:, MK * h + k, :],
                                       start=k == 0, stop=k == MK - 1, skip_group_check=True)
                mm.then_inc(m_z, 1)

            def o_group(h):
                w_over(pe, ("mo", h))
                turn_group(("ot", h), lambda t, i: mo_tok[:, t, h * W + i * P:h * W + (i + 1) * P])

            for h in range(MH):
                w_free(pe, ("mp", h))
                pe.wait_ge(m_exp, h + 1)
                for t in range(TT):
                    for m in range(TT):
                        mm = pe.transpose(ps[T0][:, (t * TT + m) * P:(t * TT + m + 1) * P],
                                          mprob[h % 2][:, t, m * P:(m + 1) * P], ident)
                mm.then_inc(ready[T0], 1)
                w_over(pe, ("mp", h))
                w_free(pe, ("mo", h))
                for t in range(TT):
                    for m in range(TT):
                        mm = pe.matmul(ps[T1][:, t * W:(t + 1) * W], mprobT[h % 2][:, t, m, :],
                                       V[:, m, h * W:(h + 1) * W], start=m == 0, stop=m == TT - 1,
                                       skip_group_check=True)
                mm.then_inc(ready[T1], 1)
                if h:
                    o_group(h - 1)
            o_group(MH - 1)

            for b in range(4):
                c, pair = C_WO + 8 * b, (A, B)[b % 2]
                w_free(pe, ("acc", c))
                for k in range(8):
                    if b == 0 and k % 2 == 0:
                        w_over(pe, ("ot", k // 2))
                    step(c, k, oT, pair)

            half_ffn(2, C_FFN2, xT3, lambda g: norm_group(2, g))

        def size(c):
            for c0 in (C_FFN1, C_FFN2):
                if c0 + 16 * NFULL <= c < c0 + 16 * (NFULL + 1):
                    return CHUNK * WL // W
                m = c - c0 - 16 * (NFULL + 1)
                if 0 <= m < 4 * KD2 and m % KD2 == KD2 - 1:
                    return CHUNK // 2
            return CHUNK

        def plus(i, step, x):
            return x if i is None else i * step + x

        def make_hi(act, c, i=None):
            if c >= C_END:
                return
            slot, n = c // 2 % NRAW, size(c)
            o = c % 2 * (CHUNK if n == CHUNK // 2 else n)
            if c % 2 == 0:
                act.wait_ge(landed[slot], plus(i, 32, 16 * (c // 8 + 1)))
            if c >= AHEAD:
                act.wait_ge(multiplied, plus(i, 16, c - AHEAD + 1))
            act.activation(whi[:, c % AHEAD, 0:n], raw[:, slot, o:o + n], ACT.Copy).then_inc(
                hi_made, 1)

        def make_lo(dve, c, i=None):
            if c >= C_END:
                return
            slot, n = c // 2 % NRAW, size(c)
            o = c % 2 * (CHUNK if n == CHUNK // 2 else n)
            dve.wait_ge(hi_made, plus(i, 16, c + 1))
            dve.tensor_tensor(wlo[:, c % AHEAD, 0:n], raw[:, slot, o:o + n],
                              whi[:, c % AHEAD, 0:n].bitcast(F32), ALU.subtract).then_inc(
                lo_made, 1)

        def split_wait(e, name, i=None):
            e.wait_ge(split_hi, plus(i, 1, U.split[name] + 1))

        def sb_work(s):
            return ([("z", h) for h, z in enumerate(SB_Z) if s == z]
                    + [("r", h) for h, z in enumerate(SB_Z) if s == z + SB_R]
                    + [("o", h) for h, z in enumerate(SB_Z) if s == z + SB_O])

        @block.scalar
        def _(act):
            steps = [0]

            def chain(ins):
                steps[0] += 1
                ins.then_inc(act_step, 1)
                act.wait_ge(act_step, steps[0])

            def group_hi(name, dst, kt, n=4, i=None):
                p, _ = U.at[name]
                act.wait_ge(ready[p], plus(i, 1, U.sends[name]))
                to = dst[0][:, kt:kt + n, :] if i is None else dst[0][:, bass.ds(i * 4, n), :]
                act.activation(to, ps[p][:, 0:n * T].rearrange("p (k t) -> p k t", t=T), ACT.Copy).then_inc(split_hi, 1)

            def group_copy(name, dst):
                w_ready(act, name)
                p, _ = U.at[name]
                n = dst.shape[1]
                act.activation(dst, ps[p][:, 0:n * T].rearrange("p (k t) -> p k t", t=T), ACT.Copy).then_inc(freed[p], 1)

            def block_copy(c, dst, scale=1.0):
                act.wait_ge(multiplied, c + 8)
                p, _ = U.at[("acc", c)]
                act.activation(dst, ps[p][:, :].rearrange("p (t w) -> p t w", t=TT), ACT.Copy,
                               scale=scale).then_inc(freed[p], 1)

            def norm_piece(i, g):
                if g == 0:
                    act.wait_ge(norm_rs, i + 1)
                for t in range(TT):
                    x = x_tok[:, t, g * W:(g + 1) * W]
                    e = act.activation(x, x, ACT.Identity, bias=nb[:, t:t + 1], scale=rs[:, t:t + 1])
                e.then_inc(norm_hat, 1)

            def half_ffn(f, c0, xT, extra):
                name = ("x", "x3")[f - 1]

                def silu(j, n=W, i=None):
                    act.wait_ge(multiplied, plus(i, 16, c0 + 16 * j + 8))
                    if i is not None or j:
                        act.wait_ge(freed[B], plus(i, 1, U.at[("acc", c0 + 16 * j - 8)][1] + 1))
                    act.activation(sil[:, :, 0:n], ps[A][:, :].rearrange("p (t w) -> p t w", t=TT)[:, :, 0:n],
                                   ACT.Silu).then_inc(freed[A], 1)

                for k in range(8):
                    if k in (3, 5):
                        group_hi((name, k // 2 + 1), xT, 4 * (k // 2 + 1))
                    make_hi(act, c0 + k + AHEAD)
                silu(0)
                with act.Fori(0, NFULL - 1) as i:
                    for k in range(8):
                        make_hi(act, c0 + 8 + k + AHEAD, i)
                    for k in range(8):
                        if k == 4:
                            group_hi(("h", f, 0), hT[f], 0, 4, i)
                        make_hi(act, c0 + 16 + k + AHEAD, i)
                    silu(1, W, i)
                c = c0 + 16 * NFULL - 8
                for k in range(8):
                    make_hi(act, c + k + AHEAD)
                for k in range(8):
                    if k == 4:
                        group_hi(("h", f, NFULL - 1), hT[f], 4 * NFULL - 4)
                    make_hi(act, c + 8 + k + AHEAD)
                silu(NFULL, WL)
                for k in range(8):
                    make_hi(act, c + 16 + k + AHEAD)
                for b in range(4):
                    for m in range(KD2):
                        if b == 0 and m == 3:
                            group_hi(("h", f, NFULL), hT[f], 4 * NFULL, WL // P)
                        extra(b, m)
                        make_hi(act, c + 24 + b * KD2 + m + AHEAD)

            mem_r = d["mem"].rearrange("(t p) n -> p t n", p=P)

            def load_mem(g):
                act.dma_start(stage[g % 2][:, :, :], mem_r[:, :, g * W:(g + 1) * W]).then_inc(mem_in[g], 16)

            def load_gb(i, dst, wait):
                act.wait_ge(multiplied, wait)
                act.dma_start(dst[:, :, :], d["ln"][i:i + 1, :, :].to_broadcast([P, 2, D])).then_inc(gb_in[i], 16)

            def extra1(b, m):
                if b == 0 and m == 4:
                    act.wait_ge(multiplied, C_DOWN1)
                    act.dma_start(wg[:, :], d["gate_w"]).then_inc(gate_in, 16)
                    w_over(act, ("h", 1, NFULL))
                    load_mem(0)
                    load_mem(1)
                if b == 0 and m in S_MEM:
                    g = S_MEM.index(m)
                    group_hi(("mem", g), memT, 4 * g)
                    if g < 2:
                        load_mem(g + 2)
                if b == 3 and m == 8:
                    load_gb(0, gb1, C_DOWN1 + 3 * KD2 + 8)

            def extra2(b, m):
                if b == 0 and m == 4:
                    load_gb(3, gb4, C_DOWN2)

            act.dma_start(const[:, :], d["const"]).then_inc(const_in, 16)
            for c in range(AHEAD):
                if c % 2 == 0:
                    group_hi(("x", c // 2), xT0, 2 * c)
                make_hi(act, c)
            half_ffn(1, C_FFN1, xT0, extra1)

            for k in range(8):
                if 1 <= k <= 4:
                    norm_piece(0, k - 1)
                if k >= 5:
                    group_hi(("x1", k - 5), x1T, 4 * (k - 5))
                make_hi(act, C_K0 + k + AHEAD)
            block_copy(C_K0, stage[1][:, :, :])

            dest = {"q": lambda i: sbq[:, 4 * i:4 * i + 4, :], "k": lambda i: sbk[:, :, :],
                    "nq": lambda i: nsq[:, 4 * i:4 * i + 4, :], "cmp": lambda i: kcT[:, :, :],
                    "slc": lambda i: kslT[:, :, :], "win": lambda i: kwnT[:, :, :]}
            def stick_breaking(s):
                for part, h in sb_work(s):
                    w = sba[:, h % 2, :]
                    if part == "z":
                        act.wait_ge(sb_z, h + 1)
                        if h >= 2:
                            act.wait_ge(sb_o, h - 1)
                        chain(act.activation(w, ps[T1][:, 0:384], ACT.Abs))
                        chain(act.activation(w, w, ACT.Exp, scale=-1.0))
                        act.activation(w, w, ACT.Ln, bias=1.0).then_inc(sb_ln, 1)
                    if part == "r":
                        act.wait_ge(sb_em, h + 1)
                        act.activation(w, w, ACT.Exp).then_inc(sb_w, 1)

            for n, (what, i, _) in enumerate(WIN):
                c = C_WIN + 8 * n
                for k in range(8):
                    if n == 0:
                        if k == 1:
                            group_hi(("x1", 3), x1T, 12)
                        if k == 4:
                            w_normed(act, 4)
                            act.dma_start(angle[:, :, :, :], d["angle"]).then_inc(angle_in, 16)
                            act.dma_start(w2[:, :, :, :], d["cmp_w2"]).then_inc(cmp_in, 16)
                        if k == 5:
                            group_copy(("kt", 0), KT[:, 0:4, :])
                            act.wait_ge(gate_in, 16)
                            act.activation(wg_parts[0][:, 0:KD * NG], wg[:, :], ACT.Copy).then_inc(gate_hi, 1)
                    elif k == 3 and WIN[n - 1][0] != "v":
                        group_copy(("w", n - 1), dest[WIN[n - 1][0]](WIN[n - 1][1]))
                    if 8 * n + k == S_GATES + 1:
                        w_ready(act, "gates")
                        act.activation(gate_t[0:NG, :], ps[T1][0:NG, 0:T], ACT.Exp, scale=-1.0).then_inc(freed[T1], 1)
                    stick_breaking(8 * n + k)
                    make_hi(act, c + k + AHEAD)
                if what == "q":
                    block_copy(c, stage[n % 2][:, :, :], SCALE)
                if what == "k":
                    block_copy(c, stage[n % 2][:, :, :])
                if what == "v":
                    block_copy(c, sbv[:, :, :])

            for k in range(8):
                stick_breaking(8 * NWIN + k)
                if k == 1:
                    act.wait_ge(multiplied, C_K1)
                    act.dma_start(posT[:, :, :], d["pos"]).then_inc(cmp_in, 16)
                    act.wait_ge(sb_o, SBH)
                    act.dma_start(mg[:, :], d["mix_norm_g"].to_broadcast([P, D])).then_inc(mg_in, 16)
                if k == 3:
                    group_copy(("w", NWIN - 1), dest["win"](0))
                make_hi(act, C_K1 + k + AHEAD)
            block_copy(C_K1, kstage[:, :, :])

            for i in range(2):
                for k in range(8):
                    if i == 0 and k == 3:
                        group_copy(("kt", 1), KT[:, 4:8, :])
                    make_hi(act, C_CMP + 8 * i + k + AHEAD)
                c, p = C_CMP + 8 * i, (B, A)[i]
                act.wait_ge(multiplied, c + 8)
                act.activation(hc[0:LOROW + GC, i, :], ps[p][0:LOROW + GC, 0:CH], ACT.Copy).then_inc(freed[p], 1)

            def outputs(g):
                w_ready(act, ("O", g))
                act.activation(nsq[:, g * REP:(g + 1) * REP, :].rearrange("p r (t d) -> p t r d", t=TT),
                               ps[B][:, :].rearrange("p (t r d) -> p t r d", t=TT, r=REP), ACT.Copy).then_inc(freed[B], 1)

            for s in range(32):
                b, k = divmod(s, 8)
                n, part = divmod(s, 4)
                g, br, tq = UNITS[n]
                keys = (tq + 1) * P
                if part == 0:
                    act.wait_ge(ns_max, n + 1)
                    for r in range(REP):
                        e = act.activation(prob[:, r, 0:keys], prob[:, r, 0:keys], ACT.Exp, bias=nm[:, r:r + 1],
                                           scale=SCALE, accum_out=sm[:, r:r + 1])
                    e.then_inc(ns_exp, 1)
                if s in S_KT:
                    b2 = 2 + S_KT.index(s)
                    group_copy(("kt", b2), KT[:, 4 * b2:4 * b2 + 4, :])
                if s == 18:
                    outputs(0)
                if s == S_CMP[3] + 1:
                    w_ready(act, "cp")
                    act.activation(pcT[:, :, :, :].rearrange("p t g q -> p (t g q)"), ps[T1][:, 0:TT * GROUPS * P],
                                   ACT.Copy).then_inc(freed[T1], 1)
                if s == S_CMP[0] + 1:
                    act.wait_ge(gelu_x, 1)
                    act.activation(ug[:, 2, :, 0:GC], ug[:, 1, :, 0:GC], ACT.Exp, scale=-2.0 * GELU).then_inc(gelu_e, 1)
                if s == S_CMP[2] + 1:
                    act.wait_ge(cs_max, 1)
                    act.activation(pcs[:, :, :, :], pcs[:, :, :, :], ACT.Exp, scale=SCALE).then_inc(cs_exp, 1)
                if part == 3:
                    w_ready(act, ("p", n))
                    act.activation(probT[:, :, 0:tq + 1, :],
                                   ps[T1][:, :].rearrange("p (r k q) -> p r k q", r=REP, k=TT)[:, :, 0:tq + 1, :],
                                   ACT.Copy).then_inc(freed[T1], 1)
                make_hi(act, C_FILL + s + AHEAD)
                if k == 7:
                    if b < 2:
                        block_copy(C_FILL + 8 * b, kstage[:, :, :])
                    else:
                        block_copy(C_FILL + 8 * b, V[:, :, (b - 2) * W:(b - 1) * W])

            def squares(half, src):
                for t, o in enumerate((prob, scrap)):
                    e = act.activation(o[:, :, :].rearrange("p a b -> p (a b)").rearrange("p (h d) -> p h d", h=8),
                                       src[:, :, t * P:(t + 1) * P], ACT.Square, scale=1.0 / 32,
                                       accum_out=ss[:, 2 * half + t:2 * half + t + 1])
                e.then_inc(sq_made, 1)

            for k in range(8):
                if k == 0:
                    squares(0, sbq)
                if k == 2:
                    outputs(1)
                    act.wait_ge(freed[B], U.at[("O", 1)][1] + 1)
                    squares(1, nsq)
                if k in S_Y:
                    group_hi(("y", S_Y.index(k)), yT, 4 * S_Y.index(k))
                make_hi(act, C_V2 + k + AHEAD)
            block_copy(C_V2, V[:, :, 2 * W:3 * W])

            for k in range(32):
                if k == 4:
                    load_gb(1, gb2, C_V2 + 8)
                make_hi(act, C_WOUT + k + AHEAD)

            for k in range(8):
                if 1 <= k <= 4:
                    norm_piece(1, k - 1)
                if k >= 5:
                    group_hi(("x2", k - 5), x2T, 4 * (k - 5))
                make_hi(act, C_V3 + k + AHEAD)
            block_copy(C_V3, V[:, :, 3 * W:4 * W])

            for b in range(4):
                for k in range(8):
                    if b == 0 and k == 1:
                        group_hi(("x2", 3), x2T, 12)
                    if b and k == 3:
                        group_copy(("qt", b - 1), qT[:, 4 * b - 4:4 * b, :])
                    make_hi(act, C_WQ + 8 * b + k + AHEAD)
                block_copy(C_WQ + 8 * b, stage[b % 2][:, :, :])
            group_copy(("qt", 3), qT[:, 12:16, :])

            def m_exps(h):
                act.wait_ge(m_max, h + 1)
                if h >= 2:
                    w_ready(act, ("mp", h - 2))
                for t in range(TT):
                    e = act.activation(mprob[h % 2][:, t, :], ps[h // 2][:, h % 2 * W + t * T:h % 2 * W + (t + 1) * T],
                                       ACT.Exp, bias=nm[:, 2 * h + t:2 * h + t + 1], scale=MSCALE,
                                       accum_out=sm[:, 2 * h + t:2 * h + t + 1])
                e.then_inc(m_exp, 1)

            m_exps(0)
            m_exps(1)
            for h in range(MH):
                if h:
                    group_hi(("ot", h - 1), oT, 4 * h - 4)
                if h + 2 < MH:
                    m_exps(h + 2)
            group_hi(("ot", MH - 1), oT, 4 * MH - 4)
            for k in range(32):
                if k == 2:
                    load_gb(2, gb3, C_WO)
                make_hi(act, C_WO + k + AHEAD)

            for g in range(4):
                norm_piece(2, g)
                if g >= 2:
                    group_hi(("x3", g - 2), xT3, 4 * (g - 2))
            half_ffn(2, C_FFN2, xT3, extra2)
            for g in range(4):
                norm_piece(3, g)

        @block.vector
        def _(dve):
            steps = [0]

            def did(ins):
                steps[0] += 1
                ins.then_inc(dve_step, 1)

            def see():
                dve.wait_ge(dve_step, steps[0])

            def chain(ins):
                did(ins)
                see()

            def group_lo(name, dst, kt, n=4, i=None):
                p, _ = U.at[name]
                split_wait(dve, name, i)
                at = slice(kt, kt + n) if i is None else bass.ds(i * 4, n)
                dve.tensor_tensor(dst[1][:, at, :], ps[p][:, 0:n * T].rearrange("p (k t) -> p k t", t=T),
                                  dst[0][:, at, :].bitcast(F32), ALU.subtract).then_inc(freed[p], 1)

            def half_ffn(f, c0, xT, extra):
                name = ("x", "x3")[f - 1]

                def hidden(j, n=W, i=None):
                    dve.wait_ge(multiplied, plus(i, 16, c0 + 16 * j + 16))
                    dve.wait_ge(freed[A], plus(i, 1, U.at[("acc", c0 + 16 * j)][1] + 1))
                    dve.tensor_tensor(hbuf[:, :, 0:n], ps[B][:, :].rearrange("p (t w) -> p t w", t=TT)[:, :, 0:n],
                                      sil[:, :, 0:n], ALU.mult).then_inc(freed[B], 1)

                for k in range(8):
                    if k in (3, 5):
                        group_lo((name, k // 2 + 1), xT, 4 * (k // 2 + 1))
                    make_lo(dve, c0 + k + AHEAD)
                with dve.Fori(0, NFULL - 1) as i:
                    for k in range(8):
                        make_lo(dve, c0 + 8 + k + AHEAD, i)
                    hidden(0, W, i)
                    for k in range(8):
                        if k == 4:
                            group_lo(("h", f, 0), hT[f], 0, 4, i)
                        make_lo(dve, c0 + 16 + k + AHEAD, i)
                c = c0 + 16 * NFULL - 8
                for k in range(8):
                    make_lo(dve, c + k + AHEAD)
                hidden(NFULL - 1)
                for k in range(8):
                    if k == 4:
                        group_lo(("h", f, NFULL - 1), hT[f], 4 * NFULL - 4)
                    make_lo(dve, c + 8 + k + AHEAD)
                for k in range(8):
                    make_lo(dve, c + 16 + k + AHEAD)
                hidden(NFULL, WL)
                for b in range(4):
                    for m in range(KD2):
                        if b == 0 and m == 3:
                            group_lo(("h", f, NFULL), hT[f], 4 * NFULL, WL // P)
                        extra(b, m)
                        if b and m == 0:
                            norm_add(c + 24 + b * KD2, ("d", f, b - 1), b - 1, 0.5)
                        make_lo(dve, c + 24 + b * KD2 + m + AHEAD)

            def norm_add(c, name, b, factor):
                p, _ = U.at[name]
                dve.wait_ge(multiplied, c)
                x = x_tok[:, :, b * W:(b + 1) * W]
                dve.scalar_tensor_tensor(out=x, in0=ps[p][:, :].rearrange("p (t w) -> p t w", t=TT),
                                         scalar=factor / ALPHA, in1=x, op0=ALU.mult, op1=ALU.add).then_inc(freed[p], 1)
                w_over(dve, name)
                for t in range(TT):
                    did(dve.bn_stats(st[:, t, b, :], x_tok[:, t, b * W:(b + 1) * W]))

            def inverse_root(r, v, w):
                chain(dve.tensor_scalar(r.bitcast(I32), v.bitcast(I32), -0.5, float(0x5F3759DF), ALU.mult, ALU.add))
                for n in range(3):
                    chain(dve.tensor_tensor(w, r, r, ALU.mult))
                    chain(dve.scalar_tensor_tensor(out=w, in0=w, scalar=-0.5, in1=v, op0=ALU.mult, op1=ALU.mult))
                    chain(dve.scalar_tensor_tensor(out=r, in0=w, scalar=1.5, in1=r, op0=ALU.add, op1=ALU.mult))

            def norm_finish():
                see()
                for t in range(TT):
                    did(dve.bn_aggr(mv[:, t, :], st[:, t, :, :].rearrange("p a b -> p (a b)")))
                see()
                r, v = rs[:, 0:TT], rv[:, 0:TT]
                chain(dve.tensor_scalar(v, mv[:, :, 1], EPS1, None, ALU.add))
                inverse_root(r, v, rw[:, 0:TT])
                dve.scalar_tensor_tensor(out=nb[:, :], in0=mv[:, :, 0], scalar=-1.0, in1=r, op0=ALU.mult,
                                         op1=ALU.mult).then_inc(norm_rs, 1)

            def norm_piece(i, g, gb):
                if g == 0:
                    dve.wait_ge(gb_in[i], 16)
                dve.wait_ge(norm_hat, 4 * i + g + 1)
                cols = slice(g * W, (g + 1) * W)
                x = x_tok[:, :, cols]
                dve.tensor_tensor(x, x, gb[:, 0:1, cols].to_broadcast([P, TT, W]), ALU.mult).then_inc(norm_gain, 1)
                dve.wait_ge(norm_gain, 4 * i + g + 1)
                dve.tensor_tensor(x_tok[:, 1, cols], x_tok[:, 1, cols], gb[:, 1, cols], ALU.add).then_inc(normed1, 1)

            def extra1(b, m):
                if b == 0 and m in S_MEM:
                    g = S_MEM.index(m)
                    group_lo(("mem", g), memT, 4 * g)

            for c in range(AHEAD):
                if c % 2 == 0:
                    group_lo(("x", c // 2), xT0, 2 * c)
                make_lo(dve, c)
            half_ffn(1, C_FFN1, xT0, extra1)

            for k in range(8):
                if k == 0:
                    norm_add(C_K0, ("d", 1, 3), 3, 0.5)
                    norm_finish()
                if 1 <= k <= 4:
                    norm_piece(0, k - 1, gb1)
                if k >= 5:
                    group_lo(("x1", k - 5), x1T, 4 * (k - 5))
                make_lo(dve, C_K0 + k + AHEAD)

            def rotate(c, n, dst, cols):
                p, _ = U.at[("acc", c)]
                heads = cols // HD
                for t in range(TT):
                    x = ps[p][:, t * W:t * W + cols].rearrange("p (h d) -> p h d", d=HD)
                    o = dst[:, t, 0:cols].rearrange("p (h d) -> p h d", d=HD)
                    r = rot[:, 0:cols].rearrange("p (h d) -> p h d", d=HD)
                    co = angle[:, 0, t:t + 1, :].to_broadcast([P, heads, HD])
                    si = angle[:, 1, t:t + 1, :].to_broadcast([P, heads, HD])
                    dve.tensor_tensor(o, x, co, ALU.mult)
                    dve.tensor_tensor(r[:, :, 0:HALF], x[:, :, HALF:HD], si[:, :, 0:HALF], ALU.mult)
                    chain(dve.tensor_tensor(r[:, :, HALF:HD], x[:, :, 0:HALF], si[:, :, HALF:HD], ALU.mult))
                    e = dve.tensor_tensor(o, o, r, ALU.add)
                    if t == 0 or cols < W:
                        chain(e)
                return e

            def stick_breaking(s):
                for part, h in sb_work(s):
                    if part == "r":
                        dve.wait_ge(sb_r, h + 1)
                        dve.tensor_tensor(sba[:, h % 2, :], ps[T1][:, 0:384], cap, ALU.min).then_inc(sb_em, 1)
                    if part == "o":
                        dve.wait_ge(sb_o, h + 1)
                        e = dve.tensor_copy(sbq[:, h, :], ps[T1][:, W:W + T])
                        e.then_inc(*((freed[T1], 1) if h == SBH - 1 else (sb_out, 1)))

            def soft_plus(s):
                for part, h in sb_work(s):
                    if part == "z":
                        l = sbl[:, h % 2, :]
                        dve.wait_ge(sb_ln, h + 1)
                        chain(dve.scalar_tensor_tensor(out=l, in0=ps[T1][:, 0:384], scalar=0.0, in1=sba[:, h % 2, :],
                                                       op0=ALU.max, op1=ALU.add))
                        diag = l.rearrange("p (a q) -> p a q", a=3)[:, 0:3:2, :]
                        dve.tensor_tensor(diag, diag, tri.rearrange("p (o q) -> p o q", o=1).to_broadcast(
                            [P, 2, P]), ALU.mult).then_inc(sb_l, 1)

            for n, (what, i, _) in enumerate(WIN):
                c = C_WIN + 8 * n
                for k in range(8):
                    if n == 0 and k == 1:
                        group_lo(("x1", 3), x1T, 12)
                    if n == 0 and k == 6:
                        dve.wait_ge(gate_hi, 1)
                        dve.tensor_tensor(wg_parts[1][:, 0:KD * NG], wg[:, :], wg_parts[0][:, 0:KD * NG].bitcast(F32),
                                          ALU.subtract).then_inc(gate_lo, 1)
                    if 8 * n + k == S_GATES + 3:
                        w_ready(dve, "gates_t")
                        dve.tensor_scalar(gate[:, :, :], ps[T1][:, 0:TT * NG].rearrange("p (t n) -> p t n", t=TT), 1.0,
                                          None, ALU.add).then_inc(freed[T1], 1)
                        w_over(dve, "gates_t")
                        did(dve.reciprocal(gate[:, :, :], gate[:, :, :]))
                    stick_breaking(8 * n + k)
                    make_lo(dve, c + k + AHEAD)
                    soft_plus(8 * n + k)
                if what in ("nq", "cmp", "slc", "win"):
                    p, _ = U.at[("acc", c)]
                    dve.wait_ge(multiplied, c + 8)
                    dve.wait_ge(angle_in, 16)
                    e = rotate(c, n, stage[n % 2], W if what == "nq" else T)
                    if what != "nq":
                        right = ps[p][:, :].rearrange("p (t w) -> p t w", t=TT)[:, :, T:W]
                        to = {"cmp": stage[n % 2][:, :, T:W], "slc": vsw[:, 0, :, :], "win": vsw[:, 1, :, :]}[what]
                        e = dve.tensor_copy(to, right)
                    e.then_inc(freed[p], 1)

            def operand(i):
                if i:
                    dve.wait_ge(fc_made, i)
                for hf in range(2):
                    for g in range(GROUPS):
                        src = kcT[:, 2 * i + g, :].rearrange("p (n s) -> p s n", s=CS)[:, :, hf:hf + NC]
                        po = posT[:, i, hf * CS:(hf + 1) * CS].rearrange("p (s o) -> p s o", o=1).to_broadcast([P, CS, NC])
                        did(dve.tensor_tensor(fs[:, hf * CS:(hf + 1) * CS, g * NC:(g + 1) * NC], src, po, ALU.add))
                see()
                chain(dve.tensor_copy(FC[i][:, :, 0:GC], fs[:, :, :]))
                dve.tensor_tensor(FC[i][:, :, LOROW:LOROW + GC], fs[:, :, :], FC[i][:, :, 0:GC].bitcast(F32),
                                  ALU.subtract).then_inc(fc_made, 1)

            for k in range(8):
                stick_breaking(8 * NWIN + k)
                if k == 3:
                    dve.wait_ge(cmp_in, 32)
                    dve.wait_ge(cleared, 2)
                    operand(0)
                if k == 5:
                    operand(1)
                make_lo(dve, C_K1 + k + AHEAD)
            for k in range(16):
                make_lo(dve, C_CMP + k + AHEAD)

            def cmp_step(n):
                if n == 0:
                    w_ready(dve, "l1")
                    x, t = ug[:, 0, :, 0:GC], ug[:, 1, :, 0:GC]
                    dve.tensor_copy(x, ps[T1][:, 0:P].rearrange("p (a b) -> p a b", a=4)[:, :, 0:GC]).then_inc(freed[T1], 1)
                    w_over(dve, "l1")
                    chain(dve.tensor_tensor(t, x, x, ALU.mult))
                    chain(dve.tensor_scalar(t, t, 0.044715, 1.0, ALU.mult, ALU.add))
                    dve.tensor_tensor(t, t, x, ALU.mult).then_inc(gelu_x, 1)
                if n == 1:
                    w_ready(dve, "l2")
                    dve.tensor_copy(kcmp[:, :], ps[T1][:, 0:GC])
                    for g in range(GROUPS):
                        for r in range(REP):
                            e = dve.tensor_copy(vblk[32 * r:32 * r + NC, g, r * HD:(r + 1) * HD],
                                                ps[T1][32 * r:32 * r + NC, W + g * HD:W + (g + 1) * HD])
                    e.then_inc(freed[T1], 1)
                if n == 2:
                    w_ready(dve, "cs")
                    dve.tensor_tensor(pcs[:, :, :, :], ps[T1][:, 0:TT * NSH * NC].rearrange(
                        "p (t h c) -> p t h c", t=TT, h=NSH), cadd.to_broadcast([P, TT, NSH, NC]),
                        ALU.add).then_inc(freed[T1], 1)
                    w_over(dve, "cs")
                    chain(dve.tensor_reduce(cmx[:, :], pcs[:, :, :, :].rearrange("p t h c -> p (t h) c"), AX.X, ALU.max))
                    flat = pcs[:, :, :, :].rearrange("p t h c -> p (t h) c")
                    dve.tensor_tensor(flat, flat, cmx[:, :].rearrange("p (n o) -> p n o", o=1).to_broadcast(
                        [P, 16, NC]), ALU.subtract).then_inc(cs_max, 1)

            for s in range(32):
                b, k = divmod(s, 8)
                n, part = divmod(s, 4)
                g, br, tq = UNITS[n]
                keys = (tq + 1) * P
                if s in S_CMP[0:3]:
                    cmp_step(S_CMP.index(s))
                if part == 0:
                    w_ready(dve, ("s", n))
                    if n:
                        w_ready(dve, ("p", n - 1))
                    p = ps[T0]
                    for r in range(REP):
                        e = dve.tensor_tensor_reduce(
                            out=prob[:, r, 0:keys], in0=p[:, r * T:r * T + keys], in1=cmask[:, T - keys:T],
                            scale=1.0, scalar=-3.0e38, op0=ALU.add, op1=ALU.max, accum_out=mx[:, r:r + 1])
                    e.then_inc(freed[T0], 1)
                    w_over(dve, ("s", n))
                    dve.tensor_scalar(nm[:, 0:REP], mx[:, 0:REP], -SCALE, None, ALU.mult).then_inc(ns_max, 1)
                if part == 1:
                    dve.wait_ge(ns_exp, n + 1)
                    chain(dve.reciprocal(cf[:, 0:REP], sm[:, 0:REP]))
                    gt = gate[:, tq, :].rearrange("p (h j) -> p h j", j=3)[:, g * REP:(g + 1) * REP, 1 + br]
                    chain(dve.tensor_tensor(cf[:, 0:REP], cf[:, 0:REP], gt, ALU.mult))
                    pr = prob[:, :, 0:keys]
                    dve.tensor_tensor(pr, pr, cf[:, 0:REP].rearrange("p (r o) -> p r o", o=1).to_broadcast(
                        [P, REP, keys]), ALU.mult).then_inc(ns_prob, 1)
                if s == S_CMP[0] + 2:
                    dve.wait_ge(gelu_e, 1)
                    e = ug[:, 2, :, 0:GC]
                    chain(dve.tensor_scalar(e, e, 1.0, None, ALU.add))
                    chain(dve.reciprocal(e, e))
                    dve.tensor_tensor(ug[:, 3, :, 0:GC], ug[:, 0, :, 0:GC], e, ALU.mult).then_inc(gelu_made, 1)
                if s == S_CMP[2] + 2:
                    dve.wait_ge(cs_exp, 1)
                    dve.wait_ge(cleared, 3)
                    flat = pcs[:, :, :, :].rearrange("p t h c -> p (t h) c")
                    chain(dve.tensor_tensor(pcs[:, :, :, :], pcs[:, :, :, :], cmul.to_broadcast([P, TT, NSH, NC]), ALU.mult))
                    chain(dve.tensor_reduce(csm[:, :], flat, AX.X, ALU.add))
                    chain(dve.tensor_scalar(csm[:, :], csm[:, :], 1e-30, None, ALU.max))
                    chain(dve.reciprocal(ccf[:, :], csm[:, :]))
                    cg = ccf[:, :].rearrange("p (t h) -> p t h", t=TT)
                    chain(dve.tensor_tensor(cg, cg, gate[:, :, :].rearrange("p t (h j) -> p t h j", j=3)[:, :, :, 0],
                                            ALU.mult))
                    dve.tensor_tensor(pcp[:, :, :, 0:NC].rearrange("p t h c -> p (t h) c"), flat,
                                      ccf[:, :].rearrange("p (n o) -> p n o", o=1).to_broadcast([P, 16, NC]),
                                      ALU.mult).then_inc(cs_made, 1)
                make_lo(dve, C_FILL + s + AHEAD)

            for s in range(8):
                if s in (0, 3):
                    k = s // 3
                    dve.wait_ge(sq_made, k + 1)
                    of = slice(2 * k, 2 * k + 2)
                    chain(dve.tensor_scalar(rv[:, of], ss[:, of], RMS_EPS, None, ALU.add))
                    inverse_root(rs[:, of], rv[:, of], rw[:, of])
                    dve.wait_ge(mg_in, 16)
                    src = (sbq, nsq)[k]
                    for t in range(TT):
                        o = src[:, :, t * P:(t + 1) * P]
                        e = dve.scalar_tensor_tensor(
                            out=o, in0=o, scalar=rs[:, 2 * k + t:2 * k + t + 1],
                            in1=mg[:, k * 1024:(k + 1) * 1024].rearrange("p (h d) -> p h d", d=HD),
                            op0=ALU.mult, op1=ALU.mult)
                    e.then_inc(y_made, 1)
                if s in S_Y:
                    group_lo(("y", S_Y.index(s)), yT, 4 * S_Y.index(s))
                make_lo(dve, C_V2 + s + AHEAD)

            for b in range(4):
                c = C_WOUT + 8 * b
                for k in range(8):
                    make_lo(dve, c + k + AHEAD)
                norm_add(c + 8, ("acc", c), b, 1.0)

            norm_finish()
            for k in range(8):
                if 1 <= k <= 4:
                    norm_piece(1, k - 1, gb2)
                if k >= 5:
                    group_lo(("x2", k - 5), x2T, 4 * (k - 5))
                make_lo(dve, C_V3 + k + AHEAD)

            for s in range(32):
                if s == 1:
                    group_lo(("x2", 3), x2T, 12)
                make_lo(dve, C_WQ + s + AHEAD)

            for h in range(MH):
                dve.wait_ge(m_z, h + 1)
                chain(dve.tensor_reduce(mx[:, 2 * h:2 * h + 2], ps[h // 2][:, h % 2 * W:(h % 2 + 1) * W].rearrange(
                    "p (t m) -> p t m", t=TT), AX.X, ALU.max))
                dve.tensor_scalar(nm[:, 2 * h:2 * h + 2], mx[:, 2 * h:2 * h + 2], -MSCALE, None,
                                  ALU.mult).then_inc(m_max, 1)
            for h in range(MH):
                dve.wait_ge(m_exp, h + 1)
                e = dve.reciprocal(cf[:, 2 * h:2 * h + 2], sm[:, 2 * h:2 * h + 2])
                if h % 2:
                    e.then_inc(freed[h // 2], 1)
                    w_over(dve, f"z{h // 2}")
                else:
                    chain(e)
                w_ready(dve, ("mp", h))
                dve.tensor_copy(mprobT[h % 2][:, :, :, :].rearrange("p t m q -> p (t m q)"),
                                ps[T0][:, 0:TT * TT * P]).then_inc(freed[T0], 1)
                w_ready(dve, ("mo", h))
                for t in range(TT):
                    e = dve.tensor_scalar(mo_tok[:, t, h * W:(h + 1) * W], ps[T1][:, t * W:(t + 1) * W],
                                          cf[:, 2 * h + t:2 * h + t + 1], None, ALU.mult)
                e.then_inc(freed[T1], 1)
                if h:
                    group_lo(("ot", h - 1), oT, 4 * h - 4)
            group_lo(("ot", MH - 1), oT, 4 * MH - 4)
            for b in range(4):
                c = C_WO + 8 * b
                for k in range(8):
                    make_lo(dve, c + k + AHEAD)
                norm_add(c + 8, ("acc", c), b, 1.0)

            norm_finish()
            for g in range(4):
                norm_piece(2, g, gb3)
                if g >= 2:
                    group_lo(("x3", g - 2), xT3, 4 * (g - 2))
            half_ffn(2, C_FFN2, xT3, lambda b, m: None)
            norm_add(C_END, ("d", 2, 3), 3, 0.5)
            norm_finish()
            for g in range(4):
                norm_piece(3, g, gb4)

        @block.gpsimd
        def _(pool):
            def norm_bias(i, gb):
                pool.wait_ge(gb_in[i], 16)
                for g in range(4):
                    cols = slice(g * W, (g + 1) * W)
                    pool.wait_ge(norm_gain, 4 * i + g + 1)
                    pool.tensor_tensor(x_tok[:, 0, cols], x_tok[:, 0, cols], gb[:, 1, cols], ALU.add).then_inc(
                        normed0, 1)

            for w in wg_parts:
                e = pool.memset(w[:, KD * NG:].bitcast(F32), 0.0)
            e.then_inc(cleared, 1)
            norm_bias(0, gb1)
            pool.wait_ge(multiplied, C_K1)
            for i in range(2):
                pool.memset(FC[i][:, :, GC:LOROW].bitcast(F32), 0.0)
            pool.memset(vblk[:, :, :], 0.0).then_inc(cleared, 1)
            pool.wait_ge(multiplied, C_FILL)
            pool.memset(pcp[:, :, :, :], 0.0).then_inc(cleared, 1)
            norm_bias(1, gb2)
            norm_bias(2, gb3)
            norm_bias(3, gb4)


_OUT = "out_0_dram"


def kernel(**inputs):
    import concourse.bacc as bacc
    from concourse.bass_utils import run_bass_kernel_spmd

    a = {k: np.asarray(v) for k, v in inputs.items()}
    const, angle = constants()
    arrays = {
        "x": a["x"][0], "mem": a["mem"][0], "const": const, "angle": angle,
        "ln": np.stack([np.stack([a[f"ln{i}_g"][0], a[f"ln{i}_b"][0]]) for i in (1, 2, 3, 4)]),
        "pos": np.stack([a["cmp_pos_k"][0].T, a["cmp_pos_v"][0].T], 1),
        "gate_w": a["w_in"][0][:, GATE_COL:].reshape(KD, P, NG).transpose(1, 0, 2).reshape(P, KD * NG),
        "cmp_w2": np.stack([a[f"cmp_w2_{i}"][0].reshape(2, P, HD) for i in "kv"]).transpose(2, 0, 1, 3),
        "mix_norm_g": a["mix_norm_g"],
    }
    for n in ("ffn1_gate", "ffn1_up", "ffn1_down", "w_in", "cmp_w1_k", "cmp_w1_v", "w_out", "mem_wq", "mem_wk",
              "mem_wv", "mem_wo", "ffn2_gate", "ffn2_up", "ffn2_down"):
        arrays[n] = a[n][0]
    arrays = {f"in_{k}_dram": np.ascontiguousarray(v) for k, v in arrays.items()}
    nc = bacc.Bacc("TRN2", target_bir_lowering=False, num_devices=1, dynamic_dma_scratch_size=1024)
    d = {k[3:-5]: nc.dram_tensor(k, v.shape, F32, kind="ExternalInput").ap() for k, v in arrays.items()}
    out = nc.dram_tensor(_OUT, (T, D), F32, kind="ExternalOutput").ap()
    hybrid_layer(nc, d, out)
    r = run_bass_kernel_spmd(nc, [arrays], core_ids=[0])
    return r.results[0][_OUT].reshape(1, T, D)
```

```python
from contextlib import ExitStack

import numpy as np

import concourse.bass as bass
import concourse.mybir as mybir
from concourse.alu_op_type import AluOpType as ALU

F32 = mybir.dt.float32
F32R = mybir.dt.float32r
I32 = mybir.dt.int32
ACT = mybir.ActivationFunctionType
AX = mybir.AxisListType

P = 128
T = 256
TT = T // P
D = 2048
KD = D // P
DFF = 5504
KF = DFF // P
W = 512
NFULL = DFF // W
WL = DFF - NFULL * W
HD = 128
HALF = HD // 2
SBH, NSH, GROUPS = 8, 8, 2
REP = NSH // GROUPS
CB, CS, CH = 32, 16, 256
NC = (T - CB) // CS + 1
GC = GROUPS * NC
LOROW = 64
MH = 4
MK = D // MH // P
SCALE = float(HD) ** -0.5
MSCALE = float(D // MH) ** -0.5
ALPHA = 2.0 ** 0.25
LN_EPS, RMS_EPS = 1e-5, 1e-6
NEG = -1e30

S_MEM = (6, 10, 14, 18)
AHEAD = 4
NRAW = 4
CHUNK = 1024
KD2 = (KF + 1) // 2
A, B, T0, T1 = range(4)
GELU = 0.7978845608028654
EPS1 = LN_EPS / ALPHA ** 2

C_FFN1 = 0
C_DOWN1 = C_FFN1 + 16 * (NFULL + 1)
C_K0 = C_DOWN1 + 4 * KD2
C_WIN = C_K0 + 8
NWIN = 11
C_K1 = C_WIN + 8 * NWIN
C_CMP = C_K1 + 8
C_FILL = C_CMP + 16
C_V2 = C_FILL + 32
C_WOUT = C_V2 + 8
C_V3 = C_WOUT + 32
C_WQ = C_V3 + 8
C_WO = C_WQ + 32
C_FFN2 = C_WO + 32
C_DOWN2 = C_FFN2 + 16 * (NFULL + 1)
C_END = C_DOWN2 + 4 * KD2

WIN = [("q", 0, 0), ("k", 0, 1024), ("v", 0, 2048), ("nq", 0, 3072), ("nq", 1, 3584), ("q", 1, 512),
       ("k", 1, 1536), ("v", 1, 2560), ("cmp", 0, 4096), ("slc", 0, 4608), ("win", 0, 5120)]
GATE_COL = 5632
NG = 24
SB_Z = (24, 32, 40, 48, 64, 70, 76, 82)
SB_R, SB_O = 3, 6
S_GATES = 8

UNITS = [(g, br, tt) for g in range(GROUPS) for br in range(2) for tt in range(TT)]

S_CMP = (1, 5, 9, 13)
S_KT = (10, 18)
S_Y = (3, 4, 6, 7)

M_AT = (("qt", (11, 19, 27, 32)), ("z", (13, 21, 29, 33)), ("mp", (17, 25, 31, 35)), ("mo", (18, 26, 33, 36)),
        ("ot", (21, 29, 34, 37)))

K_ID, K_NEGU, K_NEG1, K_TRI, K_CAP, K_CM, K_SEL, K_CADD, K_CMUL, NCONST = (
    0, 128, 256, 384, 512, 896, 1152, 1184, 1216, 1248)


def constants():
    c = np.zeros((P, NCONST), np.float32)
    r, q = np.arange(P)[:, None], np.arange(P)[None, :]
    c[:, K_ID:K_ID + P] = r == q
    c[:, K_NEGU:K_NEGU + P] = np.where(r >= q, -1.0, 0.0)
    c[:, K_NEG1:K_NEG1 + P] = -1.0
    c[:, K_TRI:K_TRI + P] = q > r
    cap = np.where(q > r, 0.0, NEG)
    c[:, K_CAP:K_CAP + 3 * P] = np.concatenate([cap, np.zeros((P, P)), cap], 1)
    c[:, K_CM + P:K_CM + 2 * P] = np.where(q <= r, 0.0, NEG)
    for n in range(GC):
        c[n, K_SEL + n] = 1.0
        c[LOROW + n, K_SEL + n] = 1.0
    end = np.arange(NC) * CS + CB - 1
    for t in range(TT):
        ok = end[None, :] <= t * P + np.arange(P)[:, None]
        c[:, K_CADD + t * 16:K_CADD + t * 16 + NC] = np.where(ok, 0.0, NEG)
        c[:, K_CMUL + t * 16:K_CMUL + t * 16 + NC] = ok
    inv = np.float32(10000.0) ** (-np.arange(HALF, dtype=np.float32) / np.float32(HALF))
    pos = np.arange(T, dtype=np.float32).reshape(TT, P)
    ang = (pos[:, :, None] * inv).astype(np.float32).transpose(1, 0, 2)
    co, si = np.cos(ang), np.sin(ang)
    a = np.stack([np.concatenate([co, co], 2), np.concatenate([-si, si], 2)], 1)
    return c, np.ascontiguousarray(a, np.float32)


def mem_work(s):
    return [(what, at.index(s)) for what, at in M_AT if s in at]


class Turns:

    def __init__(self):
        self.n = [0, 0, 0, 0]
        self.said = [0, 0, 0, 0]
        self.at = {}
        self.sends = {}
        self.split = {}

    def take(self, name, pair, split=False):
        self.at[name] = (pair, self.n[pair])
        self.n[pair] += 1
        if name != "sb" and name[0] not in ("acc", "d"):
            self.said[pair] += 1
            self.sends[name] = self.said[pair]
        if split:
            self.split[name] = len(self.split)


def turns():
    u = Turns()

    def acc(c, pair):
        u.take(("acc", c), pair)

    for g in range(4):
        u.take(("x", g), g, True)
    for f, c0 in ((1, C_FFN1), (2, C_FFN2)):
        if f == 2:
            for g in range(4):
                u.take(("x3", g), T0 + g % 2, True)
        acc(c0, A)
        for j in range(NFULL + 1):
            acc(c0 + 16 * j + 8, B)
            if j < NFULL:
                acc(c0 + 16 * j + 16, A)
            u.take(("h", f, j), T0, True)
        for b in range(4):
            u.take(("d", f, b), (A, B)[b % 2])
            if f == 1 and b == 0:
                for g in range(4):
                    u.take(("mem", g), (T1, T0)[g % 2], True)
        if f == 2:
            break
        acc(C_K0, A)
        for g in range(4):
            u.take(("x1", g), T0 + g % 2, True)
        u.take(("kt", 0), T0)
        for n in range(NWIN):
            acc(C_WIN + 8 * n, (B, A)[n % 2])
            if n and WIN[n - 1][0] != "v":
                u.take(("w", n - 1), T0)
        u.take("gates", T1)
        u.take("gates_t", T1)
        u.take("sb", T1)
        acc(C_K1, A)
        u.take(("w", NWIN - 1), T0)
        acc(C_CMP, B)
        u.take(("kt", 1), T0)
        acc(C_CMP + 8, A)
        for s in range(32):
            n, k = divmod(s, 4)
            if s in S_CMP:
                u.take(("l1", "l2", "cs", "cp")[S_CMP.index(s)], T1)
            if s in S_KT:
                u.take(("kt", 2 + S_KT.index(s)), T0)
            if k == 0:
                u.take(("s", n), T0)
            if k == 3:
                u.take(("p", n), T1)
            if s % 16 == 4:
                u.take(("O", s // 16), B)
        for b in range(4):
            u.take(("acc", C_FILL + 8 * b), A)
        acc(C_V2, A)
        for g in range(4):
            u.take(("y", g), T0 + g % 2, True)
        for b in range(4):
            acc(C_WOUT + 8 * b, (B, A)[b % 2])
        acc(C_V3, B)
        for g in range(4):
            u.take(("x2", g), T0 + g % 2, True)
        for s in range(64):
            if s % 8 == 0:
                acc(C_WQ + s, (A, B)[s // 8 % 2])
            for what, h in mem_work(s):
                u.take((what, h), T1 if what in ("z", "mp") else T0, what == "ot")
    return u


def hybrid_layer(nc, d, out):
    U = turns()
    KB = 1024
    base = (nc.sbuf_base + 31) // 32 * 32
    o_raw, o_hi, o_lo, o_x = base, base + 32 * KB, base + 48 * KB, base + 64 * KB
    o_X, o_H, o_S = base + 80 * KB, base + 112 * KB, base + 200 * KB

    def sb(name, shape, dt, offset):
        return nc.alloc_sbuf_tensor_at(name, shape, dt, offset=offset)

    def two(name, kt, offset):
        return [sb(f"{name}_{n}", [P, kt, T], F32R, offset + i * kt * KB) for i, n in enumerate(("hi", "lo"))]

    raw = sb("raw", [P, NRAW, 2 * CHUNK], F32, o_raw)
    whi = sb("whi", [P, AHEAD, CHUNK], F32R, o_hi)
    wlo = sb("wlo", [P, AHEAD, CHUNK], F32R, o_lo)
    x_tok = sb("x_tok", [P, TT, D], F32, o_x)
    xT0 = two("xT0", KD, o_X)
    memT = two("memT", KD, o_X)
    oT = two("oT", KD, o_X)
    xT3 = two("xT3", KD, o_X)
    gb4 = sb("gb4", [P, 2, D], F32, o_X)
    hT = {1: two("hT1", KF, o_H), 2: two("hT2", KF, o_H)}
    gb1 = sb("gb1", [P, 2, D], F32, o_H)
    V = sb("V", [P, TT, D], F32, o_H)
    sba = sb("sba", [P, 2, 384], F32, o_H)
    sbl = sb("sbl", [P, 2, 384], F32, o_H + 3 * KB)
    rot = sb("rot", [P, W], F32, o_H + 6 * KB)
    angle = sb("angle", [P, 2, TT, P], F32, o_H + 8 * KB)
    kcT = sb("kcT", [P, 4, T], F32, o_H + 12 * KB)
    kstage = sb("kstage", [P, TT, W], F32, o_H)
    fs = sb("fs", [P, CB, GC], F32, o_H + 4 * KB)
    ug = sb("ug", [P, 4, 4, 32], F32, o_H + 4 * KB)
    w2 = sb("w2", [P, 2, 2, HD], F32, o_H + 10 * KB)
    x1T = two("x1T", KD, o_H + 16 * KB)
    FC = [sb(f"FC{i}", [P, CB, LOROW + GC], F32R, o_H + (16 + i * 12) * KB) for i in range(2)]
    pcs = sb("pcs", [P, TT, NSH, NC], F32, o_H + 16 * KB)
    pcp = sb("pcp", [P, TT, NSH, 32], F32, o_H + 18 * KB)
    pcT = sb("pcT", [P, TT, GROUPS, P], F32, o_H + 20 * KB)
    scrap = sb("scrap", [P, REP, T], F32, o_H + 32 * KB)
    hc = sb("hc", [P, 2, CH], F32, o_H + 40 * KB)
    vblk = sb("vblk", [P, GROUPS, W], F32, o_H + 42 * KB)
    posT = sb("posT", [P, 2, CB], F32, o_H + 46 * KB)
    kcmp = sb("kcmp", [P, GC], F32, o_H + 46 * KB + 512)
    yT = two("yT", KD, o_H + 16 * KB)
    x2T = two("x2T", KD, o_H + 16 * KB)
    mo_tok = sb("mo_tok", [P, 2, TT, W], F32, o_H + 80 * KB)
    gb3 = sb("gb3", [P, 2, D], F32, o_H + 32 * KB)
    KT = sb("KT", [P, KD, T], F32, o_H + 48 * KB)
    sbq = sb("sbq", [P, SBH, T], F32, o_H + 64 * KB)
    nsq = sb("nsq", [P, NSH, T], F32, o_H + 72 * KB)
    gb2 = sb("gb2", [P, 2, D], F32, o_H + 64 * KB)
    qT = sb("qT", [P, KD, T], F32, o_H + 64 * KB)
    sbk = sb("sbk", [P, 4, T], F32, o_H + 80 * KB)
    sbv = sb("sbv", [P, TT, W], F32, o_H + 84 * KB)
    mg = sb("mg", [P, D], F32, o_H + 80 * KB)
    at = [o_S]

    def small(name, shape):
        t = sb(name, shape, F32, at[0])
        at[0] += (4 * int(np.prod(shape[1:])) + 31) // 32 * 32
        return t

    const = small("const", [P, NCONST])
    o_stage = at[0]
    stage = [small("stage0", [P, TT, W]), small("stage1", [P, TT, W])]
    sil = sb("sil", [P, TT, W], F32, o_stage)
    hbuf = sb("hbuf", [P, TT, W], F32, o_stage + 4 * KB)
    prob = sb("prob", [P, REP, T], F32, o_stage)
    probT = sb("probT", [P, REP, TT, P], F32, o_stage + 4 * KB)
    o_keys = at[0]
    mprob = [sb(f"mprob{i}", [P, TT, T], F32, o_keys + 2 * i * KB) for i in range(2)]
    mprobT = [sb(f"mprobT{i}", [P, TT, TT, P], F32, o_keys + (4 + 2 * i) * KB) for i in range(2)]
    kslT = small("kslT", [P, GROUPS, T])
    kwnT = small("kwnT", [P, GROUPS, T])
    wg = sb("wg", [P, KD * NG], F32, at[0] - 2 * KB)
    gate_t = sb("gate_t", [P, T], F32, at[0] - 4 * KB)
    wg_parts = [sb(f"wg_{n}", [P, KD * NG + P - NG], F32R, at[0] + 2 * KB * i) for i, n in enumerate(("hi", "lo"))]
    vsw = small("vsw", [P, 2, TT, T])
    st = small("st", [P, TT, 4, 6])
    mv = small("mv", [P, TT, 2])
    rs = small("rs", [P, 4])
    rv = small("rv", [P, 4])
    rw = small("rw", [P, 4])
    nb = small("nb", [P, TT])
    ss = small("ss", [P, 4])
    gate = small("gate", [P, TT, NG])
    mx = small("mx", [P, 8])
    nm = small("nm", [P, 8])
    sm = small("sm", [P, 8])
    cf = small("cf", [P, 8])
    cmx = small("cmx", [P, 16])
    csm = small("csm", [P, 16])
    ccf = small("ccf", [P, 16])
    assert at[0] <= 229368

    ident = const[:, K_ID:K_ID + P]
    negu = const[:, K_NEGU:K_NEGU + P]
    neg1 = const[:, K_NEG1:K_NEG1 + P]
    tri = const[:, K_TRI:K_TRI + P]
    cap = const[:, K_CAP:K_CAP + 3 * P]
    cmask = const[:, K_CM:K_CM + 2 * P]
    sel = const[:, K_SEL:K_SEL + GC]
    cadd = const[:, K_CADD:K_CADD + 32].rearrange("p (t o c) -> p t o c", t=TT, o=1)[:, :, :, 0:NC]
    cmul = const[:, K_CMUL:K_CMUL + 32].rearrange("p (t o c) -> p t o c", t=TT, o=1)[:, :, :, 0:NC]

    with ExitStack() as ctx:
        ps = [ctx.enter_context(nc.psum_tensor(f"ps_{n}", [P, 2 * W], F32)) for n in ("A", "B", "T0", "T1")]

        def sem(name):
            return ctx.enter_context(nc.semaphore(name))

        landed = [sem(f"landed{i}") for i in range(NRAW)]
        hi_made, lo_made, multiplied = sem("hi_made"), sem("lo_made"), sem("multiplied")
        ready = [sem(f"ready_{n}") for n in ("A", "B", "T0", "T1")]
        freed = [sem(f"freed_{n}") for n in ("A", "B", "T0", "T1")]
        split_hi = sem("split_hi")
        x_in = [sem(f"x_in{g}") for g in range(4)]
        mem_in = [sem(f"mem_in{g}") for g in range(4)]
        ident_in, const_in, angle_in, gate_in, cmp_in, mg_in = (
            sem("ident_in"), sem("const_in"), sem("angle_in"), sem("gate_in"), sem("cmp_in"), sem("mg_in"))
        gate_hi, gate_lo = sem("gate_hi"), sem("gate_lo")
        gb_in = [sem(f"gb_in{i}") for i in range(4)]
        norm_rs, norm_hat, norm_gain, normed0, normed1 = (
            sem("norm_rs"), sem("norm_hat"), sem("norm_gain"), sem("normed0"), sem("normed1"))
        sb_z, sb_ln, sb_l, sb_r, sb_em, sb_w, sb_o, sb_out = (
            sem("sb_z"), sem("sb_ln"), sem("sb_l"), sem("sb_r"), sem("sb_em"), sem("sb_w"),
            sem("sb_o"), sem("sb_out"))
        cleared, fc_made, gelu_x, gelu_e, gelu_made = (
            sem("cleared"), sem("fc_made"), sem("gelu_x"), sem("gelu_e"), sem("gelu_made"))
        cs_max, cs_exp, cs_made = sem("cs_max"), sem("cs_exp"), sem("cs_made")
        ns_max, ns_exp, ns_prob = sem("ns_max"), sem("ns_exp"), sem("ns_prob")
        sq_made, y_made = sem("sq_made"), sem("y_made")
        m_max = sem("m_max")
        dve_step, act_step = sem("dve_step"), sem("act_step")
        stored = sem("stored")
        block = ctx.enter_context(nc.Block())

        def w_ready(e, name):
            e.wait_ge(ready[U.at[name][0]], U.sends[name])

        def w_free(e, name, more=0):
            p, n = U.at[name]
            if n:
                e.wait_ge(freed[p], n + more)

        def w_normed(e, n):
            e.wait_ge(normed0, n)
            e.wait_ge(normed1, n)

        def w_over(e, name):
            p, n = U.at[name]
            e.wait_ge(freed[p], n + 1)

        @block.sync
        def _(sp):
            def piece(n, slot, src, cols, wait=True):
                if wait:
                    sp.wait_ge(lo_made, 2 * (n - NRAW) + 2)
                k = src.shape[1]
                sp.dma_start(raw[:, slot, 0:k * cols].rearrange("p (k w) -> p k w", w=cols), src).then_inc(
                    landed[slot], 16)

            def cols_of(w, k0, k1, c0, n):
                return w.rearrange("(k p) n -> p k n", p=P)[:, k0:k1, bass.ds(c0, n)]

            def blk(w, first, c0, n=W):
                for k in range(4):
                    piece(first + k, k, cols_of(w, 4 * k, 4 * k + 4, c0, n), n)

            def half_ffn(f, c0):
                g, u, dn = d[f"ffn{f}_gate"], d[f"ffn{f}_up"], d[f"ffn{f}_down"]
                if f == 2:
                    blk(g, c0 // 2, 0)
                else:
                    for k in range(4):
                        sp.dma_start(x_tok[:, :, k * W:(k + 1) * W], d["x"].rearrange("(t p) n -> p t n", p=P)[
                            :, :, k * W:(k + 1) * W]).then_inc(x_in[k], 16)
                        piece(k, k, cols_of(g, 4 * k, 4 * k + 4, 0, W), W, False)
                with sp.Fori(0, NFULL - 1) as i:
                    blk(u, i * 8 + (c0 + 8) // 2, i * W)
                    blk(g, i * 8 + (c0 + 16) // 2, i * W + W)
                blk(u, (c0 + 16 * NFULL - 8) // 2, (NFULL - 1) * W)
                blk(g, (c0 + 16 * NFULL) // 2, NFULL * W, WL)
                blk(u, (c0 + 16 * NFULL + 8) // 2, NFULL * W, WL)
                for b in range(4):
                    for m in range(KD2 // 2):
                        n = (c0 + 16 * (NFULL + 1) + b * KD2) // 2 + m
                        piece(n, n % NRAW, cols_of(dn, 4 * m, min(4 * m + 4, KF), b * W, W), W)

            half_ffn(1, C_FFN1)
            blk(d["mem_wk"], C_K0 // 2, 0)
            for n, (_, _, c0) in enumerate(WIN):
                blk(d["w_in"], C_WIN // 2 + 4 * n, c0)
            blk(d["mem_wk"], C_K1 // 2, W)
            for i, w in enumerate(("cmp_w1_k", "cmp_w1_v")):
                for k in range(4):
                    piece((C_CMP + 8 * i) // 2 + k, k, cols_of(d[w], 8 * k, 8 * k + 8, 0, CH), CH)
            for b, (w, c) in enumerate((("mem_wk", 2), ("mem_wk", 3), ("mem_wv", 0), ("mem_wv", 1), ("mem_wv", 2))):
                blk(d[w], C_FILL // 2 + 4 * b, c * W)
            with sp.Fori(0, 4) as i:
                blk(d["w_out"], i * 4 + C_WOUT // 2, i * W)
            blk(d["mem_wv"], C_V3 // 2, 3 * W)
            with sp.Fori(0, 4) as i:
                blk(d["mem_wq"], i * 4 + C_WQ // 2, i * W)
            with sp.Fori(0, 4) as i:
                blk(d["mem_wo"], i * 4 + C_WO // 2, i * W)
            half_ffn(2, C_FFN2)
            for g in range(4):
                w_normed(sp, 13 + g)
                sp.dma_start(out.rearrange("(t p) n -> p t n", p=P)[:, :, g * W:(g + 1) * W],
                             x_tok[:, :, g * W:(g + 1) * W]).then_inc(stored, 16)
            sp.wait_ge(stored, 64)

        @block.tensor
        def _(pe):
            def chunk(c, slot, lhs, kts, n, pair, first, last):
                pe.wait_ge(lo_made, c + 1)
                for q, kt in enumerate(kts):
                    for t in range(TT):
                        for a, w in ((0, whi), (0, wlo), (1, whi)):
                            mm = pe.matmul(ps[pair][:, t * W:t * W + n], lhs[a][:, kt, t * P:(t + 1) * P],
                                           w[:, slot, q * n:(q + 1) * n],
                                           start=first and q == 0 and a == 0 and w is whi,
                                           stop=last and q == len(kts) - 1 and a == 1, skip_group_check=True)
                mm.then_inc(multiplied, 1)

            def step(c, k, lhs, pair, n=W):
                chunk(c + k, k % AHEAD, lhs, (2 * k, 2 * k + 1), n, pair, k == 0, k == 7)

            def turn_group(name, src, n=4, more=None):
                p, _ = U.at[name]
                w_free(pe, name, 0) if more is None else pe.wait_ge(freed[p], more)
                for i in range(n):
                    for t in range(TT):
                        mm = pe.transpose(ps[p][:, i * T + t * P:i * T + (t + 1) * P], src(t, i), ident)
                mm.then_inc(ready[p], 1)

            def half_ffn(f, c0, xT, group):
                name = ("x", "x3")[f - 1]

                def h_group(j, n=4, i=None):
                    n_up = U.at[("acc", c0 + 16 * j + 8)][1] + 1
                    pe.wait_ge(freed[B], n_up if i is None else i + n_up)
                    turn_group(("h", f, j), lambda t, k: hbuf[:, t, k * P:(k + 1) * P], n,
                               None if i is None else i + U.at[("h", f, 0)][1])

                group(0)
                w_free(pe, ("acc", c0))
                for k in range(8):
                    if k % 2 == 0:
                        w_over(pe, (name, k // 2))
                    elif k < 7:
                        group(k // 2 + 1)
                    step(c0, k, xT, A)
                with pe.Fori(0, NFULL - 1) as i:
                    pe.wait_ge(freed[B], i + U.at[("acc", c0 + 8)][1])
                    for k in range(8):
                        step(i * 16 + (c0 + 8), k, xT, B)
                    pe.wait_ge(freed[A], i + U.at[("acc", c0 + 16)][1])
                    for k in range(8):
                        if k == 3:
                            h_group(0, i=i)
                        step(i * 16 + (c0 + 16), k, xT, A)
                c = c0 + 16 * NFULL - 8
                w_free(pe, ("acc", c))
                for k in range(8):
                    step(c, k, xT, B)
                w_free(pe, ("acc", c + 8))
                for k in range(8):
                    if k == 3:
                        h_group(NFULL - 1)
                    step(c + 8, k, xT, A, WL)
                w_free(pe, ("acc", c + 16))
                for k in range(8):
                    step(c + 16, k, xT, B, WL)
                for b in range(4):
                    w_free(pe, ("d", f, b))
                    for m in range(KD2):
                        if b == 0 and m == 2:
                            h_group(NFULL, WL // P)
                        if b == 0 and m == 2 * NFULL - 2:
                            w_over(pe, ("h", f, NFULL - 1))
                        if b == 0 and m == 2 * NFULL:
                            w_over(pe, ("h", f, NFULL))
                        if b == 0 and f == 1 and m in S_MEM:
                            g = S_MEM.index(m)
                            pe.wait_ge(mem_in[g], 16)
                            turn_group(("mem", g), lambda t, i: stage[g % 2][:, t, i * P:(i + 1) * P])
                        c = c0 + 16 * (NFULL + 1) + b * KD2 + m
                        chunk(c, c % AHEAD, hT[f], range(2 * m, min(2 * m + 2, KF)), W, (A, B)[b % 2], m == 0,
                              m == KD2 - 1)

            def norm_group(i, g):
                w_normed(pe, 4 * i + g + 1)
                turn_group((f"x{i + 1}", g), lambda t, k: x_tok[:, t, g * W + k * P:g * W + (k + 1) * P])

            def kt_group(b):
                src = stage[1] if b == 0 else kstage
                w_over(pe, ("acc", (C_K0, C_K1, C_FILL, C_FILL + 8)[b]))
                turn_group(("kt", b), lambda t, i: src[:, t, i * P:(i + 1) * P])

            pe.wait_ge(ident_in, 16)

            def x_group(g):
                pe.wait_ge(x_in[g], 16)
                turn_group(("x", g), lambda t, i: x_tok[:, t, g * W + i * P:g * W + (i + 1) * P])

            half_ffn(1, C_FFN1, xT0, x_group)

            w_free(pe, ("acc", C_K0))
            w_over(pe, ("mem", 2))
            w_over(pe, ("mem", 3))
            for k in range(8):
                if k >= 6:
                    norm_group(0, k - 6)
                step(C_K0, k, memT, A)

            def sb_scores(h):
                hh = h % 4
                if h == 0:
                    w_free(pe, "sb")
                else:
                    pe.wait_ge(sb_em, h)
                z = ps[T1][:, 0:384]
                pe.matmul(z[:, 0:T], sbk[:, hh, 0:P], sbq[:, h, :], start=True, stop=True, skip_group_check=True)
                pe.matmul(z[:, T:384], sbk[:, hh, P:T], sbq[:, h, P:T], start=False, stop=True,
                          skip_group_check=True).then_inc(sb_z, 1)

            def sb_rest(h):
                pe.wait_ge(sb_l, h + 1)
                z, l = ps[T1][:, 0:384], sbl[:, h % 2, :]
                pe.matmul(z, negu, l, start=False, stop=True, skip_group_check=True)
                pe.matmul(z[:, P:T], neg1, l[:, T:384], start=False, stop=True,
                          skip_group_check=True).then_inc(sb_r, 1)

            def sb_values(h):
                pe.wait_ge(sb_w, h + 1)
                if h:
                    pe.wait_ge(sb_out, h)
                o, w, v = ps[T1][:, W:W + T], sba[:, h % 2, :], sbv[:, :, h % 4 * HD:(h % 4 + 1) * HD]
                pe.matmul(o[:, 0:P], w[:, 0:P], v[:, 0, :], start=True, stop=True, skip_group_check=True)
                pe.matmul(o[:, P:T], w[:, P:T], v[:, 0, :], start=False, stop=False, skip_group_check=True)
                pe.matmul(o[:, P:T], w[:, T:384], v[:, 1, :], start=False, stop=True,
                          skip_group_check=True).then_inc(sb_o, 1)

            def w_group(n):
                w_over(pe, ("acc", C_WIN + 8 * n))
                turn_group(("w", n), lambda t, i: stage[n % 2][:, t, i * P:(i + 1) * P],
                           2 if WIN[n][0] in ("slc", "win") else 4)

            def gates():
                w_free(pe, "gates")
                pe.wait_ge(gate_lo, 1)
                pe.wait_ge(cleared, 1)
                for kt in range(KD):
                    cols = slice(kt * NG, kt * NG + P)
                    for a, x in ((0, 0), (0, 1), (1, 0)):
                        mm = pe.matmul(ps[T1][:, 0:T], wg_parts[a][:, cols], x1T[x][:, kt, :],
                                       start=kt == 0 and a == x, stop=kt == KD - 1 and a == 1, skip_group_check=True)
                mm.then_inc(ready[T1], 1)

            def gates_turn():
                w_over(pe, "gates")
                for t in range(TT):
                    mm = pe.transpose(ps[T1][:, t * NG:(t + 1) * NG], gate_t[0:NG, t * P:(t + 1) * P],
                                      ident[0:NG, 0:NG])
                mm.then_inc(ready[T1], 1)

            def stick_breaking(s):
                for h, z in enumerate(SB_Z):
                    if s == z:
                        if h == 0:
                            pe.wait_ge(const_in, 16)
                        if h in (0, 4):
                            w_over(pe, ("w", 1 if h == 0 else 6))
                        sb_scores(h)
                for h, z in enumerate(SB_Z):
                    if s == z + SB_R:
                        sb_rest(h)
                    if s == z + SB_O:
                        if h in (0, 4):
                            w_over(pe, ("acc", C_WIN + 8 * (2 if h == 0 else 7)))
                        sb_values(h)

            for n in range(NWIN):
                c = C_WIN + 8 * n
                w_free(pe, ("acc", c))
                for k in range(8):
                    if n == 0:
                        if k in (1, 3):
                            norm_group(0, 2 + k // 2)
                        if k == 5:
                            kt_group(0)
                        if k % 2 == 0:
                            w_over(pe, ("x1", k // 2))
                    elif k == 3 and WIN[n - 1][0] != "v":
                        w_group(n - 1)
                    if 8 * n + k == S_GATES:
                        gates()
                    if 8 * n + k == S_GATES + 2:
                        gates_turn()
                    stick_breaking(8 * n + k)
                    step(c, k, x1T, (B, A)[n % 2])

            w_free(pe, ("acc", C_K1))
            for k in range(8):
                stick_breaking(8 * NWIN + k)
                if k == 3:
                    w_group(NWIN - 1)
                step(C_K1, k, memT, A)

            for i in range(2):
                c, pair = C_CMP + 8 * i, (B, A)[i]
                w_free(pe, ("acc", c))
                pe.wait_ge(fc_made, i + 1)
                for k in range(8):
                    if i == 0 and k == 3:
                        kt_group(1)
                    pe.wait_ge(lo_made, c + k + 1)
                    for q in range(4):
                        for w in (whi, wlo):
                            mm = pe.matmul(ps[pair][0:LOROW + GC, 0:CH], FC[i][:, 4 * k + q, :],
                                           w[:, k % AHEAD, q * CH:(q + 1) * CH],
                                           start=k == 0 and q == 0 and w is whi, stop=k == 7 and q == 3 and w is wlo,
                                           skip_group_check=True)
                    mm.then_inc(multiplied, 1)

            def cmp_step(n):
                if n == 0:
                    w_free(pe, "l1")
                    for i in range(2):
                        w_over(pe, ("acc", C_CMP + 8 * i))
                    for i in range(2):
                        for m in range(2):
                            mm = pe.matmul(ps[T1][:, (2 * i + m) * 32:(2 * i + m) * 32 + GC],
                                           hc[0:LOROW + GC, i, m * P:(m + 1) * P], sel[0:LOROW + GC, :],
                                           start=True, stop=True, skip_group_check=True)
                    mm.then_inc(ready[T1], 1)
                if n == 1:
                    w_free(pe, "l2")
                    pe.wait_ge(gelu_made, 1)
                    for m in range(2):
                        pe.matmul(ps[T1][:, 0:GC], w2[:, 0, m, :], ug[:, 3, m, 0:GC],
                                  start=m == 0, stop=m == 1, skip_group_check=True)
                    for g in range(GROUPS):
                        for r in range(REP):
                            for m in range(2):
                                mm = pe.matmul(ps[T1][32 * r:32 * r + NC, W + g * HD:W + (g + 1) * HD],
                                               ug[:, 3, 2 + m, g * NC:(g + 1) * NC], w2[:, 1, m, :],
                                               start=m == 0, stop=m == 1, skip_group_check=True)
                    mm.then_inc(ready[T1], 1)
                if n == 2:
                    w_free(pe, "cs")
                    w_over(pe, "l2")
                    for t in range(TT):
                        for h in range(NSH):
                            g = h // REP
                            o = (t * NSH + h) * NC
                            mm = pe.matmul(ps[T1][:, o:o + NC], nsq[:, h, t * P:(t + 1) * P],
                                           kcmp[:, g * NC:(g + 1) * NC], start=True, stop=True, skip_group_check=True)
                    mm.then_inc(ready[T1], 1)
                if n == 3:
                    w_free(pe, "cp")
                    pe.wait_ge(cs_made, 1)
                    for t in range(TT):
                        for g in range(GROUPS):
                            o = (t * GROUPS + g) * P
                            mm = pe.transpose(ps[T1][:, o:o + P],
                                              pcp[:, t, g * REP:(g + 1) * REP, :].rearrange("p a b -> p (a b)"), ident)
                    mm.then_inc(ready[T1], 1)

            def unit_values(s):
                n, part = divmod(s - 4, 4)
                if part or not 0 <= n < len(UNITS):
                    return
                g, br, tq = UNITS[n]
                w_over(pe, ("p", n))
                if n % 4 == 0:
                    w_free(pe, ("O", g))
                for r in range(REP):
                    for kk in range(tq + 1):
                        pe.matmul(ps[B][:, tq * W + r * HD:tq * W + (r + 1) * HD], probT[:, r, kk, :],
                                  vsw[:, br, kk, g * HD:(g + 1) * HD], start=br == 0 and r == 0 and kk == 0,
                                  stop=False, skip_group_check=True)
                if n % 4 == 3:
                    w_over(pe, "cp")
                    for t in range(TT):
                        mm = pe.matmul(ps[B][:, t * W:(t + 1) * W], pcT[:, t, g, :], vblk[:, g, :],
                                       start=False, stop=True, skip_group_check=True)
                    mm.then_inc(ready[B], 1)

            for s in range(32):
                b, k = divmod(s, 8)
                n, part = divmod(s, 4)
                g, br, tq = UNITS[n]
                keys = (tq + 1) * P
                unit_values(s)
                if s in S_CMP:
                    cmp_step(S_CMP.index(s))
                if s in S_KT:
                    kt_group(2 + S_KT.index(s))
                if part == 0:
                    w_free(pe, ("s", n))
                    if n == 0:
                        w_over(pe, ("w", NWIN - 1))
                    kT = (kslT, kwnT)[br]
                    for r in range(REP):
                        mm = pe.matmul(ps[T0][:, r * T:r * T + keys], nsq[:, g * REP + r, tq * P:(tq + 1) * P],
                                       kT[:, g, 0:keys], start=True, stop=True, skip_group_check=True)
                    mm.then_inc(ready[T0], 1)
                if part == 3:
                    w_free(pe, ("p", n))
                    pe.wait_ge(ns_prob, n + 1)
                    for r in range(REP):
                        for kk in range(tq + 1):
                            o = (r * TT + kk) * P
                            mm = pe.transpose(ps[T1][:, o:o + P], prob[:, r, kk * P:(kk + 1) * P], ident)
                    mm.then_inc(ready[T1], 1)
                if k == 0:
                    w_free(pe, ("acc", C_FILL + 8 * b))
                step(C_FILL + 8 * b, k, memT, A)

            w_free(pe, ("acc", C_V2))
            for k in range(8):
                unit_values(32 + k)
                if k in S_Y:
                    g = S_Y.index(k)
                    pe.wait_ge(y_made, 1 + g // 2)
                    src = (sbq, nsq)[g // 2]
                    turn_group(("y", g), lambda t, i: src[:, 4 * (g % 2) + i, t * P:(t + 1) * P])
                step(C_V2, k, memT, A)

            with pe.Fori(0, 2) as i:
                for b, pair in enumerate((B, A)):
                    c = C_WOUT + 8 * b
                    pe.wait_ge(freed[pair], i + U.at[("acc", c)][1])
                    for k in range(8):
                        if k % 2 == 0:
                            w_over(pe, ("y", k // 2))
                        step(i * 16 + c, k, yT, pair)

            w_free(pe, ("acc", C_V3))
            for k in range(8):
                if k >= 6:
                    norm_group(1, k - 6)
                step(C_V3, k, memT, B)

            def mem_step(what, h):
                if what == "qt":
                    w_over(pe, ("acc", C_WQ + 8 * h))
                    turn_group(("qt", h), lambda t, i: stage[0][:, t, i * P:(i + 1) * P])
                    return
                if what == "ot":
                    w_over(pe, ("mo", h))
                    turn_group(("ot", h), lambda t, i: mo_tok[:, h % 2, t, i * P:(i + 1) * P])
                    return
                w_free(pe, (what, h))
                if what == "z":
                    w_over(pe, ("qt", h))
                    for t in range(TT):
                        for k in range(MK):
                            mm = pe.matmul(ps[T1][:, t * T:(t + 1) * T], qT[:, MK * h + k, t * P:(t + 1) * P],
                                           KT[:, MK * h + k, :], start=k == 0, stop=k == MK - 1,
                                           skip_group_check=True)
                if what == "mp":
                    w_over(pe, ("z", h))
                    for t in range(TT):
                        for m in range(TT):
                            mm = pe.transpose(ps[T1][:, (t * TT + m) * P:(t * TT + m + 1) * P],
                                              mprob[h % 2][:, t, m * P:(m + 1) * P], ident)
                if what == "mo":
                    w_over(pe, ("mp", h))
                    for t in range(TT):
                        for m in range(TT):
                            mm = pe.matmul(ps[T0][:, t * W:(t + 1) * W], mprobT[h % 2][:, t, m, :],
                                           V[:, m, h * W:(h + 1) * W], start=m == 0, stop=m == TT - 1,
                                           skip_group_check=True)
                mm.then_inc(ready[U.at[(what, h)][0]], 1)

            for s in range(64):
                b, k = divmod(s, 8)
                c, pair = C_WQ + 8 * b, (A, B)[b % 2]
                if k == 0:
                    w_free(pe, ("acc", c))
                if s in (1, 3):
                    norm_group(1, 2 + s // 2)
                if b == 0 and k % 2 == 0:
                    w_over(pe, ("x2", k // 2))
                for what, h in mem_work(s):
                    mem_step(what, h)
                if b == 4 and k % 2 == 0:
                    w_over(pe, ("ot", k // 2))
                step(c, k, x2T if b < 4 else oT, pair)

            half_ffn(2, C_FFN2, xT3, lambda g: norm_group(2, g))

        def size(c):
            for c0 in (C_FFN1, C_FFN2):
                if c0 + 16 * NFULL <= c < c0 + 16 * (NFULL + 1):
                    return CHUNK * WL // W
                m = c - c0 - 16 * (NFULL + 1)
                if 0 <= m < 4 * KD2 and m % KD2 == KD2 - 1:
                    return CHUNK // 2
            return CHUNK

        def plus(i, step, x):
            return x if i is None else i * step + x

        def make_hi(act, c, i=None):
            if c >= C_END:
                return
            slot, n = c // 2 % NRAW, size(c)
            o = c % 2 * (CHUNK if n == CHUNK // 2 else n)
            if c % 2 == 0:
                act.wait_ge(landed[slot], plus(i, 32, 16 * (c // 8 + 1)))
            if c >= AHEAD:
                act.wait_ge(multiplied, plus(i, 16, c - AHEAD + 1))
            act.activation(whi[:, c % AHEAD, 0:n], raw[:, slot, o:o + n], ACT.Copy).then_inc(
                hi_made, 1)

        def make_lo(dve, c, i=None):
            if c >= C_END:
                return
            slot, n = c // 2 % NRAW, size(c)
            o = c % 2 * (CHUNK if n == CHUNK // 2 else n)
            dve.wait_ge(hi_made, plus(i, 16, c + 1))
            dve.tensor_tensor(wlo[:, c % AHEAD, 0:n], raw[:, slot, o:o + n],
                              whi[:, c % AHEAD, 0:n].bitcast(F32), ALU.subtract).then_inc(
                lo_made, 1)

        def split_wait(e, name, i=None):
            e.wait_ge(split_hi, plus(i, 1, U.split[name] + 1))

        def sb_work(s):
            return ([("z", h) for h, z in enumerate(SB_Z) if s == z]
                    + [("r", h) for h, z in enumerate(SB_Z) if s == z + SB_R]
                    + [("o", h) for h, z in enumerate(SB_Z) if s == z + SB_O])

        @block.scalar
        def _(act):
            steps = [0]

            def chain(ins):
                steps[0] += 1
                ins.then_inc(act_step, 1)
                act.wait_ge(act_step, steps[0])

            def group_hi(name, dst, kt, n=4, i=None):
                p, _ = U.at[name]
                act.wait_ge(ready[p], plus(i, 1, U.sends[name]))
                to = dst[0][:, kt:kt + n, :] if i is None else dst[0][:, bass.ds(i * 4, n), :]
                act.activation(to, ps[p][:, 0:n * T].rearrange("p (k t) -> p k t", t=T), ACT.Copy).then_inc(split_hi, 1)

            def group_copy(name, dst):
                w_ready(act, name)
                p, _ = U.at[name]
                n = dst.shape[1]
                act.activation(dst, ps[p][:, 0:n * T].rearrange("p (k t) -> p k t", t=T), ACT.Copy).then_inc(
                    freed[p], 1)

            def block_copy(c, dst, scale=1.0):
                act.wait_ge(multiplied, c + 8)
                p, _ = U.at[("acc", c)]
                act.activation(dst, ps[p][:, :].rearrange("p (t w) -> p t w", t=TT), ACT.Copy,
                               scale=scale).then_inc(freed[p], 1)

            def norm_piece(i, g):
                if g == 0:
                    act.wait_ge(norm_rs, i + 1)
                for t in range(TT):
                    x = x_tok[:, t, g * W:(g + 1) * W]
                    act.activation(x, x, ACT.Identity, bias=nb[:, t:t + 1], scale=rs[:, t:t + 1]).then_inc(norm_hat, 1)

            def half_ffn(f, c0, xT, extra):
                name = ("x", "x3")[f - 1]

                def silu(j, n=W, i=None):
                    act.wait_ge(multiplied, plus(i, 16, c0 + 16 * j + 8))
                    if i is not None or j:
                        act.wait_ge(freed[B], plus(i, 1, U.at[("acc", c0 + 16 * j - 8)][1] + 1))
                    act.activation(sil[:, :, 0:n], ps[A][:, :].rearrange("p (t w) -> p t w", t=TT)[:, :, 0:n],
                                   ACT.Silu).then_inc(freed[A], 1)

                for k in range(8):
                    if k in (3, 5):
                        group_hi((name, k // 2 + 1), xT, 4 * (k // 2 + 1))
                    make_hi(act, c0 + k + AHEAD)
                silu(0)
                with act.Fori(0, NFULL - 1) as i:
                    for k in range(8):
                        make_hi(act, c0 + 8 + k + AHEAD, i)
                    for k in range(8):
                        if k == 4:
                            group_hi(("h", f, 0), hT[f], 0, 4, i)
                        make_hi(act, c0 + 16 + k + AHEAD, i)
                    silu(1, W, i)
                c = c0 + 16 * NFULL - 8
                for k in range(8):
                    make_hi(act, c + k + AHEAD)
                for k in range(8):
                    if k == 4:
                        group_hi(("h", f, NFULL - 1), hT[f], 4 * NFULL - 4)
                    make_hi(act, c + 8 + k + AHEAD)
                silu(NFULL, WL)
                for k in range(8):
                    make_hi(act, c + 16 + k + AHEAD)
                for b in range(4):
                    for m in range(KD2):
                        if b == 0 and m == 3:
                            group_hi(("h", f, NFULL), hT[f], 4 * NFULL, WL // P)
                        extra(b, m)
                        make_hi(act, c + 24 + b * KD2 + m + AHEAD)

            mem_r = d["mem"].rearrange("(t p) n -> p t n", p=P)

            def load_mem(g):
                act.dma_start(stage[g % 2][:, :, :], mem_r[:, :, g * W:(g + 1) * W]).then_inc(mem_in[g], 16)

            def load_gb(i, dst, wait):
                act.wait_ge(multiplied, wait)
                act.dma_start(dst[:, :, :], d["ln"][i:i + 1, :, :].to_broadcast([P, 2, D])).then_inc(gb_in[i], 16)

            def extra1(b, m):
                if b == 0 and m == 4:
                    act.wait_ge(multiplied, C_DOWN1)
                    act.dma_start(const[:, P:], d["const"][:, P:]).then_inc(const_in, 16)
                    act.dma_start(wg[:, :], d["gate_w"]).then_inc(gate_in, 16)
                    w_over(act, ("h", 1, NFULL))
                    load_mem(0)
                    load_mem(1)
                if b == 0 and m in S_MEM:
                    g = S_MEM.index(m)
                    group_hi(("mem", g), memT, 4 * g)
                    if g < 2:
                        load_mem(g + 2)
                if b == 3 and m == 8:
                    load_gb(0, gb1, C_DOWN1 + 3 * KD2 + 8)

            def extra2(b, m):
                if b == 0 and m == 4:
                    load_gb(3, gb4, C_DOWN2)

            act.dma_start(ident, d["const"][:, 0:P]).then_inc(ident_in, 16)
            for c in range(AHEAD):
                if c % 2 == 0:
                    group_hi(("x", c // 2), xT0, 2 * c)
                make_hi(act, c)
            half_ffn(1, C_FFN1, xT0, extra1)

            for k in range(8):
                if 1 <= k <= 4:
                    norm_piece(0, k - 1)
                if k >= 6:
                    group_hi(("x1", k - 6), x1T, 4 * (k - 6))
                make_hi(act, C_K0 + k + AHEAD)
            block_copy(C_K0, stage[1][:, :, :])

            dest = {"q": lambda i: sbq[:, 4 * i:4 * i + 4, :], "k": lambda i: sbk[:, :, :],
                    "nq": lambda i: nsq[:, 4 * i:4 * i + 4, :], "cmp": lambda i: kcT[:, :, :],
                    "slc": lambda i: kslT[:, :, :], "win": lambda i: kwnT[:, :, :]}
            def stick_breaking(s):
                for part, h in sb_work(s):
                    w = sba[:, h % 2, :]
                    if part == "z":
                        act.wait_ge(sb_z, h + 1)
                        if h >= 2:
                            act.wait_ge(sb_o, h - 1)
                        chain(act.activation(w, ps[T1][:, 0:384], ACT.Abs))
                        chain(act.activation(w, w, ACT.Exp, scale=-1.0))
                        act.activation(w, w, ACT.Ln, bias=1.0).then_inc(sb_ln, 1)
                    if part == "r":
                        act.wait_ge(sb_em, h + 1)
                        act.activation(w, w, ACT.Exp).then_inc(sb_w, 1)

            for n, (what, i, _) in enumerate(WIN):
                c = C_WIN + 8 * n
                for k in range(8):
                    if n == 0:
                        if k in (1, 3):
                            group_hi(("x1", 2 + k // 2), x1T, 8 + 4 * (k // 2))
                        if k == 4:
                            w_normed(act, 4)
                            act.dma_start(angle[:, :, :, :], d["angle"]).then_inc(angle_in, 16)
                            act.dma_start(w2[:, :, :, :], d["cmp_w2"]).then_inc(cmp_in, 16)
                        if k == 5:
                            group_copy(("kt", 0), KT[:, 0:4, :])
                            act.wait_ge(gate_in, 16)
                            act.activation(wg_parts[0][:, 0:KD * NG], wg[:, :], ACT.Copy).then_inc(gate_hi, 1)
                    elif k == 3 and WIN[n - 1][0] != "v":
                        group_copy(("w", n - 1), dest[WIN[n - 1][0]](WIN[n - 1][1]))
                    if 8 * n + k == S_GATES + 1:
                        w_ready(act, "gates")
                        act.activation(gate_t[0:NG, :], ps[T1][0:NG, 0:T], ACT.Exp, scale=-1.0).then_inc(freed[T1], 1)
                    stick_breaking(8 * n + k)
                    make_hi(act, c + k + AHEAD)
                if what == "q":
                    block_copy(c, stage[n % 2][:, :, :], SCALE)
                if what == "k":
                    block_copy(c, stage[n % 2][:, :, :])
                if what == "v":
                    block_copy(c, sbv[:, :, :])

            for k in range(8):
                stick_breaking(8 * NWIN + k)
                if k == 1:
                    act.wait_ge(multiplied, C_K1)
                    act.dma_start(posT[:, :, :], d["pos"]).then_inc(cmp_in, 16)
                    act.wait_ge(sb_o, SBH)
                    act.dma_start(mg[:, :], d["mix_norm_g"].to_broadcast([P, D])).then_inc(mg_in, 16)
                if k == 3:
                    group_copy(("w", NWIN - 1), dest["win"](0))
                make_hi(act, C_K1 + k + AHEAD)
            block_copy(C_K1, kstage[:, :, :])

            for i in range(2):
                for k in range(8):
                    if i == 0 and k == 3:
                        group_copy(("kt", 1), KT[:, 4:8, :])
                    if k == 7:
                        c, p = C_CMP + 8 * i, (B, A)[i]
                        act.wait_ge(multiplied, c + 8)
                        act.activation(hc[0:LOROW + GC, i, :], ps[p][0:LOROW + GC, 0:CH], ACT.Copy).then_inc(
                            freed[p], 1)
                    make_hi(act, C_CMP + 8 * i + k + AHEAD)

            def outputs(g):
                w_ready(act, ("O", g))
                act.activation(nsq[:, g * REP:(g + 1) * REP, :].rearrange("p r (t d) -> p t r d", t=TT),
                               ps[B][:, :].rearrange("p (t r d) -> p t r d", t=TT, r=REP), ACT.Copy).then_inc(
                                   freed[B], 1)

            for s in range(32):
                b, k = divmod(s, 8)
                n, part = divmod(s, 4)
                g, br, tq = UNITS[n]
                keys = (tq + 1) * P
                if part == 0:
                    act.wait_ge(ns_max, n + 1)
                    for r in range(REP):
                        e = act.activation(prob[:, r, 0:keys], prob[:, r, 0:keys], ACT.Exp, bias=nm[:, r:r + 1],
                                           scale=SCALE, accum_out=sm[:, r:r + 1])
                    e.then_inc(ns_exp, 1)
                if s in S_KT:
                    b2 = 2 + S_KT.index(s)
                    group_copy(("kt", b2), KT[:, 4 * b2:4 * b2 + 4, :])
                if s == 18:
                    outputs(0)
                if s == S_CMP[3] + 1:
                    w_ready(act, "cp")
                    act.activation(pcT[:, :, :, :].rearrange("p t g q -> p (t g q)"), ps[T1][:, 0:TT * GROUPS * P],
                                   ACT.Copy).then_inc(freed[T1], 1)
                if s == S_CMP[0] + 1:
                    act.wait_ge(gelu_x, 1)
                    act.activation(ug[:, 2, :, 0:GC], ug[:, 1, :, 0:GC], ACT.Exp, scale=-2.0 * GELU).then_inc(gelu_e, 1)
                if s == S_CMP[2] + 1:
                    act.wait_ge(cs_max, 1)
                    act.activation(pcs[:, :, :, :], pcs[:, :, :, :], ACT.Exp, scale=SCALE).then_inc(cs_exp, 1)
                if part == 3:
                    w_ready(act, ("p", n))
                    act.activation(probT[:, :, 0:tq + 1, :],
                                   ps[T1][:, :].rearrange("p (r k q) -> p r k q", r=REP, k=TT)[:, :, 0:tq + 1, :],
                                   ACT.Copy).then_inc(freed[T1], 1)
                if k == 7:
                    if b < 2:
                        block_copy(C_FILL + 8 * b, kstage[:, :, :])
                    else:
                        block_copy(C_FILL + 8 * b, V[:, :, (b - 2) * W:(b - 1) * W])
                make_hi(act, C_FILL + s + AHEAD)

            def squares(half, src):
                for t, o in enumerate((prob, scrap)):
                    e = act.activation(o[:, :, :].rearrange("p a b -> p (a b)").rearrange("p (h d) -> p h d", h=8),
                                       src[:, :, t * P:(t + 1) * P], ACT.Square, scale=1.0 / 32,
                                       accum_out=ss[:, 2 * half + t:2 * half + t + 1])
                e.then_inc(sq_made, 1)

            for k in range(8):
                if k == 0:
                    squares(0, sbq)
                if k == 1:
                    outputs(1)
                    act.wait_ge(freed[B], U.at[("O", 1)][1] + 1)
                    squares(1, nsq)
                if k in S_Y:
                    group_hi(("y", S_Y.index(k)), yT, 4 * S_Y.index(k))
                make_hi(act, C_V2 + k + AHEAD)
            block_copy(C_V2, V[:, :, 2 * W:3 * W])

            load_gb(1, gb2, C_V2 + 8)
            with act.Fori(0, 2) as i:
                for k in range(16):
                    make_hi(act, C_WOUT + k + AHEAD, i)

            for k in range(8):
                if 1 <= k <= 4:
                    norm_piece(1, k - 1)
                if k >= 6:
                    group_hi(("x2", k - 6), x2T, 4 * (k - 6))
                make_hi(act, C_V3 + k + AHEAD)
            block_copy(C_V3, V[:, :, 3 * W:4 * W])

            def m_exps(h):
                act.wait_ge(m_max, h + 1)
                for t in range(TT):
                    e = act.activation(mprob[h % 2][:, t, :], ps[T1][:, t * T:(t + 1) * T],
                                       ACT.Exp, bias=nm[:, 2 * h + t:2 * h + t + 1], scale=MSCALE,
                                       accum_out=sm[:, 2 * h + t:2 * h + t + 1])
                e.then_inc(freed[T1], 1)

            for s in range(64):
                if s in (1, 3):
                    group_hi(("x2", 2 + s // 2), x2T, 8 + 4 * (s // 2))
                for what, h in mem_work(s - 1):
                    if what == "z":
                        m_exps(h)
                for what, h in mem_work(s):
                    if what == "qt":
                        group_copy(("qt", h), qT[:, MK * h:MK * (h + 1), :])
                    if what == "ot":
                        group_hi(("ot", h), oT, MK * h)
                if s == 34:
                    load_gb(2, gb3, C_WO)
                if s < 32 and s % 8 == 7:
                    block_copy(C_WQ + s - 7, stage[0][:, :, :])
                make_hi(act, C_WQ + s + AHEAD)

            for g in range(4):
                norm_piece(2, g)
                if g in (1, 2):
                    group_hi(("x3", g - 1), xT3, 4 * (g - 1))
            half_ffn(2, C_FFN2, xT3, extra2)
            for g in range(4):
                norm_piece(3, g)

        @block.vector
        def _(dve):
            steps = [0]

            def did(ins):
                steps[0] += 1
                ins.then_inc(dve_step, 1)

            def see():
                dve.wait_ge(dve_step, steps[0])

            def chain(ins):
                did(ins)
                see()

            def group_lo(name, dst, kt, n=4, i=None):
                p, _ = U.at[name]
                split_wait(dve, name, i)
                at = slice(kt, kt + n) if i is None else bass.ds(i * 4, n)
                dve.tensor_tensor(dst[1][:, at, :], ps[p][:, 0:n * T].rearrange("p (k t) -> p k t", t=T),
                                  dst[0][:, at, :].bitcast(F32), ALU.subtract).then_inc(freed[p], 1)

            def half_ffn(f, c0, xT, extra):
                name = ("x", "x3")[f - 1]

                def hidden(j, n=W, i=None):
                    dve.wait_ge(multiplied, plus(i, 16, c0 + 16 * j + 16))
                    dve.wait_ge(freed[A], plus(i, 1, U.at[("acc", c0 + 16 * j)][1] + 1))
                    dve.tensor_tensor(hbuf[:, :, 0:n], ps[B][:, :].rearrange("p (t w) -> p t w", t=TT)[:, :, 0:n],
                                      sil[:, :, 0:n], ALU.mult).then_inc(freed[B], 1)

                for k in range(8):
                    if k in (3, 5):
                        group_lo((name, k // 2 + 1), xT, 4 * (k // 2 + 1))
                    make_lo(dve, c0 + k + AHEAD)
                with dve.Fori(0, NFULL - 1) as i:
                    for k in range(8):
                        make_lo(dve, c0 + 8 + k + AHEAD, i)
                    hidden(0, W, i)
                    for k in range(8):
                        if k == 4:
                            group_lo(("h", f, 0), hT[f], 0, 4, i)
                        make_lo(dve, c0 + 16 + k + AHEAD, i)
                c = c0 + 16 * NFULL - 8
                for k in range(8):
                    make_lo(dve, c + k + AHEAD)
                hidden(NFULL - 1)
                for k in range(8):
                    if k == 4:
                        group_lo(("h", f, NFULL - 1), hT[f], 4 * NFULL - 4)
                    make_lo(dve, c + 8 + k + AHEAD)
                for k in range(8):
                    make_lo(dve, c + 16 + k + AHEAD)
                hidden(NFULL, WL)
                for b in range(4):
                    for m in range(KD2):
                        if b == 0 and m == 3:
                            group_lo(("h", f, NFULL), hT[f], 4 * NFULL, WL // P)
                        extra(b, m)
                        if b and m == 0:
                            norm_add(c + 24 + b * KD2, ("d", f, b - 1), b - 1, 0.5)
                        make_lo(dve, c + 24 + b * KD2 + m + AHEAD)

            def norm_add(c, name, b, factor, i=None):
                p, n = U.at[name]
                dve.wait_ge(multiplied, plus(i, 16, c))
                cols = slice(b * W, (b + 1) * W) if i is None else bass.ds(i * (2 * W) + b * W, W)
                one = slice(b, b + 1) if i is None else bass.ds(i * 2 + b, 1)
                x = x_tok[:, :, cols]
                dve.scalar_tensor_tensor(out=x, in0=ps[p][:, :].rearrange("p (t w) -> p t w", t=TT),
                                         scalar=factor / ALPHA, in1=x, op0=ALU.mult, op1=ALU.add).then_inc(freed[p], 1)
                dve.wait_ge(freed[p], plus(i, 1, n + 1))
                for t in range(TT):
                    did(dve.bn_stats(st[:, t, one, :].rearrange("p o s -> p (o s)"), x_tok[:, t, cols]))

            def inverse_root(r, v, w):
                chain(dve.tensor_scalar(r.bitcast(I32), v.bitcast(I32), -0.5, float(0x5F3759DF), ALU.mult, ALU.add))
                for n in range(3):
                    chain(dve.tensor_tensor(w, r, r, ALU.mult))
                    chain(dve.scalar_tensor_tensor(out=w, in0=w, scalar=-0.5, in1=v, op0=ALU.mult, op1=ALU.mult))
                    chain(dve.scalar_tensor_tensor(out=r, in0=w, scalar=1.5, in1=r, op0=ALU.add, op1=ALU.mult))

            def norm_finish():
                see()
                for t in range(TT):
                    did(dve.bn_aggr(mv[:, t, :], st[:, t, :, :].rearrange("p a b -> p (a b)")))
                see()
                r, v = rs[:, 0:TT], rv[:, 0:TT]
                chain(dve.tensor_scalar(v, mv[:, :, 1], EPS1, None, ALU.add))
                inverse_root(r, v, rw[:, 0:TT])
                dve.scalar_tensor_tensor(out=nb[:, :], in0=mv[:, :, 0], scalar=-1.0, in1=r, op0=ALU.mult,
                                         op1=ALU.mult).then_inc(norm_rs, 1)

            def norm_piece(i, g, gb):
                if g == 0:
                    dve.wait_ge(gb_in[i], 16)
                cols, done = slice(g * W, (g + 1) * W), (4 * i + g) * TT
                for t in range(TT):
                    dve.wait_ge(norm_hat, done + t + 1)
                    dve.tensor_tensor(x_tok[:, t, cols], x_tok[:, t, cols], gb[:, 0, cols], ALU.mult).then_inc(
                        norm_gain, 1)
                if i < 2:
                    return
                dve.wait_ge(norm_gain, done + TT)
                dve.tensor_tensor(x_tok[:, 1, cols], x_tok[:, 1, cols], gb[:, 1, cols], ALU.add).then_inc(normed1, 1)

            def extra1(b, m):
                if b == 0 and m in S_MEM:
                    g = S_MEM.index(m)
                    group_lo(("mem", g), memT, 4 * g)

            for c in range(AHEAD):
                if c % 2 == 0:
                    group_lo(("x", c // 2), xT0, 2 * c)
                make_lo(dve, c)
            half_ffn(1, C_FFN1, xT0, extra1)

            for k in range(8):
                if k == 0:
                    norm_add(C_K0, ("d", 1, 3), 3, 0.5)
                    norm_finish()
                if 1 <= k <= 4:
                    norm_piece(0, k - 1, gb1)
                if k >= 6:
                    group_lo(("x1", k - 6), x1T, 4 * (k - 6))
                make_lo(dve, C_K0 + k + AHEAD)

            def rotate(c, n, dst, cols):
                p, _ = U.at[("acc", c)]
                heads = cols // HD
                for t in range(TT):
                    x = ps[p][:, t * W:t * W + cols].rearrange("p (h d) -> p h d", d=HD)
                    o = dst[:, t, 0:cols].rearrange("p (h d) -> p h d", d=HD)
                    r = rot[:, 0:cols].rearrange("p (h d) -> p h d", d=HD)
                    co = angle[:, 0, t:t + 1, :].to_broadcast([P, heads, HD])
                    si = angle[:, 1, t:t + 1, :].to_broadcast([P, heads, HD])
                    dve.tensor_tensor(o, x, co, ALU.mult)
                    dve.tensor_tensor(r[:, :, 0:HALF], x[:, :, HALF:HD], si[:, :, 0:HALF], ALU.mult)
                    chain(dve.tensor_tensor(r[:, :, HALF:HD], x[:, :, 0:HALF], si[:, :, HALF:HD], ALU.mult))
                    e = dve.tensor_tensor(o, o, r, ALU.add)
                    if t == 0 or cols < W:
                        chain(e)
                return e

            def stick_breaking(s):
                for part, h in sb_work(s):
                    if part == "r":
                        dve.wait_ge(sb_r, h + 1)
                        dve.tensor_tensor(sba[:, h % 2, :], ps[T1][:, 0:384], cap, ALU.min).then_inc(sb_em, 1)
                    if part == "o":
                        dve.wait_ge(sb_o, h + 1)
                        e = dve.tensor_copy(sbq[:, h, :], ps[T1][:, W:W + T])
                        e.then_inc(*((freed[T1], 1) if h == SBH - 1 else (sb_out, 1)))

            def soft_plus(s):
                for part, h in sb_work(s):
                    if part == "z":
                        l = sbl[:, h % 2, :]
                        dve.wait_ge(sb_ln, h + 1)
                        if h == 0:
                            dve.wait_ge(const_in, 16)
                        chain(dve.scalar_tensor_tensor(out=l, in0=ps[T1][:, 0:384], scalar=0.0, in1=sba[:, h % 2, :],
                                                       op0=ALU.max, op1=ALU.add))
                        diag = l.rearrange("p (a q) -> p a q", a=3)[:, 0:3:2, :]
                        dve.tensor_tensor(diag, diag, tri.rearrange("p (o q) -> p o q", o=1).to_broadcast(
                            [P, 2, P]), ALU.mult).then_inc(sb_l, 1)

            for n, (what, i, _) in enumerate(WIN):
                c = C_WIN + 8 * n
                for k in range(8):
                    if n == 0 and k in (1, 3):
                        group_lo(("x1", 2 + k // 2), x1T, 8 + 4 * (k // 2))
                    if n == 0 and k == 6:
                        dve.wait_ge(gate_hi, 1)
                        dve.tensor_tensor(wg_parts[1][:, 0:KD * NG], wg[:, :], wg_parts[0][:, 0:KD * NG].bitcast(F32),
                                          ALU.subtract).then_inc(gate_lo, 1)
                    if 8 * n + k == S_GATES + 3:
                        w_ready(dve, "gates_t")
                        dve.tensor_scalar(gate[:, :, :], ps[T1][:, 0:TT * NG].rearrange("p (t n) -> p t n", t=TT), 1.0,
                                          None, ALU.add).then_inc(freed[T1], 1)
                        w_over(dve, "gates_t")
                        did(dve.reciprocal(gate[:, :, :], gate[:, :, :]))
                    stick_breaking(8 * n + k)
                    make_lo(dve, c + k + AHEAD)
                    soft_plus(8 * n + k)
                if what in ("nq", "cmp", "slc", "win"):
                    p, _ = U.at[("acc", c)]
                    dve.wait_ge(multiplied, c + 8)
                    dve.wait_ge(angle_in, 16)
                    e = rotate(c, n, stage[n % 2], W if what == "nq" else T)
                    if what != "nq":
                        right = ps[p][:, :].rearrange("p (t w) -> p t w", t=TT)[:, :, T:W]
                        to = {"cmp": stage[n % 2][:, :, T:W], "slc": vsw[:, 0, :, :], "win": vsw[:, 1, :, :]}[what]
                        e = dve.tensor_copy(to, right)
                    e.then_inc(freed[p], 1)

            def operand(i):
                if i:
                    dve.wait_ge(fc_made, i)
                for hf in range(2):
                    for g in range(GROUPS):
                        src = kcT[:, 2 * i + g, :].rearrange("p (n s) -> p s n", s=CS)[:, :, hf:hf + NC]
                        po = posT[:, i, hf * CS:(hf + 1) * CS].rearrange("p (s o) -> p s o", o=1).to_broadcast(
                            [P, CS, NC])
                        did(dve.tensor_tensor(fs[:, hf * CS:(hf + 1) * CS, g * NC:(g + 1) * NC], src, po, ALU.add))
                see()
                chain(dve.tensor_copy(FC[i][:, :, 0:GC], fs[:, :, :]))
                dve.tensor_tensor(FC[i][:, :, LOROW:LOROW + GC], fs[:, :, :], FC[i][:, :, 0:GC].bitcast(F32),
                                  ALU.subtract).then_inc(fc_made, 1)

            for k in range(8):
                stick_breaking(8 * NWIN + k)
                if k == 3:
                    dve.wait_ge(cmp_in, 32)
                    dve.wait_ge(cleared, 2)
                    operand(0)
                if k == 5:
                    operand(1)
                make_lo(dve, C_K1 + k + AHEAD)
            for k in range(16):
                make_lo(dve, C_CMP + k + AHEAD)

            def cmp_step(n):
                if n == 0:
                    w_ready(dve, "l1")
                    x, t = ug[:, 0, :, 0:GC], ug[:, 1, :, 0:GC]
                    dve.tensor_copy(x, ps[T1][:, 0:P].rearrange("p (a b) -> p a b", a=4)[:, :, 0:GC]).then_inc(
                        freed[T1], 1)
                    w_over(dve, "l1")
                    chain(dve.tensor_tensor(t, x, x, ALU.mult))
                    chain(dve.tensor_scalar(t, t, 0.044715, 1.0, ALU.mult, ALU.add))
                    dve.tensor_tensor(t, t, x, ALU.mult).then_inc(gelu_x, 1)
                if n == 1:
                    w_ready(dve, "l2")
                    dve.tensor_copy(kcmp[:, :], ps[T1][:, 0:GC])
                    for g in range(GROUPS):
                        for r in range(REP):
                            e = dve.tensor_copy(vblk[32 * r:32 * r + NC, g, r * HD:(r + 1) * HD],
                                                ps[T1][32 * r:32 * r + NC, W + g * HD:W + (g + 1) * HD])
                    e.then_inc(freed[T1], 1)
                if n == 2:
                    w_ready(dve, "cs")
                    dve.tensor_tensor(pcs[:, :, :, :], ps[T1][:, 0:TT * NSH * NC].rearrange(
                        "p (t h c) -> p t h c", t=TT, h=NSH), cadd.to_broadcast([P, TT, NSH, NC]),
                        ALU.add).then_inc(freed[T1], 1)
                    w_over(dve, "cs")
                    chain(dve.tensor_reduce(cmx[:, :], pcs[:, :, :, :].rearrange("p t h c -> p (t h) c"),
                                          AX.X, ALU.max))
                    flat = pcs[:, :, :, :].rearrange("p t h c -> p (t h) c")
                    dve.tensor_tensor(flat, flat, cmx[:, :].rearrange("p (n o) -> p n o", o=1).to_broadcast(
                        [P, 16, NC]), ALU.subtract).then_inc(cs_max, 1)

            for s in range(32):
                b, k = divmod(s, 8)
                n, part = divmod(s, 4)
                g, br, tq = UNITS[n]
                keys = (tq + 1) * P
                if s in S_CMP[0:3]:
                    cmp_step(S_CMP.index(s))
                if part == 0:
                    w_ready(dve, ("s", n))
                    if n:
                        w_ready(dve, ("p", n - 1))
                    p = ps[T0]
                    for r in range(REP):
                        e = dve.tensor_tensor_reduce(
                            out=prob[:, r, 0:keys], in0=p[:, r * T:r * T + keys], in1=cmask[:, T - keys:T],
                            scale=1.0, scalar=-3.0e38, op0=ALU.add, op1=ALU.max, accum_out=mx[:, r:r + 1])
                    e.then_inc(freed[T0], 1)
                    w_over(dve, ("s", n))
                    dve.tensor_scalar(nm[:, 0:REP], mx[:, 0:REP], -SCALE, None, ALU.mult).then_inc(ns_max, 1)
                if part == 1:
                    dve.wait_ge(ns_exp, n + 1)
                    chain(dve.reciprocal(cf[:, 0:REP], sm[:, 0:REP]))
                    gt = gate[:, tq, :].rearrange("p (h j) -> p h j", j=3)[:, g * REP:(g + 1) * REP, 1 + br]
                    chain(dve.scalar_tensor_tensor(out=cf[:, 0:REP], in0=cf[:, 0:REP], scalar=1e30, in1=gt,
                                                   op0=ALU.min, op1=ALU.mult))
                    pr = prob[:, :, 0:keys]
                    dve.tensor_tensor(pr, pr, cf[:, 0:REP].rearrange("p (r o) -> p r o", o=1).to_broadcast(
                        [P, REP, keys]), ALU.mult).then_inc(ns_prob, 1)
                if s == S_CMP[0] + 2:
                    dve.wait_ge(gelu_e, 1)
                    e = ug[:, 2, :, 0:GC]
                    chain(dve.tensor_scalar(e, e, 1.0, None, ALU.add))
                    chain(dve.reciprocal(e, e))
                    dve.tensor_tensor(ug[:, 3, :, 0:GC], ug[:, 0, :, 0:GC], e, ALU.mult).then_inc(gelu_made, 1)
                if s == S_CMP[2] + 2:
                    dve.wait_ge(cs_exp, 1)
                    dve.wait_ge(cleared, 3)
                    flat = pcs[:, :, :, :].rearrange("p t h c -> p (t h) c")
                    chain(dve.tensor_tensor(pcs[:, :, :, :], pcs[:, :, :, :], cmul.to_broadcast([P, TT, NSH, NC]),
                                            ALU.mult))
                    chain(dve.tensor_reduce(csm[:, :], flat, AX.X, ALU.add))
                    chain(dve.tensor_scalar(csm[:, :], csm[:, :], 1e-30, None, ALU.max))
                    chain(dve.reciprocal(ccf[:, :], csm[:, :]))
                    cg = ccf[:, :].rearrange("p (t h) -> p t h", t=TT)
                    chain(dve.tensor_tensor(cg, cg, gate[:, :, :].rearrange("p t (h j) -> p t h j", j=3)[:, :, :, 0],
                                            ALU.mult))
                    dve.tensor_tensor(pcp[:, :, :, 0:NC].rearrange("p t h c -> p (t h) c"), flat,
                                      ccf[:, :].rearrange("p (n o) -> p n o", o=1).to_broadcast([P, 16, NC]),
                                      ALU.mult).then_inc(cs_made, 1)
                make_lo(dve, C_FILL + s + AHEAD)

            for s in range(8):
                if s in (0, 3):
                    k = s // 3
                    dve.wait_ge(sq_made, k + 1)
                    of = slice(2 * k, 2 * k + 2)
                    chain(dve.tensor_scalar(rv[:, of], ss[:, of], RMS_EPS, None, ALU.add))
                    inverse_root(rs[:, of], rv[:, of], rw[:, of])
                    dve.wait_ge(mg_in, 16)
                    src = (sbq, nsq)[k]
                    for t in range(TT):
                        o = src[:, :, t * P:(t + 1) * P]
                        e = dve.scalar_tensor_tensor(
                            out=o, in0=o, scalar=rs[:, 2 * k + t:2 * k + t + 1],
                            in1=mg[:, k * 1024:(k + 1) * 1024].rearrange("p (h d) -> p h d", d=HD),
                            op0=ALU.mult, op1=ALU.mult)
                    e.then_inc(y_made, 1)
                if s in S_Y:
                    group_lo(("y", S_Y.index(s)), yT, 4 * S_Y.index(s))
                make_lo(dve, C_V2 + s + AHEAD)

            before = steps[0]
            with dve.Fori(0, 2) as i:
                for b in range(2):
                    c = C_WOUT + 8 * b
                    for k in range(8):
                        make_lo(dve, c + k + AHEAD, i)
                    norm_add(c + 8, ("acc", c), b, 1.0, i)
            steps[0] += steps[0] - before

            norm_finish()
            for k in range(8):
                if 1 <= k <= 4:
                    norm_piece(1, k - 1, gb2)
                if k >= 6:
                    group_lo(("x2", k - 6), x2T, 4 * (k - 6))
                make_lo(dve, C_V3 + k + AHEAD)

            def mem_step(what, h):
                two = slice(2 * h, 2 * h + 2)
                if what == "z":
                    w_ready(dve, ("z", h))
                    chain(dve.tensor_reduce(mx[:, two], ps[T1][:, 0:W].rearrange("p (t m) -> p t m", t=TT), AX.X,
                                            ALU.max))
                    dve.tensor_scalar(nm[:, two], mx[:, two], -MSCALE, None, ALU.mult).then_inc(m_max, 1)
                if what == "mp":
                    w_over(dve, ("z", h))
                    did(dve.reciprocal(cf[:, two], sm[:, two]))
                    w_ready(dve, ("mp", h))
                    dve.tensor_copy(mprobT[h % 2][:, :, :, :].rearrange("p t m q -> p (t m q)"),
                                    ps[T1][:, 0:TT * TT * P]).then_inc(freed[T1], 1)
                if what == "mo":
                    see()
                    w_ready(dve, ("mo", h))
                    for t in range(TT):
                        e = dve.tensor_scalar(mo_tok[:, h % 2, t, :], ps[T0][:, t * W:(t + 1) * W],
                                              cf[:, 2 * h + t:2 * h + t + 1], None, ALU.mult)
                    e.then_inc(freed[T0], 1)
                if what == "ot":
                    group_lo(("ot", h), oT, MK * h)

            for s in range(64):
                if s in (1, 3):
                    group_lo(("x2", 2 + s // 2), x2T, 8 + 4 * (s // 2))
                for what, h in mem_work(s):
                    mem_step(what, h)
                if s == 63:
                    norm_add(C_FFN2, ("acc", C_WO + 24), 3, 1.0)
                    norm_finish()
                    norm_piece(2, 0, gb3)
                make_lo(dve, C_WQ + s + AHEAD)
                if s in (39, 47, 55):
                    norm_add(C_WQ + s + 1, ("acc", C_WQ + s - 7), s // 8 - 4, 1.0)

            for g in (1, 2, 3):
                norm_piece(2, g, gb3)
                if g < 3:
                    group_lo(("x3", g - 1), xT3, 4 * (g - 1))
            half_ffn(2, C_FFN2, xT3, lambda b, m: None)
            norm_add(C_END, ("d", 2, 3), 3, 0.5)
            norm_finish()
            for g in range(4):
                norm_piece(3, g, gb4)

        @block.gpsimd
        def _(pool):
            def norm_bias(i, gb):
                pool.wait_ge(gb_in[i], 16)
                for g in range(4):
                    cols, done = slice(g * W, (g + 1) * W), (4 * i + g) * TT
                    pool.wait_ge(norm_gain, done + 1)
                    pool.tensor_tensor(x_tok[:, 0, cols], x_tok[:, 0, cols], gb[:, 1, cols], ALU.add).then_inc(
                        normed0, 1)
                    if i < 2:
                        pool.wait_ge(norm_gain, done + TT)
                        pool.tensor_tensor(x_tok[:, 1, cols], x_tok[:, 1, cols], gb[:, 1, cols], ALU.add).then_inc(
                            normed1, 1)

            for w in wg_parts:
                e = pool.memset(w[:, KD * NG:].bitcast(F32), 0.0)
            e.then_inc(cleared, 1)
            norm_bias(0, gb1)
            pool.wait_ge(multiplied, C_K1)
            for i in range(2):
                pool.memset(FC[i][:, :, GC:LOROW].bitcast(F32), 0.0)
            pool.memset(vblk[:, :, :], 0.0).then_inc(cleared, 1)
            pool.wait_ge(multiplied, C_FILL)
            pool.memset(pcp[:, :, :, :], 0.0).then_inc(cleared, 1)
            norm_bias(1, gb2)
            norm_bias(2, gb3)
            norm_bias(3, gb4)


_OUT = "out_0_dram"


def kernel(**inputs):
    import concourse.bacc as bacc
    from concourse.bass_utils import run_bass_kernel_spmd

    a = {k: np.asarray(v) for k, v in inputs.items()}
    const, angle = constants()
    arrays = {
        "x": a["x"][0], "mem": a["mem"][0], "const": const, "angle": angle,
        "ln": np.stack([np.stack([a[f"ln{i}_g"][0], a[f"ln{i}_b"][0]]) for i in (1, 2, 3, 4)]),
        "pos": np.stack([a["cmp_pos_k"][0].T, a["cmp_pos_v"][0].T], 1),
        "gate_w": a["w_in"][0][:, GATE_COL:].reshape(KD, P, NG).transpose(1, 0, 2).reshape(P, KD * NG),
        "cmp_w2": np.stack([a[f"cmp_w2_{i}"][0].reshape(2, P, HD) for i in "kv"]).transpose(2, 0, 1, 3),
        "mix_norm_g": a["mix_norm_g"],
    }
    for n in ("ffn1_gate", "ffn1_up", "ffn1_down", "w_in", "cmp_w1_k", "cmp_w1_v", "w_out", "mem_wq", "mem_wk",
              "mem_wv", "mem_wo", "ffn2_gate", "ffn2_up", "ffn2_down"):
        arrays[n] = a[n][0]
    arrays = {f"in_{k}_dram": np.ascontiguousarray(v) for k, v in arrays.items()}
    nc = bacc.Bacc("TRN2", target_bir_lowering=False, num_devices=1, dynamic_dma_scratch_size=1024)
    d = {k[3:-5]: nc.dram_tensor(k, v.shape, F32, kind="ExternalInput").ap() for k, v in arrays.items()}
    out = nc.dram_tensor(_OUT, (T, D), F32, kind="ExternalOutput").ap()
    hybrid_layer(nc, d, out)
    r = run_bass_kernel_spmd(nc, [arrays], core_ids=[0])
    return r.results[0][_OUT].reshape(1, T, D)
```
